# Optimizing a Trainium2 kernel written in Bass

```python
import jax, jax.numpy as jnp
from jax import lax
import numpy as np
import math
import jax
import jax.numpy as jnp

D_MODEL = 2048
BATCH = 1
SEQ = 256
DEPTH = 1

FOX_HEADS = 8
FOX_HEAD_DIM = 128
FOX_WIDTH = FOX_HEADS * FOX_HEAD_DIM
ATTN_BLOCK = 128
MLSTM_HEADS = 4
MLSTM_QK_DIM = 128
MLSTM_V_DIM = 256
MLSTM_QK_WIDTH = MLSTM_HEADS * MLSTM_QK_DIM
MLSTM_V_WIDTH = MLSTM_HEADS * MLSTM_V_DIM
MLSTM_CONV = 4
MLSTM_CHUNK = 128
MIX_WIDTH = FOX_WIDTH + MLSTM_V_WIDTH
IN_SPLITS = (FOX_WIDTH, FOX_WIDTH, FOX_WIDTH, FOX_HEADS, MLSTM_QK_WIDTH, MLSTM_QK_WIDTH, MLSTM_V_WIDTH, MLSTM_HEADS, MLSTM_HEADS, MLSTM_V_WIDTH)
IN_WIDTH = 3 * FOX_WIDTH + FOX_HEADS + 2 * MLSTM_QK_WIDTH + 2 * MLSTM_V_WIDTH + 2 * MLSTM_HEADS
PEER_HEADS = 8
PEER_KEY_DIM = 256
PEER_N_KEYS = 128
PEER_TOPK = 16
PEER_N_EXPERTS = PEER_N_KEYS * PEER_N_KEYS
PEER_TOKEN_BLOCK = 128
NORM_EPS = 1e-6


def rmsnorm(x, w):
    xf = x.astype(jnp.float32)
    y = xf * lax.rsqrt(jnp.mean(xf * xf, axis=-1, keepdims=True) + NORM_EPS)
    return (y * w).astype(x.dtype)

def head_rmsnorm(h, w):
    B, S, H, dh = h.shape
    hf = h.astype(jnp.float32)
    hf = hf * lax.rsqrt(jnp.mean(hf * hf, axis=-1, keepdims=True) + NORM_EPS)
    return (hf.reshape(B, S, H * dh) * w).astype(h.dtype)

def causal_depthwise_conv(x, w, b):
    K = w.shape[0]
    S = x.shape[1]
    xp = jnp.pad(x, ((0, 0), (K - 1, 0), (0, 0)))
    y = b
    for j in range(K):
        y = y + w[j] * xp[:, j:j + S]
    return y

def forgetting_attention(q, k, v, f_logit):
    B, S, H, Dh = q.shape
    nb = S // ATTN_BLOCK
    F = jnp.cumsum(jax.nn.log_sigmoid(f_logit.astype(jnp.float32)), axis=1).transpose(0, 2, 1)
    qh = q.transpose(0, 2, 1, 3) * (Dh ** -0.5)
    kh = k.transpose(0, 2, 1, 3)
    vh = v.transpose(0, 2, 1, 3)
    q_blocks = qh.reshape(B, H, nb, ATTN_BLOCK, Dh).transpose(2, 0, 1, 3, 4)
    F_blocks = F.reshape(B, H, nb, ATTN_BLOCK).transpose(2, 0, 1, 3)
    q_pos = jnp.arange(S).reshape(nb, ATTN_BLOCK)
    k_pos = jnp.arange(S)

    def block(args):
        qb, Fb, pos = args
        s = jnp.einsum('bhqd,bhkd->bhqk', qb, kh, preferred_element_type=jnp.float32)
        s = s + Fb[..., :, None] - F[..., None, :]
        s = jnp.where(pos[:, None] >= k_pos[None, :], s, -jnp.inf)
        p = jax.nn.softmax(s, axis=-1)
        return jnp.einsum('bhqk,bhkd->bhqd', p.astype(vh.dtype), vh)

    out = lax.map(block, (q_blocks, F_blocks, q_pos))
    return out.transpose(1, 0, 3, 2, 4).reshape(B, S, H, Dh)

def mlstm_chunkwise(q, k, v, i_pre, f_pre):
    B, S, H, dk = q.shape
    dv = v.shape[-1]
    L = MLSTM_CHUNK
    nc = S // L
    f32 = jnp.float32

    def to_chunks(a):
        a = jnp.moveaxis(a, 2, 1)
        return a.reshape(B, H, nc, L, *a.shape[3:])

    qc = to_chunks(q).astype(f32)
    kc = to_chunks(k).astype(f32) * (dk ** -0.5)
    vc = to_chunks(v).astype(f32)
    ic = to_chunks(i_pre).astype(f32)
    b = jnp.cumsum(jax.nn.log_sigmoid(to_chunks(f_pre).astype(f32)), axis=-1)
    b_last = b[..., -1]

    w_end = b_last[..., None] - b + ic
    m_loc = jnp.max(w_end, axis=-1)
    a_end = jnp.exp(w_end - m_loc[..., None])
    C_loc = jnp.einsum('bhcl,bhcld,bhcle->bhcde', a_end, kc, vc)
    n_loc = jnp.einsum('bhcl,bhcld->bhcd', a_end, kc)

    def step(carry, inp):
        C, n, m = carry
        Cl, nl, ml, bl = inp
        m_new = jnp.maximum(bl + m, ml)
        a_prev = jnp.exp(bl + m - m_new)
        a_loc = jnp.exp(ml - m_new)
        C_new = a_prev[..., None, None] * C + a_loc[..., None, None] * Cl
        n_new = a_prev[..., None] * n + a_loc[..., None] * nl
        return (C_new, n_new, m_new), (C, n, m)

    init = (jnp.zeros((B, H, dk, dv), f32), jnp.zeros((B, H, dk), f32), jnp.zeros((B, H), f32))
    xs = (jnp.moveaxis(C_loc, 2, 0), jnp.moveaxis(n_loc, 2, 0), jnp.moveaxis(m_loc, 2, 0), jnp.moveaxis(b_last, 2, 0))
    _, (C_prev, n_prev, m_prev) = lax.scan(step, init, xs)
    C_prev = jnp.moveaxis(C_prev, 0, 2)
    n_prev = jnp.moveaxis(n_prev, 0, 2)
    m_prev = jnp.moveaxis(m_prev, 0, 2)

    g = b + m_prev[..., None]
    D = b[..., :, None] - b[..., None, :] + ic[..., None, :]
    causal = jnp.tril(jnp.ones((L, L), dtype=bool))
    D = jnp.where(causal, D, -jnp.inf)
    m_t = jnp.maximum(g, jnp.max(D, axis=-1))
    Sm = jnp.einsum('bhctd,bhcsd->bhcts', qc, kc) * jnp.exp(D - m_t[..., None])
    inter = jnp.exp(g - m_t)
    num = jnp.einsum('bhcts,bhcse->bhcte', Sm, vc) + inter[..., None] * jnp.einsum('bhctd,bhcde->bhcte', qc, C_prev)
    den = jnp.sum(Sm, axis=-1) + inter * jnp.einsum('bhctd,bhcd->bhct', qc, n_prev)
    h = num / jnp.maximum(jnp.abs(den), jnp.exp(-m_t))[..., None]
    return h.reshape(B, H, S, dv).transpose(0, 2, 1, 3).astype(v.dtype)

def peer_ffn(x, w_q, keys, u, v):
    B, S, D = x.shape
    T = B * S
    xt = x.reshape(T, D)
    q = (xt @ w_q).reshape(T, PEER_HEADS, 2, PEER_KEY_DIM // 2)
    scores = jnp.einsum('thpd,pnd->thpn', q, keys, preferred_element_type=jnp.float32)
    s_top, i_top = lax.top_k(scores, PEER_TOPK)
    cand = (s_top[:, :, 0, :, None] + s_top[:, :, 1, None, :]).reshape(T, PEER_HEADS, PEER_TOPK * PEER_TOPK)
    cand_idx = (i_top[:, :, 0, :, None] * PEER_N_KEYS + i_top[:, :, 1, None, :]).reshape(T, PEER_HEADS, PEER_TOPK * PEER_TOPK)
    s_fin, pos = lax.top_k(cand, PEER_TOPK)
    idx = jnp.take_along_axis(cand_idx, pos, axis=-1)
    gate = jax.nn.softmax(s_fin, axis=-1)
    nblk = T // PEER_TOKEN_BLOCK

    def blk(args):
        xb, ib, gb = args
        ub = jnp.take(u, ib, axis=0)
        act = jax.nn.gelu(jnp.einsum('thkd,td->thk', ub, xb, preferred_element_type=jnp.float32), approximate=False) * gb
        vb = jnp.take(v, ib, axis=0)
        return jnp.einsum('thk,thkd->td', act.astype(vb.dtype), vb)

    y = lax.map(blk, (xt.reshape(nblk, PEER_TOKEN_BLOCK, D),
                      idx.reshape(nblk, PEER_TOKEN_BLOCK, PEER_HEADS, PEER_TOPK),
                      gate.reshape(nblk, PEER_TOKEN_BLOCK, PEER_HEADS, PEER_TOPK)))
    return y.reshape(B, S, D)

def first_inputs(seed: int = 0) -> dict:
    key = jax.random.key(seed)
    ks = jax.random.split(key, 18)
    f32 = jnp.float32

    def nrm(k, shape, scale):
        return jax.random.normal(k, shape, f32) * scale

    return {
        "x": nrm(ks[0], (BATCH, SEQ, D_MODEL), 1.0),
        "norm1_w": 1.0 + nrm(ks[1], (DEPTH, D_MODEL), 0.02),
        "w_in": nrm(ks[2], (DEPTH, D_MODEL, IN_WIDTH), D_MODEL ** -0.5),
        "fox_f_bias": jnp.linspace(2.0, 6.0, FOX_HEADS, dtype=f32)[None] + nrm(ks[3], (DEPTH, FOX_HEADS), 0.1),
        "mlstm_conv_w": nrm(ks[4], (DEPTH, MLSTM_CONV, 2 * MLSTM_QK_WIDTH), MLSTM_CONV ** -0.5),
        "mlstm_conv_b": nrm(ks[5], (DEPTH, 2 * MLSTM_QK_WIDTH), 0.01),
        "mlstm_i_bias": nrm(ks[6], (DEPTH, MLSTM_HEADS), 0.1),
        "mlstm_f_bias": jnp.linspace(3.0, 6.0, MLSTM_HEADS, dtype=f32)[None] + nrm(ks[7], (DEPTH, MLSTM_HEADS), 0.1),
        "fox_out_norm_w": 1.0 + nrm(ks[8], (DEPTH, FOX_WIDTH), 0.02),
        "mlstm_out_norm_w": 1.0 + nrm(ks[9], (DEPTH, MLSTM_V_WIDTH), 0.02),
        "w_out": nrm(ks[10], (DEPTH, MIX_WIDTH, D_MODEL), MIX_WIDTH ** -0.5),
        "norm2_w": 1.0 + nrm(ks[11], (DEPTH, D_MODEL), 0.02),
        "peer_w_q": nrm(ks[12], (DEPTH, D_MODEL, PEER_HEADS * PEER_KEY_DIM), D_MODEL ** -0.5),
        "peer_keys": nrm(ks[13], (DEPTH, 2, PEER_N_KEYS, PEER_KEY_DIM // 2), (PEER_KEY_DIM // 2) ** -0.5),
        "peer_u": nrm(ks[14], (DEPTH, PEER_N_EXPERTS, D_MODEL), D_MODEL ** -0.5),
        "peer_v": nrm(ks[15], (DEPTH, PEER_N_EXPERTS, D_MODEL), PEER_HEADS ** -0.5),
        "final_norm_w": 1.0 + nrm(ks[16], (D_MODEL,), 0.02),
    }

def first_block(x, norm1_w, w_in, fox_f_bias, mlstm_conv_w, mlstm_conv_b, mlstm_i_bias, mlstm_f_bias,
              fox_out_norm_w, mlstm_out_norm_w, w_out, norm2_w, peer_w_q, peer_keys, peer_u, peer_v,
              final_norm_w):
    B, S, _ = x.shape
    split_points = [int(p) for p in np.cumsum(IN_SPLITS)[:-1]]
    for l in range(DEPTH):
        h = rmsnorm(x, norm1_w[l])
        z = h @ w_in[l]
        fq, fk, fv, ff, mq, mk, mv, mi, mf, mo = jnp.split(z, split_points, axis=-1)

        att = forgetting_attention(fq.reshape(B, S, FOX_HEADS, FOX_HEAD_DIM),
                                   fk.reshape(B, S, FOX_HEADS, FOX_HEAD_DIM),
                                   fv.reshape(B, S, FOX_HEADS, FOX_HEAD_DIM),
                                   ff + fox_f_bias[l])

        mqk = jax.nn.silu(causal_depthwise_conv(jnp.concatenate([mq, mk], axis=-1), mlstm_conv_w[l], mlstm_conv_b[l]))
        mq_c, mk_c = jnp.split(mqk, 2, axis=-1)
        cell = mlstm_chunkwise(mq_c.reshape(B, S, MLSTM_HEADS, MLSTM_QK_DIM),
                               mk_c.reshape(B, S, MLSTM_HEADS, MLSTM_QK_DIM),
                               mv.reshape(B, S, MLSTM_HEADS, MLSTM_V_DIM),
                               mi + mlstm_i_bias[l], mf + mlstm_f_bias[l])
        cell = jax.nn.sigmoid(mo.astype(jnp.float32)).astype(cell.dtype).reshape(B, S, MLSTM_HEADS, MLSTM_V_DIM) * cell

        mixed = jnp.concatenate([head_rmsnorm(att, fox_out_norm_w[l]),
                                 head_rmsnorm(cell, mlstm_out_norm_w[l])], axis=-1)
        x = x + mixed @ w_out[l]

        x = x + peer_ffn(rmsnorm(x, norm2_w[l]), peer_w_q[l], peer_keys[l], peer_u[l], peer_v[l])
    return rmsnorm(x, final_norm_w)


MEM_LEN = 256
RMS_EPS = 1e-6
DN_HEAD_DIM = 128
DN_WIDTH = D_MODEL // 2
DN_HEADS = DN_WIDTH // DN_HEAD_DIM
DN_CONV = 4
DN_CHUNK = 64
RW_HEAD_DIM = 64
RW_WIDTH = D_MODEL - DN_WIDTH
RW_HEADS = RW_WIDTH // RW_HEAD_DIM
RW_DECAY_LORA = 64
RW_AAA_LORA = 64
RW_GATE_LORA = 128
RW_GN_EPS = 64e-5
DN_COLS = 4 * DN_WIDTH + 2 * DN_HEADS
RW_COLS = 3 * RW_WIDTH + RW_DECAY_LORA + RW_AAA_LORA + RW_GATE_LORA
IN_COLS = DN_COLS + RW_COLS
XA_HEADS = 4
XA_HEAD_DIM = 128
XA_WIDTH = XA_HEADS * XA_HEAD_DIM
FFN_HIDDEN = 4 * D_MODEL


def rmsnorm_2(x, w):
    xf = x.astype(jnp.float32)
    y = xf * lax.rsqrt(jnp.mean(xf * xf, axis=-1, keepdims=True) + RMS_EPS)
    return (y * w.astype(jnp.float32)).astype(x.dtype)

def l2norm(x):
    return x * lax.rsqrt(jnp.sum(x * x, axis=-1, keepdims=True) + 1e-6)

def causal_depthwise_conv_2(x, w):
    k = w.shape[0]
    return lax.conv_general_dilated(
        x, w[:, None, :].astype(x.dtype), window_strides=(1,), padding=[(k - 1, 0)],
        dimension_numbers=('NWC', 'WIO', 'NWC'), feature_group_count=x.shape[-1])

def token_shift(p):
    return jnp.pad(p, ((0, 0), (1, 0), (0, 0)))[:, :-1]

def chunked_gated_delta_rule(q, k, v, g, beta):
    b, s, h, dk = q.shape
    dv = v.shape[-1]
    c = DN_CHUNK
    n = s // c

    def chunks(t):
        return t.reshape(b, n, c, h, -1).transpose(0, 3, 1, 2, 4)

    q = chunks(q) * (dk ** -0.5)
    k = chunks(k)
    v = chunks(v)
    g = g.reshape(b, n, c, h).transpose(0, 3, 1, 2)
    beta = beta.reshape(b, n, c, h).transpose(0, 3, 1, 2)
    gc = jnp.cumsum(g, axis=-1)
    idx = jnp.arange(c)
    causal = idx[:, None] >= idx[None, :]
    strict = idx[:, None] > idx[None, :]
    decay = jnp.exp(jnp.where(causal, gc[..., :, None] - gc[..., None, :], -jnp.inf))
    kb = k * beta[..., None]
    a_strict = jnp.where(strict, jnp.einsum('bhncd,bhnmd->bhncm', kb, k) * decay, 0.0)
    lower = a_strict + jnp.eye(c, dtype=q.dtype)
    rhs = jnp.concatenate([v * beta[..., None], kb * jnp.exp(gc)[..., None]], axis=-1)
    sol = lax.linalg.triangular_solve(lower, rhs, left_side=True, lower=True)
    u, w = sol[..., :dv], sol[..., dv:]
    attn = jnp.einsum('bhncd,bhnmd->bhncm', q, k) * decay
    qg = q * jnp.exp(gc)[..., None]
    g_last = gc[..., -1]
    kd = k * jnp.exp(g_last[..., None] - gc)[..., None]
    xs = tuple(jnp.moveaxis(t, 2, 0) for t in (u, w, qg, attn, kd, g_last))

    def step(state, xs_n):
        u_n, w_n, qg_n, attn_n, kd_n, gl_n = xs_n
        v_new = u_n - jnp.einsum('bhcd,bhde->bhce', w_n, state)
        o_n = jnp.einsum('bhcd,bhde->bhce', qg_n, state) + jnp.einsum('bhcm,bhme->bhce', attn_n, v_new)
        state = state * jnp.exp(gl_n)[..., None, None] + jnp.einsum('bhcd,bhce->bhde', kd_n, v_new)
        return state, o_n

    s0 = jnp.zeros((b, h, dk, dv), q.dtype)
    _, o = lax.scan(step, s0, xs)
    return o.transpose(1, 0, 3, 2, 4).reshape(b, s, h, dv)

def wkv7_scan(r, w, k, v, kk, a):
    b, s, h, nd = r.shape
    xs = tuple(jnp.swapaxes(t, 0, 1) for t in (r, w, k, v, kk, a))

    def step(state, xs_t):
        r_t, w_t, k_t, v_t, kk_t, a_t = xs_t
        sa = jnp.einsum('bhvk,bhk->bhv', state, -kk_t)
        state = (state * w_t[:, :, None, :] + sa[..., None] * (kk_t * a_t)[:, :, None, :]
                 + v_t[..., None] * k_t[:, :, None, :])
        return state, jnp.einsum('bhvk,bhk->bhv', state, r_t)

    s0 = jnp.zeros((b, h, nd, nd), r.dtype)
    _, y = lax.scan(step, s0, xs)
    return jnp.swapaxes(y, 0, 1)

def deltanet_group(p, conv_w, a_log, dt_bias, norm_w):
    p = p.astype(jnp.float32)
    b, s, _ = p.shape
    qkv, z, ga, gb = jnp.split(p, [3 * DN_WIDTH, 4 * DN_WIDTH, 4 * DN_WIDTH + DN_HEADS], axis=-1)
    qkv = jax.nn.silu(causal_depthwise_conv_2(qkv, conv_w))
    q, k, v = (t.reshape(b, s, DN_HEADS, DN_HEAD_DIM) for t in jnp.split(qkv, 3, axis=-1))
    q = l2norm(q)
    k = l2norm(k)
    beta = jax.nn.sigmoid(gb)
    g = -jnp.exp(a_log) * jax.nn.softplus(ga + dt_bias)
    o = chunked_gated_delta_rule(q, k, v, g, beta)
    o = rmsnorm_2(o, norm_w) * jax.nn.silu(z.reshape(b, s, DN_HEADS, DN_HEAD_DIM))
    return o.reshape(b, s, DN_WIDTH)

def rwkv7_group(p, mu, w0, w2, a0, a2, g2, k_k, k_a, r_k, ln_w, ln_b):
    p = p.astype(jnp.float32)
    b, s, _ = p.shape
    p = p + (token_shift(p) - p) * mu
    pr, pk, pv, pw, pa, pg = jnp.split(
        p, [RW_WIDTH, 2 * RW_WIDTH, 3 * RW_WIDTH, 3 * RW_WIDTH + RW_DECAY_LORA,
            3 * RW_WIDTH + RW_DECAY_LORA + RW_AAA_LORA], axis=-1)

    def heads(t):
        return t.reshape(b, s, RW_HEADS, RW_HEAD_DIM)

    log_w = -jax.nn.softplus(-(w0 + jnp.tanh(pw) @ w2)) - 0.5
    decay = jnp.exp(-jnp.exp(log_w))
    a = jax.nn.sigmoid(a0 + pa @ a2)
    gate = jax.nn.sigmoid(pg) @ g2
    kk = heads(pk * k_k)
    kk = kk / jnp.maximum(jnp.sqrt(jnp.sum(kk * kk, axis=-1, keepdims=True)), 1e-12)
    k = pk * (1.0 + (a - 1.0) * k_a)
    r_h, k_h, v_h = heads(pr), heads(k), heads(pv)
    y = wkv7_scan(r_h, heads(decay), k_h, v_h, kk, heads(a))
    mean = jnp.mean(y, axis=-1, keepdims=True)
    var = jnp.mean(jnp.square(y - mean), axis=-1, keepdims=True)
    y = ((y - mean) * lax.rsqrt(var + RW_GN_EPS)).reshape(b, s, RW_WIDTH) * ln_w + ln_b
    bonus = jnp.sum(r_h * k_h * r_k, axis=-1, keepdims=True) * v_h
    return (y + bonus.reshape(b, s, RW_WIDTH)) * gate

def memory_cross_attention(hn, mn, wq, wk, wv, wo):
    b, s, _ = hn.shape
    m = mn.shape[1]
    q = (hn @ wq).reshape(b, s, XA_HEADS, XA_HEAD_DIM)
    k = (mn @ wk).reshape(b, m, XA_HEADS, XA_HEAD_DIM)
    v = (mn @ wv).reshape(b, m, XA_HEADS, XA_HEAD_DIM)
    scores = jnp.einsum('bshd,bmhd->bhsm', q, k).astype(jnp.float32) * (XA_HEAD_DIM ** -0.5)
    probs = jax.nn.softmax(scores, axis=-1).astype(v.dtype)
    o = jnp.einsum('bhsm,bmhd->bshd', probs, v).reshape(b, s, XA_WIDTH)
    return o @ wo

def squared_relu_mlp(u, w1, w2):
    return jnp.square(jax.nn.relu(u @ w1)) @ w2

def second_inputs(seed: int = 0) -> dict:
    key = jax.random.key(seed)
    ks = jax.random.split(key, 32)
    L = DEPTH
    D = D_MODEL

    def normal(i, shape, scale):
        return jax.random.normal(ks[i], shape, jnp.float32) * scale

    def uniform(i, shape, lo, hi):
        return jax.random.uniform(ks[i], shape, jnp.float32, lo, hi)

    dt = jnp.exp(uniform(6, (L, DN_HEADS), math.log(1e-3), math.log(1e-1)))
    return {
        'x': normal(0, (BATCH, SEQ, D), 1.0),
        'mem': normal(1, (BATCH, MEM_LEN, D), 1.0),
        'mix_norm_w': 1.0 + normal(2, (L, D), 0.02),
        'w_in': normal(3, (L, D, IN_COLS), D ** -0.5),
        'dn_conv_w': normal(4, (L, DN_CONV, 3 * DN_WIDTH), DN_CONV ** -0.5),
        'dn_a_log': jnp.log(uniform(5, (L, DN_HEADS), 1.0, 16.0)),
        'dn_dt_bias': dt + jnp.log(-jnp.expm1(-dt)),
        'dn_norm_w': 1.0 + normal(7, (L, DN_HEAD_DIM), 0.02),
        'rw_mu': uniform(8, (L, RW_COLS), 0.0, 1.0),
        'rw_w0': uniform(9, (L, RW_WIDTH), -6.0, 1.0),
        'rw_w2': normal(10, (L, RW_DECAY_LORA, RW_WIDTH), 0.1 * RW_DECAY_LORA ** -0.5),
        'rw_a0': normal(11, (L, RW_WIDTH), 0.1),
        'rw_a2': normal(12, (L, RW_AAA_LORA, RW_WIDTH), 0.1 * RW_AAA_LORA ** -0.5),
        'rw_g2': normal(13, (L, RW_GATE_LORA, RW_WIDTH), RW_GATE_LORA ** -0.5),
        'rw_k_k': 0.85 + normal(14, (L, RW_WIDTH), 0.02),
        'rw_k_a': 1.0 + normal(15, (L, RW_WIDTH), 0.02),
        'rw_r_k': normal(16, (L, RW_HEADS, RW_HEAD_DIM), 0.1),
        'rw_ln_w': 1.0 + normal(17, (L, RW_WIDTH), 0.02),
        'rw_ln_b': normal(18, (L, RW_WIDTH), 0.02),
        'w_out': normal(19, (L, D, D), D ** -0.5),
        'xa_norm_w': 1.0 + normal(20, (L, D), 0.02),
        'mem_norm_w': 1.0 + normal(21, (L, D), 0.02),
        'xa_wq': normal(22, (L, D, XA_WIDTH), D ** -0.5),
        'xa_wk': normal(23, (L, D, XA_WIDTH), D ** -0.5),
        'xa_wv': normal(24, (L, D, XA_WIDTH), D ** -0.5),
        'xa_wo': normal(25, (L, XA_WIDTH, D), XA_WIDTH ** -0.5),
        'ffn_norm_w': 1.0 + normal(26, (L, D), 0.02),
        'ffn_w1': normal(27, (L, D, FFN_HIDDEN), D ** -0.5),
        'ffn_w2': normal(28, (L, FFN_HIDDEN, D), FFN_HIDDEN ** -0.5),
        'final_norm_w': 1.0 + normal(29, (D,), 0.02),
    }

def second_block(x, mem, mix_norm_w, w_in, dn_conv_w, dn_a_log, dn_dt_bias, dn_norm_w, rw_mu, rw_w0,
              rw_w2, rw_a0, rw_a2, rw_g2, rw_k_k, rw_k_a, rw_r_k, rw_ln_w, rw_ln_b, w_out,
              xa_norm_w, mem_norm_w, xa_wq, xa_wk, xa_wv, xa_wo, ffn_norm_w, ffn_w1, ffn_w2,
              final_norm_w):
    h = x
    for l in range(DEPTH):
        u = rmsnorm_2(h, mix_norm_w[l])
        p = u @ w_in[l]
        o_dn = deltanet_group(p[..., :DN_COLS], dn_conv_w[l], dn_a_log[l], dn_dt_bias[l], dn_norm_w[l])
        o_rw = rwkv7_group(p[..., DN_COLS:], rw_mu[l], rw_w0[l], rw_w2[l], rw_a0[l], rw_a2[l], rw_g2[l],
                           rw_k_k[l], rw_k_a[l], rw_r_k[l], rw_ln_w[l], rw_ln_b[l])
        h = h + jnp.concatenate([o_dn, o_rw], axis=-1).astype(h.dtype) @ w_out[l]
        h = h + memory_cross_attention(rmsnorm_2(h, xa_norm_w[l]), rmsnorm_2(mem, mem_norm_w[l]),
                                       xa_wq[l], xa_wk[l], xa_wv[l], xa_wo[l])
        h = h + squared_relu_mlp(rmsnorm_2(h, ffn_norm_w[l]), ffn_w1[l], ffn_w2[l])
    return rmsnorm_2(h, final_norm_w)


def setup_inputs(seed=0):
    out = dict(first_inputs(seed))
    for name, value in second_inputs(seed + 1).items():
        if name != "x":
            out[name + "_2"] = value
    return out


def reference(
    x, norm1_w, w_in, fox_f_bias, mlstm_conv_w, mlstm_conv_b, mlstm_i_bias, mlstm_f_bias,
    fox_out_norm_w, mlstm_out_norm_w, w_out, norm2_w, peer_w_q, peer_keys, peer_u, peer_v,
    final_norm_w, mem_2, mix_norm_w_2, w_in_2, dn_conv_w_2, dn_a_log_2, dn_dt_bias_2,
    dn_norm_w_2, rw_mu_2, rw_w0_2, rw_w2_2, rw_a0_2, rw_a2_2, rw_g2_2, rw_k_k_2, rw_k_a_2,
    rw_r_k_2, rw_ln_w_2, rw_ln_b_2, w_out_2, xa_norm_w_2, mem_norm_w_2, xa_wq_2, xa_wk_2,
    xa_wv_2, xa_wo_2, ffn_norm_w_2, ffn_w1_2, ffn_w2_2, final_norm_w_2,
):
    x = first_block(
        x, norm1_w, w_in, fox_f_bias, mlstm_conv_w, mlstm_conv_b, mlstm_i_bias, mlstm_f_bias,
        fox_out_norm_w, mlstm_out_norm_w, w_out, norm2_w, peer_w_q, peer_keys, peer_u, peer_v,
        final_norm_w,
    )
    return second_block(
        x, mem_2, mix_norm_w_2, w_in_2, dn_conv_w_2, dn_a_log_2, dn_dt_bias_2, dn_norm_w_2,
        rw_mu_2, rw_w0_2, rw_w2_2, rw_a0_2, rw_a2_2, rw_g2_2, rw_k_k_2, rw_k_a_2, rw_r_k_2,
        rw_ln_w_2, rw_ln_b_2, w_out_2, xa_norm_w_2, mem_norm_w_2, xa_wq_2, xa_wk_2, xa_wv_2,
        xa_wo_2, ffn_norm_w_2, ffn_w1_2, ffn_w2_2, final_norm_w_2,
    )


_drawn_inputs = setup_inputs


def setup_inputs(seed=0):
    import zlib

    import numpy as np

    out = dict(_drawn_inputs(seed))
    spreads = {}
    factors = {'mlstm_conv_b': 3.554,
     'mlstm_i_bias': 8.0,
     'mix_norm_w_2': 2.85,
     'dn_norm_w_2': 7.809,
     'rw_w2_2': 8.0,
     'rw_a0_2': 3.142,
     'rw_a2_2': 3.395,
     'rw_k_k_2': 4.561,
     'rw_k_a_2': 3.991,
     'rw_ln_w_2': 21.824,
     'rw_ln_b_2': 23.434,
     'xa_norm_w_2': 8.0,
     'mem_norm_w_2': 8.0,
     'ffn_norm_w_2': 12.386,
     'final_norm_w_2': 21.137}
    for name, (base, spread) in spreads.items():
        noise = np.random.default_rng([zlib.crc32(name.encode()), seed]).standard_normal(out[name].shape)
        drawn = base * np.exp(spread * noise) if base else spread * noise
        out[name] = jnp.asarray(drawn.astype(out[name].dtype))
    for name, factor in factors.items():
        out[name] = (out[name] * factor).astype(out[name].dtype)
    return out
```

```python
from contextlib import ExitStack

import numpy as np
import concourse.bass as bass
from concourse import mybir

F32 = mybir.dt.float32
U32 = mybir.dt.uint32
I32 = mybir.dt.int32
ALU = mybir.AluOpType
ACT = mybir.ActivationFunctionType
AX = mybir.AxisListType

P = 128
T = 256
NT = T // P
D = 2048
KT = D // P
BLK = 512
EPS = 1e-6
NEG = -1e30
FH, MH, MV = 8, 4, 256
PH, NK, TOPK = 8, 128, 16
NHALF = 2
EB = NK // 4
FB = 4 * D // BLK
DH = 8
QK_SCALE = float(P) ** -0.5
RW_EPS = 64e-5
DECAY = float(np.exp(-0.5))

STREAM = [("win", 12), ("wout", 4), ("wq", 4), ("peer", 2 * EB), ("dn", 8), ("small", 1), ("rw", 6),
          ("out2", 4), ("xk", 1), ("xv", 1), ("xq", 1), ("xo", 1), ("ffn", 2 * FB)]
SLOT0, _n = {}, 0
for _name, _groups in STREAM:
    SLOT0[_name] = _n
    _n += 4 * _groups
UNITS = [("win", 12, 1, 1), ("wout", 4, 1, 0), ("wq", 4, 1, 1), ("peer", 4 * EB, 1, 0), ("dn", 8, 1, 1),
         ("small", 1, 1, 1), ("rw", 6, 1, 1), ("out2", 4, 1, 0), ("xk", 1, 1, 1), ("xv", 1, 1, 1),
         ("xq", 1, 1, 1), ("xo", 4, 1, 0), ("ffn", 4 * FB, 1, 0)]
UNIT0, DVE0, ACT0 = {}, {}, {}
_u, _d, _a = 0, 2, 2
for _name, _units, _dv, _ac in UNITS:
    UNIT0[_name], DVE0[_name], ACT0[_name] = _u, _d, _a
    _u, _d, _a = _u + _units, _d + _units * _dv, _a + _units * _ac

COLS1 = [("norm1", 16), ("mix", 16), ("norm2", 16), ("cw", 32), ("cb", 8)]
COLS2 = [("mix2", 16), ("xa", 16), ("mem", 16), ("ffn", 16), ("dcw", 96), ("dnw", 1), ("mur", 8), ("muk", 8),
         ("muv", 8), ("muw", 1), ("mug", 1), ("w0", 8), ("a0", 8), ("kk", 8), ("ka", 8), ("rk", 8),
         ("lnw", 8), ("lnb", 8)]


STEPS = {
    "scalar_steps": [("gate_ln", 1), ("qk_silu", 1), ("mo_gate", 1), ("m_exp", 1), ("smt_out", 2), ("cp_out", 4),
                     ("inter_out", 4), ("mix_sq", 1), ("mix_root", 1), ("scores_out", 8), ("gate_exp", 1),
                     ("dn_silu", 6), ("z_silu", 1), ("dn_sq", 1), ("l2_root", 8), ("g_act", 1), ("gc_exp", 1),
                     ("dec_out", 1), ("atn_out", 4), ("at_out", 4), ("v_tok", 4), ("qs_out", 8), ("od_sq", 1),
                     ("od_root", 1), ("xa_exp", 1), ("xa_pt", 4), ("xo_ready", 1)],
    "tensor_steps": [("gate_mm", 1), ("cumsum_mm", 1), ("r_mm", 1), ("qk_mm", 2), ("k_turned", 1), ("sm_turned", 2),
                     ("cp_mm", 4), ("num0_mm", 4), ("inter_mm", 4), ("num1_mm", 4), ("scores_mm", 8), ("hk_turned", 1),
                     ("l2_mm", 8), ("gc_mm", 1), ("dec_mm", 4), ("kk_gram", 4), ("qk_gram", 4), ("qd_turned", 4),
                     ("a_turned", 4), ("v_turned", 4), ("kd_turned", 1), ("xa_mm", 1), ("xa_turned", 4), ("xa_o", 4)],
    "vector_steps": [("gate_abs", 1), ("log_f", 1), ("fox_diag", 1), ("conv_out", 1), ("mo_ready", 1), ("m_diag", 1),
                     ("r_read", 2), ("m_arg", 1), ("sm_ready", 2), ("ka_ready", 1), ("num0_out", 4), ("mix_ready", 2),
                     ("mix_sum", 1), ("gate_arg", 1), ("sel_ready", 4), ("gate_ready", 1), ("hk_ready", 1),
                     ("cin_pad", 1), ("dn_conv", 6), ("g_abs", 1), ("dn_qk", 1), ("g_ready", 1), ("gc_out", 1),
                     ("dn_diag", 1), ("dec_arg", 1), ("a_ready", 1), ("qd_ready", 4), ("kd_ready", 1), ("xa_max", 1),
                     ("xa_p", 1)],
}
STEP = {}
for _sem, _list in STEPS.items():
    _n = 0
    for _name, _times in _list:
        STEP[_name] = (_sem, _n)
        _n += _times


def offsets(table):
    out, at = {}, 0
    for name, n in table:
        out[name] = at
        at += n
    return out, at


C1, NC1 = offsets(COLS1)
C2, NC2 = offsets(COLS2)
NCOL = max(NC1, NC2)


class Own:

    def __init__(self, eng, order):
        self.eng, self.order, self.n = eng, order, {}

    def tell(self, ins, sem):
        self.n[id(sem)] = self.n.get(id(sem), 0) + 1
        ins.then_inc(sem, 1)

    def done(self, ins, sem=None):
        sem = self.order if sem is None else sem
        self.tell(ins, sem)
        self.eng.wait_ge(sem, self.n[id(sem)])


def build(nc, a, out):
    ctx = ExitStack()
    with ctx:
        def sb(name, cols, dt=F32):
            return ctx.enter_context(nc.sbuf_tensor(name, [P, cols], dt))

        X_ = sb("x_res", NT * D)
        XT_ = sb("x_t", KT * T)
        ring = [ctx.enter_context(nc.sbuf_tensor(f"ring{i}", [P, 4, BLK], F32)) for i in range(4)]
        AR = sb("arena", 32768)
        ID_ = sb("ident", P)
        ONES_ = sb("ones", P)
        IOTA_ = sb("iota", P)
        SM = sb("scratch", 320)
        HKT = sb("hkt", 3 * T)
        ACTB = sb("act_buf", 2048)
        PP = ctx.enter_context(nc.psum_tensor("pairs", [P, 2, 2, BLK], F32))
        PQ = ctx.enter_context(nc.psum_tensor("quad", [P, 4, BLK], F32))

        X = X_[:, :].rearrange("p (t d) -> p t d", t=NT)
        XT = XT_[:, :].rearrange("p (k t) -> p k t", k=KT)
        ID, ONES, IOTA = ID_[:, :], ONES_[:, :], IOTA_[:, :]

        class Signals(dict):

            def __missing__(self, name):
                if name in STEP:
                    return self[STEP[name][0]]
                self[name] = ctx.enter_context(nc.semaphore(name))
                return self[name]

        ev = Signals()

        def nth(name, n):
            return ev[name], STEP[name][1] + n

        used = ev["weights_used"]
        slot_full = [ev[f"slot_full{i}"] for i in range(4)]

        def av(off, *dims):
            n = int(np.prod(dims))
            v = AR[:, off:off + n]
            if len(dims) == 2:
                v = v.rearrange("p (a b) -> p a b", a=dims[0])
            if len(dims) == 3:
                v = v.rearrange("p (a b c) -> p a b c", a=dims[0], b=dims[1])
            if len(dims) == 4:
                v = v.rearrange("p (a b c d) -> p a b c d", a=dims[0], b=dims[1], c=dims[2])
            return v

        def bc(ap, n):
            return ap.unsqueeze(len(ap.shape)).broadcast_to([*ap.shape, n])

        def rep(ap, n):
            return ap.unsqueeze(1).broadcast_to([ap.shape[0], n, *ap.shape[1:]])

        MB = 32768 - 3200
        UI = av(MB, 128)
        LS = av(MB + 128, 128)
        TRI = av(MB + 256, 256)
        COL = av(MB + 512, NCOL)
        ROW = av(MB + 512 + NCOL, 32)
        at = MB + 544 + NCOL
        BD = [av(at + 128 * i, 128) for i in range(7)]
        LV = [av(at + 896 + 128 * i, 128) for i in range(7)]
        M4 = av(at + 1792, 4, 128)
        assert at + 2304 <= 32768
        EPSC, RWEPSC = SM[:, 0:1], SM[:, 1:2]
        SS, RS, RSTD = SM[:, 2:4], SM[:, 4:6], SM[:, 6:8]

        def col1(name, i=0, n=1):
            return COL[:, C1[name] + i:C1[name] + i + n]

        def col2(name, i=0, n=1):
            return COL[:, C2[name] + i:C2[name] + i + n]

        SCR = av(0, NT, D)
        FQ = av(4096, FH, T)
        FK = av(6144, FH, T)
        FV = av(8192, NT, FH * P)
        MQK = av(10240, 8, T + 3)
        MQC = av(12320, 8, T)
        MV1 = av(14368, NT, MH, MV + 1)
        MO = av(16424, NT, MH * MV)
        MIX = av(18472, NT, D)
        WG = av(22568, KT, 16)
        GT = av(22824, NT, 16)
        LF = av(22856, NT, 16)
        CS = av(22888, 4, 16)
        TM = av(22952, 8, 16)
        RC = av(23080, NT, MH)
        KCOL = av(23088, MH)
        MT = av(23092, NT, MH)
        EXB = av(23100, NT, MH)
        EM = av(23108, NT, MH)
        INTER = av(23116, MH)
        RM = av(23120, NT, MH)
        MREC = av(23128, 2, MH)
        FCOL = av(23136, NT, FH)
        NFCOL = av(23152, NT, FH)
        FST = av(23168, 2, 4)
        HN = av(23184, 2, 24)
        DG = av(4096 + 19136, FH, NT, P)
        FS = av(25280, 2, 384)
        FP = av(26048, 2, 384)
        FPT = av(26816, 2, 384)
        DGM = av(23232, NT, MH, P)
        DM = av(24256, NT, MH, P)
        SMM = av(25280, NT, MH, P)
        SMT = av(26304, NT, MH, P)
        KA = av(27328, MH, P)
        CP = av(27840, MH, MV + 1)
        NUM = av(4096, NT, MH, MV + 1)
        TMP = av(8192, MH, MV + 1)
        PQT = av(4096, 16, T)
        SC = av(8192, NT, 16, NK)
        SW = av(12288, NT, 16, NK)
        KEYS = av(16384, 2, NK)
        S16 = av(16640, NT, 16, TOPK)
        I16 = av(17152, NT, 16, TOPK)
        CD = av(0, NT, PH, 256)
        SF = av(17664, NT, PH, TOPK)
        PF = av(17920, NT, PH, TOPK)
        PA = av(18176, NT, PH, TOPK)
        PB = av(18432, NT, PH, TOPK)
        SEL = av(18688, 2, NT, P)
        IF = av(19200, NT, 16, TOPK)
        GS = av(19712, 4, NT, PH)
        GA = av(19776, NT, P)
        OH = av(20032, P, TOPK)
        OH2 = av(22080, P, TOPK)
        IO32 = SM[:, 32:160].bitcast(I32)
        CW = av(24448, NT, PH, 256)
        G = av(0, P, T)
        A0 = ACTB[:, 0:1024].rearrange("p (b t i) -> p b t i", b=2, t=4)
        B0 = ACTB[:, 1024:2048].rearrange("p (b t i) -> p b t i", b=2, t=4)
        HK = HKT[:, :].rearrange("p (w t) -> p w t", w=3)

        CIN = av(0, 8, T + 3)
        QKV = av(2080, 24, T)
        ZT = av(8224, NT, DH * P)
        YT = av(10272, KT, T)
        LW = av(14368, T + 1)
        LG = av(14625, T + 1)
        GB = av(14882, NT, 16)
        DST = av(14914, 12, NT, 8)
        VT = av(15106, NT, DH, P)
        KD = av(17154, DH, P)
        DEC = av(18178, NT, DH, P)
        AM = av(20226, 16, P)
        AT_ = av(22274, 16, P)
        TI = av(24322, 16, P)
        TTI = av(26370, 16, P)
        AOF = av(28418, 4, P)
        GV = av(28930, 16)
        DGD = TI
        SQD = av(20226, 16, T)
        ATN = av(0, 16, P)
        VN = av(22274, DH, P)
        RH = av(18178, DH, P)
        SD = av(19202, DH, P)
        OD = av(20226, NT, DH * P)
        OTM = av(24322, DH, P)

        J, HH = 4, 8
        W2, A2, G2 = av(0, 1024), av(1024, 1024), av(2048, 1024)
        GATE = av(3072, J, T)
        BON = av(4096, J, T)
        KRS = av(5120, 2, J, P)
        BKS = av(6144, 2, J, P)
        VTK = av(7168, NT, 512)
        BKT = av(8192, 2, J * P)
        RX = av(9216, 512)
        S1 = av(9728, J, P)
        E2 = av(9216, J, T)
        E1 = YT[:, 12:16, :]
        KRD = av(14882, J, 2, T)
        BKD = av(16930, 2, J, T)
        KRO = av(18978, J, 2, NT, 64)
        BKO = av(20002, 2, J, NT, 64)
        RAW = av(21026, 3, J, T + 1)
        RKV = av(24110, 3, J, T)
        LDX = av(27182, J, T)
        AA = av(28206, J, T)
        CUM = ACTB[:, 0:1024].rearrange("p (j t) -> p j t", j=J)
        KKN = ACTB[:, 1024:2048].rearrange("p (j t) -> p j t", j=J)
        GR = av(21026, 16, 4, P)
        RAM, RTI, RTT = av(14882, 16, P), av(16930, 16, P), av(18978, 16, P)
        RY = ACTB[:, 0:1024].rearrange("p (t c) -> p t c", t=NT)
        RY2 = ACTB[:, 1024:2048].rearrange("p (t c) -> p t c", t=NT)
        SAB = HKT[:, 0:512]
        RST = HKT[:, 512:576].rearrange("p (a m) -> p a m", a=4)
        AOFB = ACTB[:, 0:1024].rearrange("p (b m j) -> p b m j", b=2, m=4)
        M1B = ACTB[:, 1024:2048].rearrange("p (b m j) -> p b m j", b=2, m=4)
        LVA = av(at + 896, 7, 128)

        MEMX = av(4096, NT, D)
        MEMT = av(8192, KT, T)
        XK = av(12288, 4, T)
        XV = av(13312, NT, 512)
        XQ = av(14336, 4, T)
        XP = av(15360, 4, NT, T)
        XPT = av(17408, 4, NT, T)
        XO = av(19456, 1024)
        FNW = av(20480, D)
        XST = av(22528, 3, 8)

        block = ctx.enter_context(nc.Block())

        def flat(ap):
            n = len(ap.shape)
            if n == 3:
                return ap.rearrange("p a b -> p (a b)")
            if n == 4:
                return ap.rearrange("p a b c -> p (a b c)")
            return ap

        def stage2_loads(sp, slots, two_layer):
            for name, groups in (("dn", 8), ("small", 1), ("rw", 6), ("out2", 4), ("xk", 1), ("xv", 1), ("xq", 1),
                                 ("xo", 1)):
                slots(name, SLOT0[name], groups, width=4 * 272 if name == "small" else 2048)
            two_layer("f1", "f2", SLOT0["ffn"], FB)
            for t in range(NT):
                sp.wait_ge(ev["final"], t + 1)
                sp.dma_start(out[t * P:(t + 1) * P, :], X[:, t, :]).then_inc(ev["stored"], 16)
            sp.wait_ge(ev["stored"], 16 * NT)


        @block.sync
        def _(sp):
            def slots(name, base, groups, rows=None, width=2048):
                w = a[name]
                def one(i, s, n):
                    if not isinstance(n, int) or n >= 4:
                        sp.wait_ge(used, n - 3)
                    src = w[bass.ds(4 * i + s, 1)].rearrange("a p b -> (a p) b")
                    sp.dma_start(flat(ring[s][:, :, :])[:, 0:width], src).then_inc(slot_full[s], 16)
                if base == 0:
                    for s in range(4):
                        one(0, s, s)
                    with sp.Fori(1, groups, 1) as i:
                        for s in range(4):
                            one(i, s, base + 4 * i + s)
                elif groups == 1:
                    for s in range(4):
                        one(0, s, base + s)
                else:
                    with sp.Fori(0, groups, 1) as i:
                        for s in range(4):
                            one(i, s, base + 4 * i + s)

            def two_layer(first, second, base, blocks):
                u, v = a[first], a[second]
                def four(w, i, n):
                    for s in range(4):
                        sp.wait_ge(used, n + s - 3)
                        src = w[bass.ds(4 * i + s, 1)].rearrange("a p b -> (a p) b")
                        sp.dma_start(flat(ring[s][:, :, :]), src).then_inc(slot_full[s], 16)
                four(u, 0, base)
                with sp.Fori(0, blocks - 1, 1) as b:
                    four(u, b + 1, base + 4 + 8 * b)
                    four(v, b, base + 8 + 8 * b)
                four(v, blocks - 1, base + 8 * blocks - 4)

            for t in range(NT):
                sp.dma_start(X[:, t, :], a["x"][t * P:(t + 1) * P, :]).then_inc(ev["x_loaded"], 16)
            sp.dma_start(COL[:, 0:NC1], a["cols1"]).then_inc(ev["consts1"], 16)
            sp.dma_start(ROW, a["rows"].partition_broadcast(P)).then_inc(ev["consts1"], 16)
            sp.dma_start(flat(WG), a["w_gates"]).then_inc(ev["consts1"], 16)
            slots("win", SLOT0["win"], 12)
            slots("wout", SLOT0["wout"], 4)
            slots("wq", SLOT0["wq"], 4)
            sp.wait_ge(ev["tp_scaled"], 6)
            sp.dma_start(flat(KEYS), a["keys"]).then_inc(ev["keys_in"], 16)
            two_layer("pu", "pv", SLOT0["peer"], EB)
            stage2_loads(sp, slots, two_layer)

        def stage2_pool(pool, o, masks):
            pool.wait_ge(ev["peer_ready"], EB)
            pool.dma_start(FNW, a["fnw1"].partition_broadcast(P)).then_inc(ev["fnw_in"], 16)
            pool.dma_start(COL[:, 0:NC2], a["cols2"]).then_inc(ev["consts2"], 16)
            pool.dma_start(ROW, a["rows"].partition_broadcast(P)).then_inc(ev["consts2"], 16)
            masks(True)
            pool.wait_ge(ev["norm_root"], 4)
            pool.wait_ge(ev["turned"], 32)
            o.done(nc.gpsimd.memset(LW[:, 0:1], 0.0))
            o.done(nc.gpsimd.memset(LG[:, 0:1], 0.0), ev["pads"])
            pool.wait_ge(ev["dn_done"], 1)
            o.done(nc.gpsimd.memset(W2[64:P, :], 0.0))
            o.done(nc.gpsimd.memset(A2[0:64, :], 0.0), ev["lora_zero"])
            pool.dma_start(W2[0:64, :], a["w2"]).then_inc(ev["lora_in"], 16)
            pool.dma_start(A2[64:P, :], a["a2"]).then_inc(ev["lora_in"], 16)
            pool.dma_start(G2, a["g2"]).then_inc(ev["lora_in"], 16)
            pool.wait_ge(ev["rw_done"], 2)
            for t in range(NT):
                pool.dma_start(MEMX[:, t, :], a["mem"][t * P:(t + 1) * P, :]).then_inc(ev["mem_in"], 16)
            pool.dma_start(FNW, a["fnw"].partition_broadcast(P)).then_inc(ev["fnw_in"], 16)


        @block.gpsimd
        def _(pool):
            o = Own(pool, ev["pool_order"])

            def select(out, in_, op, pattern, base, cm, fill=0.0):
                return nc.gpsimd.affine_select(out=out, in_=in_, compare_op=op, fill=fill, base=base,
                                               pattern=pattern, channel_multiplier=cm)

            def masks(blocks):
                o.tell(select(UI, ONES, ALU.is_ge, [[1, P]], 0, -1), ev["masks"])
                o.tell(select(LS, ONES, ALU.is_gt, [[-1, P]], 0, 1), ev["masks"])
                o.done(nc.gpsimd.memset(TRI, 0.0))
                o.done(select(TRI[:, P:2 * P], TRI[:, P:2 * P], ALU.is_ge, [[-1, P]], 0, 1, NEG), ev["masks"])
                if not blocks:
                    return
                for i in range(7):
                    b = 1 << i
                    v = BD[i].rearrange("p (n b) -> p n b", b=b)
                    one = ONES.rearrange("p (n b) -> p n b", b=b)
                    o.done(select(v, one, ALU.is_ge, [[-b, P // b], [0, b]], 0, 1))
                    o.done(select(v, v, ALU.is_ge, [[b, P // b], [0, b]], b - 1, -1), ev["masks"])
                for i in range(7):
                    o.done(nc.gpsimd.tensor_tensor(LV[i], BD[i + 1] if i < 6 else ONES, BD[i], ALU.subtract), ev["masks"])
                for i in range(2):
                    o.done(nc.gpsimd.tensor_tensor(M4[:, 2 * i + 1, :], UI, BD[6], ALU.mult))
                    o.done(nc.gpsimd.tensor_tensor(M4[:, 2 * i, :], M4[:, 2 * i + 1, :], ID, ALU.subtract), ev["masks"])

            o.done(nc.gpsimd.memset(ONES, 1.0))
            o.done(select(ID, ONES, ALU.is_equal, [[-1, P]], 0, 1))
            o.done(nc.gpsimd.iota(IO32, pattern=[[1, P]], base=0, channel_multiplier=0))
            o.done(nc.gpsimd.tensor_copy(IOTA, IO32))
            o.done(nc.gpsimd.memset(MQK[:, :, 0:3], 0.0))
            o.done(nc.gpsimd.memset(MV1[:, :, :, MV:MV + 1], 1.0))
            masks(False)
            stage2_pool(pool, o, masks)
        def gates_act(act, o):
            act.wait_ge(*nth("gate_abs", 1))
            o.done(nc.scalar.activation(TM[:, 0:2, :], TM[:, 0:2, :], ACT.Exp, scale=-1.0))
            o.tell(nc.scalar.activation(TM[:, 0:2, :], TM[:, 0:2, :], ACT.Ln, bias=1.0), ev["gate_ln"])

        def mlstm_act(act, o):
            act.wait_ge(*nth("m_arg", 1))
            nc.scalar.activation(flat(DM), flat(DM), ACT.Exp)
            nc.scalar.activation(INTER, INTER, ACT.Exp)
            nc.scalar.activation(KCOL, KCOL, ACT.Exp)
            o.tell(nc.scalar.activation(EM, MT, ACT.Exp, scale=-1.0), ev["m_exp"])
            for c in range(NT):
                act.wait_ge(*nth("sm_turned", c + 1))
                o.tell(nc.scalar.copy(flat(SMT[:, c]), PQ[:, c, :]), ev["smt_out"])
            for h in range(MH):
                act.wait_ge(*nth("cp_mm", h + 1))
                o.tell(nc.scalar.copy(CP[:, h, :], PQ[:, h, 0:MV + 1]), ev["cp_out"])
            act.wait_ge(*nth("m_exp", 1))
            for h in range(MH):
                act.wait_ge(*nth("inter_mm", h + 1))
                o.tell(nc.scalar.mul(TMP[:, h, :], PQ[:, h, 0:MV + 1], INTER[:, h:h + 1]), ev["inter_out"])

        def two_act(act, name, blocks, func):
            base = SLOT0[name]
            b01 = [ACTB[:, 0:1024], ACTB[:, 1024:2048]]
            h = PQ[:, 0:2, :].rearrange("p a b -> p (a b)")
            p = name + "_acted"
            if name == "peer":
                act.wait_ge(ev["rows_used"], T // 4 + 2)
                act.wait_ge(ev["bank_empty"], T // 4 + 2)
            act.wait_ge(used, base + 4)
            nc.scalar.activation(b01[0], h, func).then_inc(ev[p], 1)
            with act.Fori(0, blocks // 2 - 1, 1) as i:
                for par in range(2):
                    act.wait_ge(used, 16 * i + (base + 8 * (par + 1)))
                    nc.scalar.activation(b01[1 - par], h, func).then_inc(ev[p], 1)
            act.wait_ge(used, base + 8 * (blocks - 1))
            nc.scalar.activation(b01[1], h, func).then_inc(ev[p], 1)

        def inverse_act(act, c):
            if c == 0:
                for _ in range(2):
                    act.nop().then_inc(ev["inv_m1_out"], 1)
            with act.Fori(1, 7, 1) as l:
                for q in range(4):
                    g = 4 * l + (24 * c - 4 + q)
                    act.wait_ge(ev["inv_m1"], g + 3)
                    act.wait_ge(ev["inv_t"], g + 1)
                    nc.scalar.copy(M1B[:, q % 2], PQ[:, q % 2, :].rearrange("p (m j) -> p m j", m=4)
                                   ).then_inc(ev["inv_m1_out"], 1)

        def stage2_act(act, o, half, freed, sums):
            sums(2, X, (ev["dve_free"], DVE0["dn"]))
            sums(3, X, (ev["block1_out"], 2))
            for j in range(8):
                ps = half("dn", j)
                if j < 6:
                    if j == 0:
                        act.wait_ge(*nth("cin_pad", 1))
                    if j >= 2:
                        act.wait_ge(*nth("dn_conv", j - 1))
                    c = 4 * (j % 2)
                    freed(nc.scalar.copy(CIN[:, c + 2:c + 4, 3:3 + T], ps.rearrange("p (n t) -> p n t", n=2)))
                else:
                    freed(nc.scalar.activation(ZT[:, 1, BLK * (j - 6):BLK * (j - 5)], ps, ACT.Silu))
                if 1 <= j < 7:
                    act.wait_ge(*nth("dn_conv", j))
                    o.tell(nc.scalar.activation(flat(QKV[:, 4 * j - 4:4 * j, :]), flat(QKV[:, 4 * j - 4:4 * j, :]), ACT.Silu),
                           ev["dn_silu"])
            act.wait_ge(ev["dve_free"], DVE0["dn"] + 8)
            o.tell(nc.scalar.activation(ZT[:, 0, :], ZT[:, 0, :], ACT.Silu), ev["z_silu"])
            act.wait_ge(ev["pads"], 1)
            ps = half("small", 0)
            nc.scalar.copy(LW[:, 1:1 + T], ps[:, 0:T])
            freed(nc.scalar.copy(LG[:, 1:1 + T], ps[:, T:2 * T]))
            act.wait_ge(*nth("dn_silu", 6))
            o.tell(nc.scalar.activation(flat(SQD), flat(QKV[:, 0:16, :]), ACT.Square), ev["dn_sq"])
            act.wait_ge(*nth("dn_sq", 1))
            for n in range(8):
                act.wait_ge(*nth("l2_mm", n + 1))
                o.tell(nc.scalar.activation(flat(SQD)[:, BLK * n:BLK * (n + 1)], PQ[:, n % 4, :], ACT.Sqrt, bias=EPSC),
                       ev["l2_root"])
            act.wait_ge(*nth("g_abs", 1))
            o.done(nc.scalar.activation(DST[:, 1], DST[:, 1], ACT.Exp, scale=-1.0))
            nc.scalar.activation(DST[:, 1], DST[:, 1], ACT.Ln, bias=1.0)
            nc.scalar.activation(DST[:, 5, 0, :], ROW[:, 16:24], ACT.Exp)
            o.tell(nc.scalar.activation(DST[:, 4], GB[:, :, 8:16], ACT.Sigmoid), ev["g_act"])
            act.wait_ge(*nth("gc_out", 1))
            nc.scalar.activation(DST[:, 8], DST[:, 6], ACT.Exp)
            o.tell(nc.scalar.activation(DST[:, 9], DST[:, 9], ACT.Exp), ev["gc_exp"])
            act.wait_ge(*nth("dec_arg", 1))
            o.tell(nc.scalar.activation(flat(DEC), flat(DEC), ACT.Exp), ev["dec_out"])
            for n in range(4):
                act.wait_ge(*nth("qd_turned", n + 1))
                o.tell(nc.scalar.copy(flat(ATN)[:, BLK * n:BLK * (n + 1)], PP[:, n // 2, n % 2, :]), ev["atn_out"])
            for n in range(4):
                act.wait_ge(*nth("a_turned", n + 1))
                o.tell(nc.scalar.copy(flat(AT_)[:, BLK * n:BLK * (n + 1)], PQ[:, n, :]), ev["at_out"])
            for n in range(4):
                act.wait_ge(*nth("v_turned", n + 1))
                o.tell(nc.scalar.copy(VT[:, n // 2, 4 * (n % 2):4 * (n % 2) + 4, :],
                                      PP[:, n // 2, n % 2, :].rearrange("p (h d) -> p h d", h=4)), ev["v_tok"])
            inverse_act(act, 0)
            act.wait_ge(ev["qs_mm"], 1)
            for h in range(DH):
                o.tell(nc.scalar.mul(OTM[:, h, :], PP[:, 0, h // 4, (h % 4) * P:(h % 4 + 1) * P], DST[:, 8, 1, h:h + 1]),
                       ev["qs_out"])
            act.wait_ge(ev["od_ready"], 1)
            o.done(nc.scalar.activation(flat(VT), flat(OD), ACT.Square), ev["od_sq"])
            act.wait_ge(ev["od_sum"], 1)
            o.tell(nc.scalar.activation(DST[:, 1], DST[:, 0], ACT.Sqrt, scale=1.0 / P, bias=EPSC), ev["od_root"])
            for hf in range(2):
                rw_act(act, o, hf, half, freed)
            sums(4, MEMX, (ev["mem_in"], 32))
            for name, dst in (("xk", XK), ("xv", None)):
                ps = half(name, 0)
                if dst is None:
                    freed(nc.scalar.copy(XV[:, 1, :], ps))
                else:
                    freed(nc.scalar.copy(flat(dst[:, 2:4, :]), ps))
            sums(5, X, (ev["dve_free"], DVE0["xk"]))
            freed(nc.scalar.copy(flat(XQ[:, 2:4, :]), half("xq", 0)))
            act.wait_ge(*nth("xa_max", 1))
            for n in range(8):
                ins = nc.scalar.activation(XP[:, n // 2, n % 2, :], PQ[:, n // 2, (n % 2) * T:(n % 2 + 1) * T], ACT.Exp,
                                           scale=QK_SCALE, bias=XST[:, 0, n:n + 1], accum_out=XST[:, 1, n:n + 1])
            o.tell(ins, ev["xa_exp"])
            for n in range(4):
                act.wait_ge(*nth("xa_turned", n + 1))
                o.tell(nc.scalar.copy(flat(XPT[:, n]), PP[:, n // 2, n % 2, :]), ev["xa_pt"])
            for n in range(4):
                act.wait_ge(*nth("xa_o", n + 1))
                ins = nc.scalar.copy(XO[:, n * T:(n + 1) * T], PQ[:, n, 0:T])
            o.tell(ins, ev["xo_ready"])
            sums(6, X, (ev["dve_free"], DVE0["ffn"]))
            two_act(act, "ffn", FB, ACT.Relu)
            sums(7, X, (ev["dve_free"], DVE0["ffn"] + 4 * FB))

        def rw_act(act, o, hf, half, freed):
            for w in range(3):
                ps = half("rw", 3 * hf + w)
                freed(nc.scalar.copy(RAW[:, w, 2:4, 1:1 + T], ps.rearrange("p (n t) -> p n t", n=2)))
            if hf == 0:
                act.wait_ge(ev["lw_shift"], 1)
                nc.scalar.activation(LW[0:64, 0:T], LW[0:64, 0:T], ACT.Tanh)
                o.tell(nc.scalar.activation(LG[:, 0:T], LG[:, 0:T], ACT.Sigmoid), ev["lw_act"])
            for n, (dst, bias) in enumerate(((LDX, "w0"), (AA, "a0"), (GATE, None))):
                act.wait_ge(ev["lora_mm"], 3 * hf + n + 1)
                for j in range(J):
                    b = 2 * (n % 2) + j // 2
                    src = PQ[:, b, (j % 2) * T:(j % 2 + 1) * T]
                    if bias:
                        ins = nc.scalar.activation(dst[:, j, :], src, ACT.Sigmoid, bias=col2(bias, J * hf + j))
                    else:
                        ins = nc.scalar.copy(dst[:, j, :], src)
                o.tell(ins, ev["lora_out"])
            act.wait_ge(ev["kk_mm"], hf + 1)
            o.tell(nc.scalar.activation(flat(E1), PQ[:, 2:4, :].rearrange("p a b -> p (a b)"), ACT.Sqrt), ev["kk_root"])
            for n in range(9):
                act.wait_ge(ev["decay_arg"], 9 * hf + n + 1)
                w = 1024 if n < 3 else 512
                o.tell(nc.scalar.activation(flat(E2)[:, 0:w], flat(E1)[:, 0:w], ACT.Exp, scale=-1.0 if n == 1 else 1.0),
                       ev["decay_exp"])
            for n in range(2):
                act.wait_ge(ev["rv_turned"], 2 * hf + n + 1)
                o.tell(nc.scalar.copy(VTK[:, n, :], PP[:, n, 0, :]), ev["rv_tok"])
            for n in range(2):
                act.wait_ge(ev["bk_turned"], 2 * hf + n + 1)
                o.tell(nc.scalar.copy(BKT[:, n, :], PP[:, n, 1, :]), ev["bk_tok"])
            for m in range(16):
                act.wait_ge(ev["gram_diag"], 16 * hf + m + 1)
                o.tell(nc.scalar.copy(GR[0:64, m, :, 64:P], PP[0:64, (m % 4) // 2, m % 2, 0:256].rearrange("p (a t) -> p a t", a=4)),
                       ev["gram_out"])
            inverse_act(act, 1 + hf)
            act.wait_ge(ev["gn_mean"], hf + 1)
            o.tell(nc.scalar.activation(flat(RY2), flat(RY), ACT.Square), ev["gn_sq"])
            act.wait_ge(ev["gn_sum"], hf + 1)
            o.tell(nc.scalar.activation(RST[:, 1, :], RST[:, 0, :], ACT.Sqrt, scale=1.0 / 64, bias=RWEPSC), ev["gn_root"])


        @block.scalar
        def _(act):
            o = Own(act, ev["act_order"])
            copy = nc.scalar.activation

            def half(name, j):
                act.wait_ge(used, SLOT0[name] + 4 * (j + 1))
                return PP[:, (UNIT0[name] + j) % 2, 1, :]

            def freed(ins):
                o.tell(ins, ev["act_free"])

            def sums(i, src, ready):
                act.wait_ge(*ready)
                for t in range(NT):
                    o.done(nc.scalar.activation(SCR[:, t, :], src[:, t, :], ACT.Square, accum_out=SS[:, t:t + 1]))
                o.tell(nc.scalar.activation(RS, SS, ACT.Sqrt, scale=1.0 / D, bias=EPSC), ev["norm_root"])

            for _ in range(2):
                act.nop().then_inc(ev["act_free"], 1)
            act.wait_ge(ev["dve_init"], 2)
            sums(0, X, (ev["x_loaded"], 32))
            for j in range(12):
                if j == 2:
                    gates_act(act, o)
                ps = half("win", j)
                if j < 2:
                    freed(nc.scalar.copy(MQK[:, 4 * j + 2:4 * j + 4, 3:3 + T], ps.rearrange("p (n t) -> p n t", n=2)))
                elif j < 4:
                    freed(nc.scalar.mul(flat(FQ[:, 4 * (j - 2) + 2:4 * (j - 2) + 4, :]), ps, QK_SCALE))
                elif j < 6:
                    freed(nc.scalar.copy(flat(FK[:, 4 * (j - 4) + 2:4 * (j - 4) + 4, :]), ps))
                elif j < 8:
                    freed(nc.scalar.copy(FV[:, 1, BLK * (j - 6):BLK * (j - 5)], ps))
                elif j < 10:
                    freed(nc.scalar.copy(MV1[:, 1, 2 * (j - 8):2 * (j - 8) + 2, 0:MV], ps.rearrange("p (h v) -> p h v", h=2)))
                else:
                    freed(nc.scalar.copy(MO[:, 1, BLK * (j - 10):BLK * (j - 9)], ps))
            act.wait_ge(*nth("conv_out", 1))
            o.done(nc.scalar.activation(flat(MQC), flat(MQC), ACT.Silu), ev["qk_silu"])
            act.wait_ge(*nth("mo_ready", 1))
            act.wait_ge(ev["act_free"], 2 + 12)
            o.done(nc.scalar.activation(flat(MO), flat(MO), ACT.Sigmoid), ev["mo_gate"])
            for h in range(FH):
                act.wait_ge(ev["fox_max"], h + 1)
                b = h % 2
                nc.scalar.activation(FP[:, b, 0:P], FS[:, b, 0:P], ACT.Exp, bias=FST[:, b, 0:1], accum_out=FST[:, b, 2:3])
                o.tell(nc.scalar.activation(FP[:, b, P:384], FS[:, b, P:384], ACT.Exp, bias=FST[:, b, 1:2],
                                            accum_out=FST[:, b, 3:4]), ev["fox_exp"])
                act.wait_ge(ev["fox_turned"], h + 1)
                if h >= 2:
                    act.wait_ge(ev["fox_pv"], h - 1)
                o.tell(nc.scalar.copy(FPT[:, b, :], PQ[:, 2 + b, 0:384]), ev["fox_pt"])
            mlstm_act(act, o)
            act.wait_ge(*nth("mix_ready", 2))
            o.done(nc.scalar.activation(flat(SCR), flat(MIX), ACT.Square), ev["mix_sq"])
            act.wait_ge(*nth("mix_sum", 1))
            nc.scalar.activation(HN[:, 1, 0:16], HN[:, 0, 0:16], ACT.Sqrt, scale=1.0 / P, bias=EPSC)
            o.tell(nc.scalar.activation(HN[:, 1, 16:24], HN[:, 0, 16:24], ACT.Sqrt, scale=1.0 / MV, bias=EPSC),
                   ev["mix_root"])
            sums(1, X, (ev["dve_free"], DVE0["wq"]))
            for j in range(4):
                ps = half("wq", j)
                freed(nc.scalar.copy(flat(PQT[:, 4 * j + 2:4 * j + 4, :]), ps))
            for n in range(8):
                act.wait_ge(*nth("scores_mm", n + 1))
                o.tell(nc.scalar.copy(flat(SC)[:, BLK * n:BLK * (n + 1)], PQ[:, n % 4, :]), ev["scores_out"])
            act.wait_ge(*nth("gate_arg", 1))
            o.tell(nc.scalar.activation(flat(SF), flat(SF), ACT.Exp), ev["gate_exp"])
            for _ in range(2):
                act.nop().then_inc(ev["bank_empty"], 1)
            gview = G.rearrange("p j t -> p t j")
            with act.Fori(0, T // 8, 1) as i:
                for b in range(2):
                    act.wait_ge(ev["rows_used"], 2 * i + b + 3)
                    nc.scalar.copy(gview[:, bass.ds(8 * i + 4 * b, 4), :],
                                   PQ[:, b, :].rearrange("p (t j) -> p t j", t=4)).then_inc(ev["bank_empty"], 1)
            two_act(act, "peer", EB, ACT.Gelu)
            stage2_act(act, o, half, freed, sums)
        def mlstm_dve(dve, o, v):
            B = CS[:, 0:2, 12:16]
            o.done(v.tensor_tensor(RC, GT[:, :, 8:12], B, ALU.subtract))
            o.done(v.tensor_tensor(DGM.rearrange("p c h s -> p (c h) s"), rep(ID, 8),
                                   bc(RC.rearrange("p c h -> p (c h)"), P), ALU.mult), ev["m_diag"])
            dve.wait_ge(*nth("r_mm", 1))
            R = [PQ[:, c, :].rearrange("p (h s) -> p h s", h=MH) for c in range(NT)]
            o.done(v.tensor_reduce(MREC[:, 0, :], R[0], AX.X, ALU.max))
            for c in range(NT):
                o.tell(v.tensor_tensor(DM[:, c], R[c], rep(TRI[:, P:2 * P], MH), ALU.add), ev["r_read"])
            dve.wait_ge(*nth("r_read", 2))
            o.done(v.tensor_reduce(RM, DM, AX.X, ALU.max))
            BL = CS[:, 2, 12:16]
            W = TM[:, 0, :]
            o.done(v.tensor_tensor(W[:, 0:4], BL, MREC[:, 0, :], ALU.add))
            o.done(v.tensor_tensor(W[:, 0:4], BL, W[:, 0:4], ALU.max))
            o.done(v.tensor_tensor(RM, RM, B, ALU.add))
            o.done(v.tensor_tensor(MT[:, 0], B[:, 0], RM[:, 0], ALU.max))
            o.done(v.tensor_tensor(W[:, 4:8], B[:, 1], W[:, 0:4], ALU.add))
            o.done(v.tensor_tensor(MT[:, 1], W[:, 4:8], RM[:, 1], ALU.max))
            o.done(v.tensor_tensor(INTER, W[:, 4:8], MT[:, 1], ALU.subtract))
            o.done(v.tensor_tensor(EXB, B, MT, ALU.subtract))
            o.done(v.tensor_tensor(W[:, 8:12], BL, W[:, 0:4], ALU.subtract))
            o.done(v.tensor_tensor(KCOL, RC[:, 0], W[:, 8:12], ALU.add))
            o.done(v.tensor_tensor(DM, DM, bc(EXB, P), ALU.add), ev["m_arg"])
            dve.wait_ge(*nth("m_exp", 1))
            for c in range(NT):
                dve.wait_ge(*nth("qk_mm", c + 1))
                o.done(v.scalar_tensor_tensor(SMM[:, c], PP[:, c, 0, :].rearrange("p (h s) -> p h s", h=MH), QK_SCALE,
                                              DM[:, c], ALU.mult, ALU.mult), ev["sm_ready"])
            dve.wait_ge(*nth("k_turned", 1))
            o.done(v.tensor_scalar(KCOL, KCOL, QK_SCALE, None, ALU.mult))
            o.done(v.tensor_tensor(KA, PQ[:, 2, :].rearrange("p (h s) -> p h s", h=MH), bc(KCOL, P), ALU.mult),
                   ev["ka_ready"])
            for h in range(MH):
                dve.wait_ge(*nth("num0_mm", h + 1))
                ins = v.tensor_copy(NUM[:, 0, h, :], PP[:, h // 2, h % 2, 0:MV + 1])
                o.tell(ins, ev["num0_out"])
            for h in range(MH):
                dve.wait_ge(*nth("num1_mm", h + 1))
                dve.wait_ge(*nth("inter_out", h + 1))
                o.tell(v.tensor_tensor(NUM[:, 1, h, :], PP[:, h // 2, h % 2, 0:MV + 1], TMP[:, h, :], ALU.add), o.order)
            dve.wait_ge(*nth("num0_out", 4))
            dve.wait_ge(o.order, o.n[id(o.order)])
            DEN = NUM[:, :, :, MV:MV + 1].rearrange("p c h o -> p c (h o)")
            o.done(v.scalar_tensor_tensor(MREC, DEN, -1.0, DEN, ALU.mult, ALU.max))
            o.done(v.tensor_tensor(MREC, MREC, EM, ALU.max))
            o.done(v.reciprocal(MREC, MREC))
            dve.wait_ge(*nth("mo_gate", 1))
            for c in range(NT):
                for h in range(MH):
                    ins = v.scalar_tensor_tensor(MIX[:, c, 1024 + MV * h:1024 + MV * (h + 1)], NUM[:, c, h, 0:MV],
                                                 MREC[:, c, h:h + 1], MO[:, c, MV * h:MV * (h + 1)], ALU.mult, ALU.mult)
                o.tell(ins, ev["mix_ready"])

        def select_dve(dve, o, v):
            dve.wait_ge(*nth("scores_out", 8))
            I16U, PFU = I16.bitcast(U32), PF.bitcast(U32)
            rows = [(SC[:, t, n, :], SW[:, t, n, :], S16[:, t, n, :], I16U[:, t, n, :]) for t in range(NT) for n in range(16)]
            top16(o, v, rows)
            o.done(v.tensor_copy(flat(IF), flat(I16U)))
            s16 = S16.rearrange("p t (h q) k -> p t h q k", q=2)
            for t in range(NT):
                for h in range(PH):
                    ins = v.tensor_tensor(CD[:, t, h, :].rearrange("p (a b) -> p a b", a=TOPK), bc(s16[:, t, h, 0, :], TOPK),
                                          rep(s16[:, t, h, 1, :], TOPK), ALU.add)
            o.done(ins)
            rows = [(CD[:, t, h, :], CW[:, t, h, :], SF[:, t, h, :], PFU[:, t, h, :]) for t in range(NT) for h in range(PH)]
            top16(o, v, rows)
            o.done(v.tensor_copy(GS[:, 0], SF[:, :, :, 0]))
            o.done(v.tensor_tensor(SF.rearrange("p t h k -> p (t h) k"), SF.rearrange("p t h k -> p (t h) k"),
                                   bc(GS[:, 0].rearrange("p t h -> p (t h)"), TOPK), ALU.subtract), ev["gate_arg"])
            o.done(v.tensor_scalar(PA.bitcast(U32), PFU, 4, None, ALU.logical_shift_right))
            o.done(v.tensor_scalar(PB.bitcast(U32), PFU, 15, None, ALU.bitwise_and))
            o.done(v.tensor_copy(flat(PA), flat(PA.bitcast(U32))))
            o.done(v.tensor_copy(flat(PB), flat(PB.bitcast(U32))))
            i16 = IF.rearrange("p t (h q) k -> p t h q k", q=2)
            for t in range(NT):
                for q, place in ((0, PA), (1, PB)):
                    o.done(v.tensor_tensor(OH, bc(place[:, t].rearrange("p h k -> p (h k)"), TOPK), rep(IOTA[:, 0:TOPK], P),
                                           ALU.is_equal))
                    for h in range(PH):
                        ins = v.tensor_tensor(OH2[:, TOPK * h:TOPK * (h + 1), :], OH[:, TOPK * h:TOPK * (h + 1), :],
                                              rep(i16[:, t, h, q, :], TOPK), ALU.mult)
                    o.done(ins)
                    o.done(v.tensor_reduce(SEL[:, q, t, :], OH2, AX.X, ALU.add), ev["sel_ready"])
            dve.wait_ge(*nth("gate_exp", 1))
            o.done(v.tensor_reduce(GS[:, 1], SF, AX.X, ALU.add))
            o.done(v.reciprocal(GS[:, 2], GS[:, 1]))
            o.done(v.tensor_tensor(GA.rearrange("p t (h k) -> p (t h) k", k=TOPK), SF.rearrange("p t h k -> p (t h) k"),
                                   bc(GS[:, 2].rearrange("p t h -> p (t h)"), TOPK), ALU.mult), ev["gate_ready"])
            dve.wait_ge(*nth("hk_turned", 1))
            o.tell(v.tensor_copy(HKT[:, 0:512], PQ[:, 0, :]), o.order)
            dve.wait_ge(o.order, o.n[id(o.order)])
            o.done(v.tensor_copy(HKT[:, 512:768], PQ[:, 1, 0:256]), ev["hk_ready"])

        def top16(o, v, rows):
            def wave(make):
                for r in rows:
                    ins = make(*r)
                o.done(ins)
            wave(lambda s, w, top, idx: v.max(top[:, 0:8], s))
            wave(lambda s, w, top, idx: v.max_index(idx[:, 0:8], top[:, 0:8], s))
            wave(lambda s, w, top, idx: v.match_replace(w, top[:, 0:8], s, -3e38))
            wave(lambda s, w, top, idx: v.max(top[:, 8:16], w))
            wave(lambda s, w, top, idx: v.max_index(idx[:, 8:16], top[:, 8:16], w))

        def two_dve(dve, o, v, name, blocks):
            base, acted, ready = SLOT0[name], ev[name + "_acted"], ev[name + "_ready"]
            buf = [ACTB[:, 0:1024], ACTB[:, 1024:2048]]

            def hidden(b, par):
                dve.wait_ge(acted, b + 1)
                if name == "peer":
                    g = G[:, bass.ds(4 * b, 4), :].rearrange("p j t -> p (j t)")
                    v.tensor_tensor(buf[par], buf[par], g, ALU.mult).then_inc(ready, 1)
                else:
                    v.tensor_tensor(buf[par], buf[par], buf[par], ALU.mult).then_inc(ready, 1)

            def add(b, first):
                for nb in range(4):
                    dve.wait_ge(used, first + nb + 1)
                    cols = slice(BLK * nb, BLK * (nb + 1))
                    v.tensor_tensor(X[:, :, cols], X[:, :, cols], PP[:, (UNIT0[name] + nb) % 2],
                                    ALU.add).then_inc(ev["dve_free"], 1)

            hidden(0, 0)
            with dve.Fori(0, blocks // 2 - 1, 1) as i:
                for par in range(2):
                    hidden(2 * i + (par + 1), 1 - par)
                    dve.wait_ge(ev["dve_free"], 8 * i + (DVE0[name] + 4 * par))
                    add(None, 16 * i + (base + 8 + 8 * par))
            hidden(blocks - 1, 1)
            dve.wait_ge(ev["dve_free"], DVE0[name] + 4 * (blocks - 2))
            add(None, base + 8 * (blocks - 2) + 8)
            dve.wait_ge(ev["dve_free"], DVE0[name] + 4 * (blocks - 1))
            add(None, base + 8 * (blocks - 1) + 4)
            dve.wait_ge(ev["dve_free"], DVE0[name] + 4 * blocks)
            o.n[id(ev["dve_free"])] = DVE0[name] + 4 * blocks

        def inverse_dve(dve, o, v, c, A, At, Ti, Tt):
            o.done(v.tensor_tensor(Ti, A, rep(LV[0], 16), ALU.mult))
            o.done(v.tensor_tensor(Tt, At, rep(LV[0], 16), ALU.mult))
            v.tensor_tensor(Ti, rep(ID, 16), Ti, ALU.subtract)
            o.done(v.tensor_tensor(Tt, rep(ID, 16), Tt, ALU.subtract))
            for _ in range(4):
                v.nop().then_inc(ev["inv_new"], 1)
            with dve.Fori(1, 7, 1) as l:
                def between(q):
                    dve.wait_ge(ev["inv_m1"], 4 * l + (24 * c - 4 + q) + 1)
                    v.tensor_tensor(AOFB[:, q % 2], At[:, 4 * q:4 * q + 4, :],
                                    LVA[:, bass.ds(l, 1), :].broadcast_to([P, 4, P]), ALU.mult).then_inc(ev["inv_off"], 1)

                def update(q):
                    dve.wait_ge(ev["inv_t"], 4 * l + (24 * c - 4 + q) + 3)
                    m = slice(4 * q, 4 * q + 4)
                    v.tensor_tensor(Ti[:, m, :], Ti[:, m, :], PQ[:, 2 + q % 2, :].rearrange("p (m j) -> p m j", m=4),
                                    ALU.subtract)
                    v.tensor_tensor(Tt[:, m, :], Tt[:, m, :], PP[:, q % 2, 0, :].rearrange("p (m j) -> p m j", m=4),
                                    ALU.subtract).then_inc(ev["inv_new"], 1)
                between(0)
                between(1)
                update(0)
                between(2)
                update(1)
                between(3)
                update(2)
                update(3)
            dve.wait_ge(ev["inv_new"], 28 * (c + 1))

        def stage2_dve(dve, o, v, half, freed, turn_out, scale_rows, add_pair):
            dve.wait_ge(ev["norm_root"], 3)
            o.done(v.reciprocal(RSTD, RS))
            dve.wait_ge(ev["fnw_in"], 16)
            for t in range(NT):
                o.tell(v.scalar_tensor_tensor(X[:, t, :], X[:, t, :], RSTD[:, t:t + 1], FNW, ALU.mult, ALU.mult),
                       ev["block1_out"])
            dve.wait_ge(ev["block1_out"], 2)
            scale_rows(3, X)
            dve.wait_ge(ev["consts2"], 32)
            turn_out(3, XT, col2("mix2", 0, 16))
            o.done(v.memset(CIN[:, :, 0:3], 0.0), ev["cin_pad"])
            for j in range(8):
                ps = half("dn", j)
                if j < 6:
                    c = 4 * (j % 2)
                    freed(v.tensor_copy(CIN[:, c:c + 2, 3:3 + T], ps.rearrange("p (n t) -> p n t", n=2)))
                    dve.wait_ge(ev["dve_free"], DVE0["dn"] + j + 1)
                    dve.wait_ge(ev["act_free"], ACT0["dn"] + j + 1)
                    for tap in range(4):
                        for n in range(4):
                            w = col2("dcw", 4 * (4 * j + n) + tap)
                            if tap == 0:
                                ins = v.tensor_scalar(QKV[:, 4 * j + n, :], CIN[:, c + n, 0:T], w, None, ALU.mult)
                            else:
                                ins = v.scalar_tensor_tensor(QKV[:, 4 * j + n, :], CIN[:, c + n, tap:tap + T], w,
                                                             QKV[:, 4 * j + n, :], ALU.mult, ALU.add)
                        o.done(ins, ev["dn_conv"] if tap == 3 else None)
                else:
                    freed(v.tensor_copy(ZT[:, 0, BLK * (j - 6):BLK * (j - 5)], ps))
            ps = half("small", 0)
            freed(v.tensor_copy(flat(GB), ps[:, 0:32]))
            dve.wait_ge(ev["dve_free"], DVE0["rw"])
            o.done(v.tensor_tensor(DST[:, 0], GB[:, :, 0:8], rep(ROW[:, 24:32], NT), ALU.add))
            o.done(v.scalar_tensor_tensor(DST[:, 1], DST[:, 0], -1.0, DST[:, 0], ALU.mult, ALU.max), ev["g_abs"])
            o.done(v.tensor_scalar(DST[:, 2], DST[:, 0], 0.0, None, ALU.max))
            for n in range(8):
                dve.wait_ge(*nth("l2_root", n + 1))
                sl = flat(SQD)[:, BLK * n:BLK * (n + 1)]
                o.tell(v.reciprocal(sl, sl), o.order)
            dve.wait_ge(o.order, o.n[id(o.order)])
            v.scalar_tensor_tensor(flat(QKV[:, 0:8, :]), flat(QKV[:, 0:8, :]), QK_SCALE, flat(SQD[:, 0:8, :]), ALU.mult, ALU.mult)
            o.done(v.tensor_tensor(flat(QKV[:, 8:16, :]), flat(QKV[:, 8:16, :]), flat(SQD[:, 8:16, :]), ALU.mult), ev["dn_qk"])
            dve.wait_ge(*nth("g_act", 1))
            o.done(v.tensor_tensor(DST[:, 2], DST[:, 2], DST[:, 1], ALU.add))
            o.done(v.scalar_tensor_tensor(DST[:, 3], DST[:, 2], -1.0, rep(DST[:, 5, 0, :], NT), ALU.mult, ALU.mult), ev["g_ready"])
            dve.wait_ge(*nth("gc_mm", 1))
            o.done(v.tensor_copy(DST[:, 6:8].rearrange("p a t h -> p (a t h)"), PQ[:, 0, 0:32]))
            o.done(v.tensor_tensor(DST[:, 9], DST[:, 7], DST[:, 6], ALU.subtract), ev["gc_out"])
            o.done(v.tensor_scalar(DST[:, 11], DST[:, 6], -1.0, None, ALU.mult))
            dve.wait_ge(ev["masks"], 22)
            o.done(v.tensor_tensor(DGD, rep(ID, 16), bc(DST[:, 11].rearrange("p t h -> p (t h)"), P), ALU.mult), ev["dn_diag"])
            for m in range(16):
                if m % 4 == 0:
                    dve.wait_ge(*nth("dec_mm", m // 4 + 1))
                t, h = m // 8, m % 8
                ins = v.scalar_tensor_tensor(DEC[:, t, h, :], PQ[:, m // 4, (m % 4) * P:(m % 4 + 1) * P],
                                             DST[:, 6, t, h:h + 1], TRI[:, P:2 * P], ALU.add, ALU.add)
            o.done(ins, ev["dec_arg"])
            dve.wait_ge(*nth("gc_exp", 1))
            o.done(v.tensor_scalar(DST[:, 10], DST[:, 8], -1.0, None, ALU.mult))
            dve.wait_ge(*nth("dec_out", 1))
            for m in range(16):
                if m % 4 == 0:
                    dve.wait_ge(*nth("kk_gram", m // 4 + 1))
                t, h = m // 8, m % 8
                ins = v.scalar_tensor_tensor(AM[:, m, :], PP[:, m // 8, (m // 4) % 2, (m % 4) * P:(m % 4 + 1) * P],
                                             DST[:, 4, t, h:h + 1], DEC[:, t, h, :], ALU.mult, ALU.mult)
            o.done(ins)
            o.done(v.tensor_tensor(AM, AM, rep(LS, 16), ALU.mult), ev["a_ready"])
            for n in range(4):
                dve.wait_ge(*nth("qk_gram", n + 1))
                o.tell(v.tensor_tensor(flat(TTI)[:, BLK * n:BLK * (n + 1)], PQ[:, n, :],
                                       DEC.rearrange("p t h s -> p (t h s)")[:, BLK * n:BLK * (n + 1)], ALU.mult), ev["qd_ready"])
            dve.wait_ge(*nth("kd_turned", 1))
            for n in range(2):
                ins = v.tensor_tensor(KD[:, 4 * n:4 * n + 4, :], PQ[:, n, :].rearrange("p (h d) -> p h d", h=4),
                                      bc(DST[:, 9, 0, 4 * n:4 * n + 4], P), ALU.mult)
            o.done(ins, ev["kd_ready"])
            dve.wait_ge(*nth("at_out", 4))
            dve.wait_ge(*nth("atn_out", 4))
            inverse_dve(dve, o, v, 0, AM, AT_, TI, TTI)
            dve.wait_ge(*nth("v_tok", 4))
            o.done(v.tensor_tensor(RH, VT[:, 0], bc(DST[:, 4, 0, :], P), ALU.mult), ev["dn_rhs"])
            dve.wait_ge(ev["vn_mm"], 1)
            o.done(v.tensor_copy(flat(VN), PQ[:, 0:2, :].rearrange("p a b -> p (a b)")), ev["vn_out"])
            dve.wait_ge(ev["o_mm"], 1)
            o.tell(v.tensor_copy(OD[:, 0, :], PQ[:, 2:4, :].rearrange("p a b -> p (a b)")), ev["o_out"])
            dve.wait_ge(ev["s_mm"], 1)
            o.done(v.tensor_copy(flat(SD), PQ[:, 0:2, :].rearrange("p a b -> p (a b)")), ev["s_out"])
            dve.wait_ge(ev["ks_mm"], 1)
            for h in range(DH):
                ins = v.scalar_tensor_tensor(RH[:, h, :], PQ[:, 2 + h // 4, (h % 4) * P:(h % 4 + 1) * P], DST[:, 10, 1, h:h + 1],
                                             VT[:, 1, h, :], ALU.mult, ALU.add)
            o.done(ins)
            o.done(v.tensor_tensor(RH, RH, bc(DST[:, 4, 1, :], P), ALU.mult), ev["dn_rhs"])
            dve.wait_ge(ev["vn_mm"], 2)
            o.done(v.tensor_copy(flat(VN), PQ[:, 0:2, :].rearrange("p a b -> p (a b)")), ev["vn_out"])
            dve.wait_ge(ev["o_mm"], 2)
            dve.wait_ge(*nth("qs_out", 8))
            o.done(v.tensor_tensor(OD[:, 1, :], PQ[:, 2:4, :].rearrange("p a b -> p (a b)"), flat(OTM), ALU.add))
            dve.wait_ge(ev["o_out"], 1)
            o.tell(v.nop(), ev["od_ready"])
            dve.wait_ge(*nth("od_sq", 1))
            o.done(v.tensor_reduce(DST[:, 0], VT, AX.X, ALU.add), ev["od_sum"])
            dve.wait_ge(*nth("od_root", 1))
            o.done(v.reciprocal(DST[:, 0], DST[:, 1]))
            dve.wait_ge(*nth("z_silu", 1))
            for t in range(NT):
                odt = OD[:, t, :].rearrange("p (h d) -> p h d", h=DH)
                o.done(v.tensor_tensor(odt, odt, bc(DST[:, 0, t, :], P), ALU.mult))
                o.tell(v.tensor_tensor(OD[:, t, :], OD[:, t, :], ZT[:, t, :], ALU.mult), ev["tp_scaled"])
            turn_out(4, YT, col2("dnw"), 8)
            o.tell(v.nop(), ev["dn_done"])
            for hf in range(2):
                rw_dve(dve, o, v, hf, half, freed)
            for j in range(4):
                add_pair("out2", j)
            scale_rows(4, MEMX)
            turn_out(5, MEMT, col2("mem", 0, 16))
            freed(v.tensor_copy(flat(XK[:, 0:2, :]), half("xk", 0)))
            freed(v.tensor_copy(XV[:, 0, :], half("xv", 0)))
            scale_rows(5, X)
            turn_out(6, XT, col2("xa", 0, 16))
            freed(v.tensor_copy(flat(XQ[:, 0:2, :]), half("xq", 0)))
            dve.wait_ge(*nth("xa_mm", 1))
            o.done(v.tensor_reduce(XST[:, 0, :].rearrange("p (h t) -> p h t", t=NT), PQ[:, :, :].rearrange("p h (t m) -> p h t m", t=NT), AX.X, ALU.max))
            o.done(v.tensor_scalar(XST[:, 0, :], XST[:, 0, :], -QK_SCALE, None, ALU.mult), ev["xa_max"])
            dve.wait_ge(*nth("xa_exp", 1))
            o.done(v.reciprocal(XST[:, 2, :], XST[:, 1, :]))
            o.done(v.tensor_tensor(XP.rearrange("p h t m -> p (h t) m"), XP.rearrange("p h t m -> p (h t) m"), bc(XST[:, 2, :], T), ALU.mult), ev["xa_p"])
            for nb in range(4):
                dve.wait_ge(used, SLOT0["xo"] + nb + 1)
                cols = slice(BLK * nb, BLK * (nb + 1))
                freed(v.tensor_tensor(X[:, :, cols], X[:, :, cols], PP[:, (UNIT0["xo"] + nb) % 2], ALU.add))
            dve.wait_ge(ev["dve_free"], DVE0["ffn"])
            scale_rows(6, X)
            turn_out(7, XT, col2("ffn", 0, 16))
            two_dve(dve, o, v, "ffn", FB)
            dve.wait_ge(ev["norm_root"], 8)
            o.done(v.reciprocal(RSTD, RS))
            dve.wait_ge(ev["fnw_in"], 32)
            for t in range(NT):
                o.tell(v.scalar_tensor_tensor(X[:, t, :], X[:, t, :], RSTD[:, t:t + 1], FNW, ALU.mult, ALU.mult), ev["final"])

        def rw_dve(dve, o, v, hf, half, freed):
            def mu(x, c, w):
                return v.scalar_tensor_tensor(x[0], x[1], c, x[2], ALU.mult, ALU.add)
            o.done(v.memset(RAW[:, :, :, 0:1], 0.0))
            for w in range(3):
                ps = half("rw", 3 * hf + w)
                freed(v.tensor_copy(RAW[:, w, 0:2, 1:1 + T], ps.rearrange("p (n t) -> p n t", n=2)))
                dve.wait_ge(ev["dve_free"], DVE0["rw"] + 3 * hf + w + 1)
                dve.wait_ge(ev["act_free"], ACT0["rw"] + 3 * hf + w + 1)
                o.done(v.tensor_tensor(E1, RAW[:, w, :, 0:T], RAW[:, w, :, 1:1 + T], ALU.subtract))
                for j in range(J):
                    ins = v.scalar_tensor_tensor(RKV[:, w, j, :], E1[:, j, :], col2(("mur", "muk", "muv")[w], J * hf + j),
                                                 RAW[:, w, j, 1:1 + T], ALU.mult, ALU.add)
                o.done(ins)
            R, K, V = (RKV[:, w] for w in range(3))
            if hf == 0:
                for x, c in ((LW, "muw"), (LG, "mug")):
                    o.done(v.tensor_tensor(E1[:, 0, :], x[:, 0:T], x[:, 1:1 + T], ALU.subtract))
                    o.done(v.scalar_tensor_tensor(E1[:, 1, :], E1[:, 0, :], col2(c), x[:, 1:1 + T], ALU.mult, ALU.add))
                    o.done(v.tensor_copy(x[:, 0:T], E1[:, 1, :]))
                o.tell(v.nop(), ev["lw_shift"])
            dve.wait_ge(ev["lora_out"], 3 * hf + 2)
            o.done(v.tensor_scalar(flat(LDX), flat(LDX), -DECAY, None, ALU.mult))
            for j in range(J):
                for t in range(NT):
                    ins = v.tensor_tensor_scan(CUM[:, j, t * P:(t + 1) * P], ONES, LDX[:, j, t * P:(t + 1) * P], 0.0,
                                               ALU.mult, ALU.add)
            o.done(ins)
            o.done(v.tensor_tensor(LDX, CUM, LDX, ALU.subtract))
            for j in range(J):
                ins = v.tensor_scalar(KKN[:, j, :], K[:, j, :], col2("kk", J * hf + j), None, ALU.mult)
            o.done(ins)
            o.done(v.tensor_tensor(E1, KKN, KKN, ALU.mult), ev["kk_sq"])
            dve.wait_ge(ev["kk_root"], hf + 1)
            o.done(v.tensor_scalar(flat(E1), flat(E1), 1e-12, None, ALU.max))
            o.done(v.reciprocal(flat(E1), flat(E1)))
            o.done(v.tensor_tensor(KKN, KKN, E1, ALU.mult))
            for j in range(J):
                ins = v.tensor_scalar(E1[:, j, :], AA[:, j, :], 1.0, col2("ka", J * hf + j), ALU.subtract, ALU.mult)
            o.done(ins)
            o.done(v.scalar_tensor_tensor(flat(K), flat(E1), 1.0, flat(K), ALU.add, ALU.mult))
            o.done(v.tensor_tensor(AA, AA, KKN, ALU.mult))
            for j in range(J):
                ins = v.scalar_tensor_tensor(E1[:, j, :], R[:, j, :], col2("rk", J * hf + j), K[:, j, :], ALU.mult, ALU.mult)
            o.done(ins, ev["rk_ready"])
            dve.wait_ge(ev["bonus_mm"], hf + 1)
            o.done(v.tensor_tensor(flat(BON), PQ[:, 2:4, :].rearrange("p a b -> p (a b)"), flat(V), ALU.mult))
            blocks = lambda x: x.rearrange("p j (b s) -> p (j b) s", s=64)
            tiles = lambda x: x.rearrange("p j (t s) -> p (j t) s", s=P)
            mid = blocks(CUM)[:, :, 31:32].broadcast_to([P, 16, 64])
            edge = tiles(CUM)[:, :, 63:64].broadcast_to([P, 8, 64])
            end = CUM[:, :, P - 1:P].broadcast_to([P, J, P])
            e1b = flat(E1).rearrange("p (b s) -> p b s", s=64)
            lo, hi = (lambda x: tiles(x)[:, :, 0:64]), (lambda x: tiles(x)[:, :, 64:P])
            e1h = flat(E1)[:, 0:512].rearrange("p (b s) -> p b s", s=64)
            e2h = flat(E2)[:, 0:512].rearrange("p (b s) -> p b s", s=64)
            e1s = flat(E1)[:, 0:512].rearrange("p (j s) -> p j s", s=P)
            e2s = flat(E2)[:, 0:512].rearrange("p (j s) -> p j s", s=P)
            osl = lambda x: x.rearrange("p j t s -> p (j t) s")
            t0, t1 = (lambda x: x[:, :, 0:P]), (lambda x: x[:, :, P:T])
            sub = lambda out, x, y: v.tensor_tensor(out, x, y, ALU.subtract)
            mul = lambda out, x, y: v.tensor_tensor(out, x, y, ALU.mult)
            tasks = [
                (lambda: sub(e1b, blocks(CUM), mid), [lambda: mul(KRD[:, :, 1, :], R, E2)]),
                (lambda: None, [lambda: mul(BKD[:, 0], AA, E2), lambda: mul(BKD[:, 1], K, E2)]),
                (lambda: sub(e1b, blocks(LDX), mid), [lambda: mul(KRD[:, :, 0, :], KKN, E2)]),
                (lambda: sub(e1h, hi(CUM), edge), [lambda j=j: mul(KRO[:, j, 1], e2h[:, 2 * j:2 * j + 2, :], hi(R)[:, 2 * j:2 * j + 2, :]) for j in range(J)]),
                (lambda: sub(e1h, hi(LDX), edge), [lambda j=j: mul(KRO[:, j, 0], e2h[:, 2 * j:2 * j + 2, :], hi(KKN)[:, 2 * j:2 * j + 2, :]) for j in range(J)]),
                (lambda: sub(e1h, edge, lo(CUM)), [lambda: mul(osl(BKO[:, 0]), lo(AA), e2h), lambda: mul(osl(BKO[:, 1]), lo(K), e2h)]),
                (lambda: v.tensor_copy(e1s, t1(CUM)), [lambda: mul(KRS[:, 1], t1(R), e2s)]),
                (lambda: v.tensor_copy(e1s, t1(LDX)), [lambda: mul(KRS[:, 0], t1(KKN), e2s)]),
                (lambda: sub(e1s, end, t0(CUM)), [lambda: mul(BKS[:, 0], t0(AA), e2s), lambda: mul(BKS[:, 1], t0(K), e2s)]),
            ]
            for n, (arg, uses) in enumerate(tasks):
                o.done(arg() or v.nop(), ev["decay_arg"])
                dve.wait_ge(ev["decay_exp"], 9 * hf + n + 1)
                for use in uses:
                    ins = use()
                o.done(ins)
            o.tell(v.nop(), ev["decayed"])
            dve.wait_ge(ev["rv_tok"], 2 * hf + 2)
            for m in range(16):
                dve.wait_ge(ev["gram_mm"], 16 * hf + m + 1)
                o.done(v.tensor_tensor(flat(GR[:, m]), PQ[:, m % 4, :], flat(M4), ALU.mult), ev["gram_diag"])
            for n in range(4):
                dve.wait_ge(ev["ram_turned"], 4 * hf + n + 1)
                ins = v.tensor_copy(flat(RAM)[:, BLK * n:BLK * (n + 1)], PQ[:, n, :])
            o.done(ins)
            inverse_dve(dve, o, v, 1 + hf, RAM, GR[:, :, 0, :], RTI, RTT)
            n = 2 * hf
            for t in range(NT):
                dve.wait_ge(ev["rx_mm"], n + t + 1)
                o.done(v.tensor_scalar(RX, PQ[:, 0, :], -1.0, None, ALU.mult), ev["rx_out"])
                dve.wait_ge(ev["sa_mm"], n + t + 1)
                o.done(v.tensor_copy(SAB, PQ[:, 1, :]), ev["sa_out"])
                dve.wait_ge(ev["ry_mm"], n + t + 1)
                o.done(v.tensor_copy(RY[:, t, :], PQ[:, 2, :]), ev["ry_out"])
                if t == 0:
                    dve.wait_ge(ev["rs_mm"], hf + 1)
                    o.done(v.tensor_tensor(S1, PQ[:, 3, :].rearrange("p (j s) -> p j s", j=J), rep(BD[6], J), ALU.mult),
                           ev["rs_out"])
            y3 = flat(RY).rearrange("p (m d) -> p m d", d=64)
            y23 = flat(RY2).rearrange("p (m d) -> p m d", d=64)
            o.done(v.tensor_reduce(RST[:, 0, :], y3, AX.X, ALU.add))
            o.done(v.tensor_scalar(RST[:, 0, :], RST[:, 0, :], 1.0 / 64, None, ALU.mult))
            o.done(v.tensor_tensor(y3, y3, bc(RST[:, 0, :], 64), ALU.subtract), ev["gn_mean"])
            dve.wait_ge(ev["gn_sq"], hf + 1)
            o.done(v.tensor_reduce(RST[:, 0, :], y23, AX.X, ALU.add), ev["gn_sum"])
            dve.wait_ge(ev["gn_root"], hf + 1)
            o.done(v.reciprocal(RST[:, 2, :], RST[:, 1, :]))
            o.done(v.tensor_tensor(y3, y3, bc(RST[:, 2, :], 64), ALU.mult), ev["gn_out"])
            y0 = DH + J * hf
            for t in range(NT):
                dve.wait_ge(ev["ry_turned"], 2 * hf + t + 1)
                for j in range(J):
                    ins = v.tensor_scalar(YT[:, y0 + j, t * P:(t + 1) * P], PP[:, t, 0, j * P:(j + 1) * P],
                                          col2("lnw", J * hf + j), col2("lnb", J * hf + j), ALU.mult, ALU.add)
            o.done(ins)
            yt = flat(YT[:, y0:y0 + J, :])
            o.done(v.tensor_tensor(yt, yt, flat(BON), ALU.add))
            o.done(v.tensor_tensor(yt, yt, flat(GATE), ALU.mult), ev["rw_done"])


        @block.vector
        def _(dve):
            o = Own(dve, ev["dve_order"])
            v = nc.vector

            def half(name, j):
                dve.wait_ge(used, SLOT0[name] + 4 * (j + 1))
                return PP[:, (UNIT0[name] + j) % 2, 0, :]

            def freed(ins):
                o.tell(ins, ev["dve_free"])

            def turn_out(i, dst, weights, tiles=16):
                for t in range(NT):
                    for g in range(tiles // 4):
                        dve.wait_ge(ev["turned"], turn_out.n + 1)
                        turn_out.n += 1
                        w = weights[:, 4 * g:4 * g + 4] if weights.shape[1] > 1 else weights.broadcast_to([P, 4])
                        o.tell(v.tensor_tensor(dst[:, 4 * g:4 * g + 4, t * P:(t + 1) * P],
                                               PQ[:, g, :].rearrange("p (n t) -> p n t", n=4), bc(w, P), ALU.mult),
                               ev["turn_out"])
            turn_out.n = 0

            def scale_rows(i, src):
                dve.wait_ge(ev["norm_root"], i + 1)
                o.done(v.reciprocal(RSTD, RS))
                for t in range(NT):
                    o.tell(v.tensor_scalar(SCR[:, t, :], src[:, t, :], RSTD[:, t:t + 1], None, ALU.mult),
                           ev["tp_scaled"])

            def add_pair(name, j):
                dve.wait_ge(used, SLOT0[name] + 4 * (j + 1))
                cols = slice(BLK * j, BLK * (j + 1))
                freed(v.tensor_tensor(X[:, :, cols], X[:, :, cols], PP[:, (UNIT0[name] + j) % 2], ALU.add))

            for _ in range(2):
                dve.nop().then_inc(ev["dve_free"], 1)
                o.n[id(ev["dve_free"])] = o.n.get(id(ev["dve_free"]), 0) + 1
            v.memset(EPSC, EPS).then_inc(ev["dve_init"], 1)
            v.memset(RWEPSC, RW_EPS).then_inc(ev["dve_init"], 1)
            scale_rows(0, X)
            dve.wait_ge(ev["consts1"], 48)
            turn_out(0, XT, col1("norm1", 0, 16))
            dve.wait_ge(*nth("gate_mm", 1))
            o.done(v.tensor_tensor(GT, PQ[:, 0, 0:32].rearrange("p (t g) -> p t g", t=2), rep(ROW[:, 0:16], NT), ALU.add))
            o.done(v.scalar_tensor_tensor(TM[:, 0:2, :], GT, -1.0, GT, ALU.mult, ALU.max), ev["gate_abs"])
            o.done(v.tensor_scalar(TM[:, 2:4, :], GT, 0.0, None, ALU.min))
            dve.wait_ge(*nth("gate_ln", 1))
            o.done(v.tensor_tensor(LF, TM[:, 2:4, :], TM[:, 0:2, :], ALU.subtract), ev["log_f"])
            dve.wait_ge(*nth("cumsum_mm", 1))
            o.done(v.tensor_copy(flat(CS), PQ[:, 1, 0:64]))
            o.done(v.tensor_copy(FCOL[:, 0, :], CS[:, 0, 0:FH]))
            o.done(v.tensor_tensor(FCOL[:, 1, :], CS[:, 1, 0:FH], CS[:, 2, 0:FH], ALU.add))
            o.done(v.tensor_scalar(NFCOL, FCOL, -1.0, None, ALU.mult))
            dve.wait_ge(ev["masks"], 3)
            o.tell(v.tensor_tensor(DG, rep(ID, 16).rearrange("p (h t) s -> p h t s", t=2),
                                   bc(NFCOL.rearrange("p t h -> p h t"), P), ALU.mult), ev["fox_diag"])
            for j in range(12):
                ps = half("win", j)
                if j < 2:
                    freed(v.tensor_copy(MQK[:, 4 * j:4 * j + 2, 3:3 + T], ps.rearrange("p (n t) -> p n t", n=2)))
                elif j < 4:
                    freed(v.tensor_scalar(flat(FQ[:, 4 * (j - 2):4 * (j - 2) + 2, :]), ps, QK_SCALE, None, ALU.mult))
                elif j < 6:
                    freed(v.tensor_copy(flat(FK[:, 4 * (j - 4):4 * (j - 4) + 2, :]), ps))
                elif j < 8:
                    freed(v.tensor_copy(FV[:, 0, BLK * (j - 6):BLK * (j - 5)], ps))
                elif j < 10:
                    freed(v.tensor_copy(MV1[:, 0, 2 * (j - 8):2 * (j - 8) + 2, 0:MV], ps.rearrange("p (h v) -> p h v", h=2)))
                else:
                    ins = v.tensor_copy(MO[:, 0, BLK * (j - 10):BLK * (j - 9)], ps)
                    freed(ins)
                if j == 2:
                    dve.wait_ge(ev["act_free"], 4)
                    dve.wait_ge(ev["dve_free"], 4)
                    for n in range(8):
                        o.tell(v.tensor_scalar(MQC[:, n, :], MQK[:, n, 0:T], col1("cw", 4 * n), col1("cb", n),
                                               ALU.mult, ALU.add), o.order)
                    dve.wait_ge(o.order, o.n[id(o.order)])
                    for tap in range(1, 4):
                        for n in range(8):
                            ins = v.scalar_tensor_tensor(MQC[:, n, :], MQK[:, n, tap:tap + T], col1("cw", 4 * n + tap),
                                                         MQC[:, n, :], ALU.mult, ALU.add)
                            o.tell(ins, o.order)
                        dve.wait_ge(o.order, o.n[id(o.order)])
                    o.tell(v.nop(), ev["conv_out"])
            dve.wait_ge(ev["dve_free"], 2 + 12)
            o.tell(v.nop(), ev["mo_ready"])
            for h in range(FH + 1):
                if h < FH:
                    b = h % 2
                    dve.wait_ge(ev["fox_scores"], h + 1)
                    if h >= 2:
                        dve.wait_ge(ev["fox_exp"], h - 1)
                    o.tell(v.scalar_tensor_tensor(FS[:, b, 0:P], PQ[:, b, 0:P], FCOL[:, 0, h:h + 1], TRI[:, P:2 * P],
                                                  ALU.add, ALU.add), o.order)
                    o.done(v.scalar_tensor_tensor(FS[:, b, P:384], PQ[:, b, P:384], FCOL[:, 1, h:h + 1], TRI,
                                                  ALU.add, ALU.add))
                    v.tensor_reduce(FST[:, b, 0:1], FS[:, b, 0:P], AX.X, ALU.max, negate=True)
                    o.done(v.tensor_reduce(FST[:, b, 1:2], FS[:, b, P:384], AX.X, ALU.max, negate=True), ev["fox_max"])
                if h >= 1:
                    g, b = h - 1, (h - 1) % 2
                    dve.wait_ge(ev["fox_exp"], g + 1)
                    o.done(v.reciprocal(RM[:, 0, 2 * b:2 * b + 2], FST[:, b, 2:4]))
                    dve.wait_ge(ev["fox_pv"], g + 1)
                    for t in range(NT):
                        ins = v.tensor_scalar(MIX[:, t, g * P:(g + 1) * P], PP[:, b, 0, t * P:(t + 1) * P],
                                              RM[:, 0, 2 * b + t:2 * b + t + 1], None, ALU.mult)
                    o.done(ins, ev["fox_out"])
            mlstm_dve(dve, o, v)
            dve.wait_ge(*nth("mix_sq", 1))
            o.done(v.tensor_reduce(HN[:, 0, 0:16].rearrange("p (t h) -> p t h", t=NT),
                                   SCR[:, :, 0:1024].rearrange("p t (h d) -> p t h d", d=P), AX.X, ALU.add))
            o.done(v.tensor_reduce(HN[:, 0, 16:24].rearrange("p (t h) -> p t h", t=NT),
                                   SCR[:, :, 1024:2048].rearrange("p t (h d) -> p t h d", d=MV), AX.X, ALU.add),
                   ev["mix_sum"])
            dve.wait_ge(*nth("mix_root", 1))
            o.done(v.reciprocal(HN[:, 0, :], HN[:, 1, :]))
            for t in range(NT):
                v.tensor_tensor(SCR[:, t, 0:1024].rearrange("p (h d) -> p h d", d=P),
                                MIX[:, t, 0:1024].rearrange("p (h d) -> p h d", d=P),
                                bc(HN[:, 0, 8 * t:8 * t + 8], P), ALU.mult)
                o.tell(v.tensor_tensor(SCR[:, t, 1024:2048].rearrange("p (h d) -> p h d", d=MV),
                                       MIX[:, t, 1024:2048].rearrange("p (h d) -> p h d", d=MV),
                                       bc(HN[:, 0, 16 + 4 * t:20 + 4 * t], MV), ALU.mult), ev["tp_scaled"])
            turn_out(1, XT, col1("mix", 0, 16))
            for j in range(4):
                add_pair("wout", j)
            scale_rows(1, X)
            turn_out(2, XT, col1("norm2", 0, 16))
            for j in range(4):
                ps = half("wq", j)
                freed(v.tensor_copy(flat(PQT[:, 4 * j:4 * j + 2, :]), ps))
            select_dve(dve, o, v)
            with dve.Fori(0, T // 8, 1) as i:
                for b in range(2):
                    dve.wait_ge(ev["rows_used"], 2 * i + b + 1)
                    for t in range(4):
                        ins = v.tensor_scalar(A0[:, b, t, :], IOTA, HK[:, 0, bass.ds(8 * i + (4 * b + t), 1)],
                                              HK[:, 2, bass.ds(8 * i + (4 * b + t), 1)], ALU.is_equal, ALU.mult)
                    v.tensor_tensor(B0[:, b], rep(IOTA, 4), bc(HK[:, 1, bass.ds(8 * i + 4 * b, 4)], P),
                                    ALU.is_equal).then_inc(ev["onehots"], 1)
            two_dve(dve, o, v, "peer", EB)
            stage2_dve(dve, o, v, half, freed, turn_out, scale_rows, add_pair)
        def mlstm_pe(pe, mm):
            pe.wait_ge(*nth("m_diag", 1))
            pe.wait_ge(ev["fox_out"], FH)
            for c in range(NT):
                ins = mm(PQ[:, c, :], ONES, flat(DGM[:, c]), start=True, stop=True)
            ins.then_inc(ev["r_mm"], 1)
            pe.wait_ge(*nth("qk_silu", 1))
            for c in range(NT):
                for h in range(MH):
                    ins = mm(PP[:, c, 0, h * P:(h + 1) * P], MQC[:, h, c * P:(c + 1) * P],
                             MQC[:, MH + h, c * P:(c + 1) * P], start=True, stop=True)
                ins.then_inc(ev["qk_mm"], 1)
            for h in range(MH):
                ins = nc.tensor.transpose(PQ[:, 2, h * P:(h + 1) * P], MQC[:, MH + h, 0:P], ID)
            ins.then_inc(ev["k_turned"], 1)
            pe.wait_ge(*nth("r_read", 2))
            for c in range(NT):
                pe.wait_ge(*nth("sm_ready", c + 1))
                for h in range(MH):
                    ins = nc.tensor.transpose(PQ[:, c, h * P:(h + 1) * P], SMM[:, c, h, :], ID)
                ins.then_inc(ev["sm_turned"], 1)
            pe.wait_ge(*nth("ka_ready", 1))
            pe.wait_ge(*nth("smt_out", 2))
            for h in range(MH):
                mm(PQ[:, h, 0:MV + 1], KA[:, h, :], MV1[:, 0, h, :], start=True, stop=True).then_inc(ev["cp_mm"], 1)
            for h in range(MH):
                mm(PP[:, h // 2, h % 2, 0:MV + 1], SMT[:, 0, h, :], MV1[:, 0, h, :], start=True,
                   stop=True).then_inc(ev["num0_mm"], 1)
            for h in range(MH):
                pe.wait_ge(*nth("cp_out", h + 1))
                mm(PQ[:, h, 0:MV + 1], MQC[:, h, P:2 * P], CP[:, h, :], start=True, stop=True).then_inc(ev["inter_mm"], 1)
            for h in range(MH):
                pe.wait_ge(*nth("num0_out", h + 1))
                mm(PP[:, h // 2, h % 2, 0:MV + 1], SMT[:, 1, h, :], MV1[:, 1, h, :], start=True,
                   stop=True).then_inc(ev["num1_mm"], 1)
            pe.wait_ge(*nth("inter_out", MH))
            pe.wait_ge(*nth("mix_ready", 2))

        def second(pe, mm, name, buf, full, d):
            for nb in range(4):
                pe.wait_ge(ev["dve_free"], d + nb)
                pe.wait_ge(slot_full[nb], full)
                for t in range(NT):
                    for k in range(4):
                        ins = mm(PP[:, (UNIT0[name] + nb) % 2, t, :], buf[:, k * T + t * P:k * T + (t + 1) * P],
                                 ring[nb][:, k, :], start=(k == 0), stop=(k == 3))
                ins.then_inc(used, 1)

        def two_pe(pe, mm, name, blocks):
            base, acted, ready = SLOT0[name], ev[name + "_acted"], ev[name + "_ready"]
            buf = [ACTB[:, 0:1024], ACTB[:, 1024:2048]]

            def first(full):
                for s in range(4):
                    pe.wait_ge(slot_full[s], full)
                    for k in range(4):
                        kt = 4 * s + k
                        for n in range(4):
                            ins = mm(PQ[:, n // 2, (n % 2) * T:(n % 2 + 1) * T], ring[s][:, k, n * P:(n + 1) * P],
                                     XT[:, kt, :], start=(kt == 0 and n % 2 == 0), stop=(kt == KT - 1),
                                     skip_group_check=True)
                    ins.then_inc(used, 1)

            if name == "peer":
                pe.wait_ge(ev["bank_empty"], T // 4 + 2)
            pe.wait_ge(ev["act_free"], ACT0[name])
            pe.wait_ge(ev["dve_free"], DVE0[name])
            first(4 * base + 16)
            with pe.Fori(0, blocks // 2 - 1, 1) as i:
                for par in range(2):
                    pe.wait_ge(acted, 2 * i + (par + 1))
                    first(64 * i + (4 * base + 32 + 32 * par))
                    pe.wait_ge(ready, 2 * i + (par + 1))
                    second(pe, mm, name, buf[par], 64 * i + (4 * base + 48 + 32 * par), 8 * i + (DVE0[name] - 1 + 4 * par))
            pe.wait_ge(acted, blocks - 1)
            first(4 * base + 32 * (blocks - 1))
            for b in (blocks - 2, blocks - 1):
                pe.wait_ge(ready, b + 1)
                full = 4 * base + 48 + 32 * b - (16 if b == blocks - 1 else 0)
                second(pe, mm, name, buf[b % 2], full, DVE0[name] - 1 + 4 * b)

        def inverse_pe(pe, mm, c, Ti, Tt):
            if c == 0:
                for _ in range(2):
                    pe.nop().then_inc(ev["inv_m1"], 1)
                    pe.nop().then_inc(ev["inv_t"], 1)
            with pe.Fori(1, 7, 1) as l:
                def first(q):
                    g = 4 * l + (24 * c - 4 + q)
                    pe.wait_ge(ev["inv_off"], g + 1)
                    pe.wait_ge(ev["inv_new"], 4 * l + (28 * c - 4 + q + 1))
                    pe.wait_ge(ev["inv_m1_out"], g + 1)
                    for m in range(4):
                        ins = mm(PQ[:, q % 2, m * P:(m + 1) * P], AOFB[:, q % 2, m, :], Ti[:, 4 * q + m, :], start=True, stop=True)
                    ins.then_inc(ev["inv_m1"], 1)

                def then(q):
                    pe.wait_ge(ev["inv_m1_out"], 4 * l + (24 * c - 4 + q) + 3)
                    pe.wait_ge(ev["inv_new"], 4 * l + (28 * c - 4 + q + 3))
                    for m in range(4):
                        mm(PQ[:, 2 + q % 2, m * P:(m + 1) * P], Tt[:, 4 * q + m, :], M1B[:, q % 2, m, :], start=True, stop=True)
                    for m in range(4):
                        ins = mm(PP[:, q % 2, 0, m * P:(m + 1) * P], M1B[:, q % 2, m, :], Tt[:, 4 * q + m, :], start=True, stop=True)
                    ins.then_inc(ev["inv_t"], 1)
                first(0)
                first(1)
                then(0)
                first(2)
                then(1)
                first(3)
                then(2)
                then(3)

        def stage2_pe(pe, mm, product, turn):
            pe.wait_ge(ev["masks"], 22)
            turn()
            product("dn", 0, 6, True)
            product("dn", 6, 2, False)
            pair = PP[:, UNIT0["small"] % 2]
            pe.wait_ge(ev["dve_free"], DVE0["small"] - 1)
            pe.wait_ge(ev["act_free"], ACT0["small"] - 1)
            for s in range(4):
                w = flat(ring[s][:, :, :])[:, 0:4 * 272].rearrange("p (k n) -> p k n", k=4)
                pe.wait_ge(slot_full[s], 4 * SLOT0["small"] + 16)
                for k in range(4):
                    kt = 4 * s + k
                    for t in range(NT):
                        mm(pair[:, 0, 16 * t:16 * t + 16], XT[:, kt, t * P:(t + 1) * P], w[:, k, 0:16],
                           start=(kt == 0 and t == 0), stop=(kt == KT - 1), skip_group_check=True)
                    for n in range(2):
                        ins = mm(pair[:, 1, n * T:(n + 1) * T], w[:, k, 16 + n * P:16 + (n + 1) * P], XT[:, kt, :],
                                 start=(kt == 0 and n == 0), stop=(kt == KT - 1), skip_group_check=True)
                ins.then_inc(used, 1)
            pe.wait_ge(*nth("dn_sq", 1))
            for n in range(8):
                if n >= 4:
                    pe.wait_ge(*nth("l2_root", n - 3))
                mm(PQ[:, n % 4, :], ONES, flat(SQD)[:, BLK * n:BLK * (n + 1)], start=True, stop=True).then_inc(ev["l2_mm"], 1)
            pe.wait_ge(*nth("g_ready", 1))
            pe.wait_ge(*nth("l2_root", 8))
            g16 = DST[:, 3].rearrange("p t h -> p (t h)")
            mm(PQ[:, 0, 0:16], UI, g16, start=True, stop=True)
            mm(PQ[:, 0, 16:32], ONES, g16, start=True, stop=True).then_inc(ev["gc_mm"], 1)
            pe.wait_ge(*nth("dn_diag", 1))
            for n in range(4):
                mm(PQ[:, n, :], ONES, flat(DGD)[:, BLK * n:BLK * (n + 1)], start=True, stop=True).then_inc(ev["dec_mm"], 1)
            pe.wait_ge(*nth("dn_qk", 1))
            pe.wait_ge(ev["dve_free"], DVE0["rw"])
            pe.wait_ge(ev["act_free"], ACT0["rw"])
            for dst, q0, e in ((None, 8, "kk_gram"), (PQ, 0, "qk_gram")):
                if dst is PQ:
                    pe.wait_ge(*nth("dec_arg", 1))
                for n in range(4):
                    for i in range(4):
                        m = 4 * n + i
                        t, h = m // 8, m % 8
                        ps = PP[:, n // 2, n % 2, i * P:(i + 1) * P] if dst is None else PQ[:, n, i * P:(i + 1) * P]
                        ins = mm(ps, QKV[:, q0 + h, t * P:(t + 1) * P], QKV[:, 8 + h, t * P:(t + 1) * P], start=True, stop=True)
                    ins.then_inc(ev[e], 1)
            pe.wait_ge(*nth("a_ready", 1))
            for n in range(4):
                pe.wait_ge(*nth("qd_ready", n + 1))
                for i in range(4):
                    ins = nc.tensor.transpose(PP[:, n // 2, n % 2, i * P:(i + 1) * P], TTI[:, 4 * n + i, :], ID)
                ins.then_inc(ev["qd_turned"], 1)
            for n in range(4):
                for i in range(4):
                    ins = nc.tensor.transpose(PQ[:, n, i * P:(i + 1) * P], AM[:, 4 * n + i, :], ID)
                ins.then_inc(ev["a_turned"], 1)
            pe.wait_ge(*nth("dn_silu", 6))
            for n in range(4):
                pe.wait_ge(*nth("atn_out", n + 1))
                for i in range(4):
                    m = 4 * n + i
                    t, h = m // 8, m % 8
                    ins = nc.tensor.transpose(PP[:, n // 2, n % 2, i * P:(i + 1) * P], QKV[:, 16 + h, t * P:(t + 1) * P], ID)
                ins.then_inc(ev["v_turned"], 1)
            pe.wait_ge(*nth("at_out", 4))
            for h in range(DH):
                ins = nc.tensor.transpose(PQ[:, h // 4, (h % 4) * P:(h % 4 + 1) * P], QKV[:, 8 + h, 0:P], ID)
            ins.then_inc(ev["kd_turned"], 1)
            pe.wait_ge(*nth("kd_ready", 1))
            pe.wait_ge(*nth("v_tok", 4))
            inverse_pe(pe, mm, 0, TI, TTI)
            at = lambda b, h: PQ[:, b + h // 4, (h % 4) * P:(h % 4 + 1) * P]
            pe.wait_ge(ev["inv_new"], 28)
            for t in range(NT):
                if t == 1:
                    pe.wait_ge(ev["s_out"], 1)
                    for h in range(DH):
                        ins = mm(at(2, h), QKV[:, 8 + h, P:T], SD[:, h, :], start=True, stop=True)
                    ins.then_inc(ev["ks_mm"], 1)
                    for h in range(DH):
                        ins = mm(PP[:, 0, h // 4, (h % 4) * P:(h % 4 + 1) * P], QKV[:, h, P:T], SD[:, h, :], start=True, stop=True)
                    ins.then_inc(ev["qs_mm"], 1)
                pe.wait_ge(ev["dn_rhs"], t + 1)
                for h in range(DH):
                    ins = mm(at(0, h), TTI[:, DH * t + h, :], RH[:, h, :], start=True, stop=True)
                ins.then_inc(ev["vn_mm"], 1)
                pe.wait_ge(ev["vn_out"], t + 1)
                for h in range(DH):
                    ins = mm(at(2, h), ATN[:, DH * t + h, :], VN[:, h, :], start=True, stop=True)
                ins.then_inc(ev["o_mm"], 1)
                if t == 0:
                    for h in range(DH):
                        ins = mm(at(0, h), KD[:, h, :], VN[:, h, :], start=True, stop=True)
                    ins.then_inc(ev["s_mm"], 1)
                    pe.wait_ge(ev["o_out"], 1)
            turn(8, OD)
            for hf in range(2):
                rw_pe(pe, mm, product, hf)
            product("out2", 0, 4, False, YT)
            turn()
            product("xk", 0, 1, True, MEMT)
            product("xv", 0, 1, False, MEMT)
            turn()
            product("xq", 0, 1, True)
            pe.wait_ge(ev["dve_free"], DVE0["xo"])
            pe.wait_ge(ev["act_free"], ACT0["xo"])
            for n in range(8):
                h, t = n // 2, n % 2
                ins = mm(PQ[:, h, t * T:(t + 1) * T], XQ[:, h, t * P:(t + 1) * P], XK[:, h, :], start=True, stop=True)
            ins.then_inc(ev["xa_mm"], 1)
            pe.wait_ge(*nth("xa_p", 1))
            for h in range(4):
                for m in range(NT):
                    for t in range(NT):
                        ins = nc.tensor.transpose(PP[:, h // 2, h % 2, m * T + t * P:m * T + (t + 1) * P], XP[:, h, t, m * P:(m + 1) * P], ID)
                ins.then_inc(ev["xa_turned"], 1)
            for h in range(4):
                pe.wait_ge(*nth("xa_pt", h + 1))
                for m in range(NT):
                    ins = mm(PQ[:, h, 0:T], XV[:, m, h * P:(h + 1) * P], XPT[:, h, m, :], start=(m == 0), stop=(m == 1))
                ins.then_inc(ev["xa_o"], 1)
            pe.wait_ge(*nth("xo_ready", 1))
            second(pe, mm, "xo", XO, 4 * SLOT0["xo"] + 16, DVE0["xo"] - 1)
            turn()
            two_pe(pe, mm, "ffn", FB)

        def rw_pe(pe, mm, product, hf):
            if hf == 0:
                product("rw", 0, 3, True)
            else:
                pe.wait_ge(ev["rw_done"], 1)
                product("rw", 3, 3, True)
            if hf == 0:
                pe.wait_ge(ev["lw_act"], 1)
                pe.wait_ge(ev["lw_shift"], 1)
                pe.wait_ge(ev["lora_in"], 48)
                pe.wait_ge(ev["lora_zero"], 1)
            for n, (w, x) in enumerate(((W2, LW), (A2, LW), (G2, LG))):
                if n == 2:
                    pe.wait_ge(ev["lora_out"], 3 * hf + 1)
                for j in range(J):
                    c = J * hf + j
                    ins = mm(PQ[:, 2 * (n % 2) + j // 2, (j % 2) * T:(j % 2 + 1) * T], w[:, c * P:(c + 1) * P], x[:, 0:T],
                             start=True, stop=True)
                ins.then_inc(ev["lora_mm"], 1)
            for e, done in (("kk_sq", "kk_mm"), ("rk_ready", "bonus_mm")):
                pe.wait_ge(ev[e], hf + 1)
                for n in range(2):
                    ins = mm(PQ[:, 2 + n, :], BD[6], flat(E1)[:, BLK * n:BLK * (n + 1)], start=True, stop=True)
                ins.then_inc(ev[done], 1)
            pe.wait_ge(ev["dve_free"], DVE0["rw"] + 3 * (hf + 1))
            pe.wait_ge(ev["act_free"], ACT0["rw"] + 3 * (hf + 1))
            for t in range(NT):
                for j in range(J):
                    ins = nc.tensor.transpose(PP[:, t, 0, j * P:(j + 1) * P], RKV[:, 2, j, t * P:(t + 1) * P], ID)
                ins.then_inc(ev["rv_turned"], 1)
            pe.wait_ge(ev["decayed"], hf + 1)
            for w in range(2):
                for j in range(J):
                    ins = nc.tensor.transpose(PP[:, w, 1, j * P:(j + 1) * P], BKS[:, w, j, :], ID)
                ins.then_inc(ev["bk_turned"], 1)
            pe.wait_ge(ev["rv_tok"], 2 * hf + 2)
            pe.wait_ge(ev["bk_tok"], 2 * hf + 2)
            pe.wait_ge(ev["lora_out"], 3 * hf + 3)
            for m in range(16):
                t, j, e = m // 8, (m % 8) // 2, m % 2
                rows = slice(64 * e, 64 * e + 64)
                if m >= 4:
                    pe.wait_ge(ev["gram_out"], 16 * hf + m - 3)
                for w in range(2):
                    mm(PQ[:, m % 4, w * T:(w + 1) * T], BKD[rows, w, j, t * P:(t + 1) * P],
                       KRD[rows, j, :, t * P:(t + 1) * P], start=True, stop=True)
                    ins = mm(PP[0:64, (m % 4) // 2, m % 2, w * P:(w + 1) * P], BKO[rows, w, j, t, :], KRO[rows, j, :, t, :],
                             start=True, stop=True)
                ins.then_inc(ev["gram_mm"], 1)
            pe.wait_ge(ev["gram_out"], 16 * hf + 16)
            for n in range(4):
                for i in range(4):
                    ins = nc.tensor.transpose(PQ[:, n, i * P:(i + 1) * P], GR[:, 4 * n + i, 0, :], ID)
                ins.then_inc(ev["ram_turned"], 1)
            inverse_pe(pe, mm, 1 + hf, RTI, RTT)
            pe.wait_ge(ev["inv_new"], 28 * (hf + 2))
            for t in range(NT):
                n = 2 * hf + t + 1
                if t == 1:
                    pe.wait_ge(ev["rs_out"], hf + 1)
                    for j in range(J):
                        mm(PQ[:, 0, j * P:(j + 1) * P], KRS[:, 0, j, :], S1[:, j, :], start=(j == 0), stop=False, skip_group_check=True)
                for h in range(HH):
                    c = slice(h * 64, h * 64 + 64)
                    ins = mm(PQ[:, 0, c], GR[:, HH * t + h, 2, :], VTK[:, t, c], start=(t == 0), stop=True, skip_group_check=True)
                ins.then_inc(ev["rx_mm"], 1)
                pe.wait_ge(ev["rx_out"], n)
                for h in range(HH):
                    c = slice(h * 64, h * 64 + 64)
                    ins = mm(PQ[:, 1, c], RTT[:, HH * t + h, :], RX[:, c], start=True, stop=True)
                ins.then_inc(ev["sa_mm"], 1)
                pe.wait_ge(ev["sa_out"], n)
                if t == 1:
                    for j in range(J):
                        mm(PQ[:, 2, j * P:(j + 1) * P], KRS[:, 1, j, :], S1[:, j, :], start=(j == 0), stop=False, skip_group_check=True)
                for h in range(HH):
                    c = slice(h * 64, h * 64 + 64)
                    mm(PQ[:, 2, c], GR[:, HH * t + h, 1, :], SAB[:, c], start=(t == 0), stop=False, skip_group_check=True)
                    ins = mm(PQ[:, 2, c], GR[:, HH * t + h, 3, :], VTK[:, t, c], start=False, stop=True, skip_group_check=True)
                ins.then_inc(ev["ry_mm"], 1)
                if t == 0:
                    for j in range(J):
                        c = slice(j * P, (j + 1) * P)
                        mm(PQ[:, 3, c], BKT[:, 0, c], SAB[:, c], start=True, stop=False)
                        ins = mm(PQ[:, 3, c], BKT[:, 1, c], VTK[:, 0, c], start=False, stop=True)
                    ins.then_inc(ev["rs_mm"], 1)
                    pe.wait_ge(ev["ry_out"], n)
            pe.wait_ge(ev["gn_out"], hf + 1)
            for t in range(NT):
                for j in range(J):
                    ins = nc.tensor.transpose(PP[:, t, 0, j * P:(j + 1) * P], RY[:, t, j * P:(j + 1) * P], ID)
                ins.then_inc(ev["ry_turned"], 1)
            pe.wait_ge(ev["rw_done"], hf + 1)


        @block.tensor
        def _(pe):
            o = Own(pe, ev["pe_order"])
            mm = nc.tensor.matmul

            def group(name, j, pair, feat, act):
                for s in range(4):
                    pe.wait_ge(slot_full[s], 4 * (SLOT0[name] + 4 * j) + 16)
                    for k in range(4):
                        kt = 4 * s + k
                        if feat:
                            for n in range(4):
                                ins = mm(pair[:, n // 2, (n % 2) * T:(n % 2 + 1) * T], ring[s][:, k, n * P:(n + 1) * P],
                                         act[:, kt, :], start=(kt == 0 and n % 2 == 0), stop=(kt == KT - 1),
                                         skip_group_check=True)
                        else:
                            for t in range(NT):
                                ins = mm(pair[:, t, :], act[:, kt, t * P:(t + 1) * P], ring[s][:, k, :],
                                         start=(kt == 0), stop=(kt == KT - 1))
                    ins.then_inc(used, 1)

            def product(name, first, n, feat, act=XT):
                d, ac = [(x[2], x[3]) for x in UNITS if x[0] == name][0]

                def one(j, par):
                    pe.wait_ge(ev["dve_free"], j * d + (DVE0[name] - d))
                    if ac:
                        pe.wait_ge(ev["act_free"], j * ac + (ACT0[name] - ac))
                    group(name, j, PP[:, (UNIT0[name] + par) % 2], feat, act)

                if first == 0:
                    pe.wait_ge(ev["dve_free"], DVE0[name])
                    pe.wait_ge(ev["act_free"], ACT0[name])
                if n % 2 or n == 2:
                    for j in range(first, first + n):
                        one(j, j)
                else:
                    with pe.Fori(0, n // 2, 1) as i:
                        for par in range(2):
                            one(2 * i + (first + par), first + par)

            def turn(tiles=16, src=SCR):
                for t in range(NT):
                    pe.wait_ge(ev["tp_scaled"], turn.rows + 1)
                    turn.rows += 1
                    for g in range(tiles // 4):
                        if t == 1:
                            pe.wait_ge(ev["turn_out"], turn.n - tiles // 4 + 1)
                        for n in range(4):
                            kt = 4 * g + n
                            ins = nc.tensor.transpose(PQ[:, g, n * P:(n + 1) * P], src[:, t, kt * P:(kt + 1) * P], ID)
                        ins.then_inc(ev["turned"], 1)
                        turn.n += 1
                pe.wait_ge(ev["turn_out"], turn.n)
            turn.n = turn.rows = 0

            pe.wait_ge(ev["masks"], 3)
            turn()
            pe.wait_ge(ev["consts1"], 48)
            for t in range(NT):
                for kt in range(KT):
                    ins = mm(PQ[:, 0, 16 * t:16 * t + 16], XT[:, kt, t * P:(t + 1) * P], WG[:, kt, :],
                             start=(kt == 0), stop=(kt == KT - 1))
            ins.then_inc(ev["gate_mm"], 1)
            product("win", 0, 2, True)
            pe.wait_ge(*nth("log_f", 1))
            for n, (w, t) in enumerate(((UI, 0), (UI, 1), (ONES, 0), (ONES, 1))):
                ins = mm(PQ[:, 1, 16 * n:16 * n + 16], w, LF[:, t, :], start=True, stop=True)
            ins.then_inc(ev["cumsum_mm"], 1)
            product("win", 2, 4, True)
            product("win", 6, 6, False)
            pe.wait_ge(*nth("fox_diag", 1))
            pe.wait_ge(ev["act_free"], 2 + 12)
            pe.wait_ge(ev["dve_free"], 2 + 12)
            for h in range(FH + 1):
                if h < FH:
                    b = h % 2
                    if h >= 2:
                        pe.wait_ge(ev["fox_max"], h - 1)
                    for t in range(NT):
                        dst = PQ[:, b, 0:P] if t == 0 else PQ[:, b, P:384]
                        mm(dst, FQ[:, h, t * P:(t + 1) * P], FK[:, h, 0:P * (t + 1)], start=True, stop=False)
                        ins = mm(dst, ONES, flat(DG[:, h, 0:t + 1, :]), start=False, stop=True)
                    ins.then_inc(ev["fox_scores"], 1)
                if h >= 1:
                    g, b = h - 1, (h - 1) % 2
                    pe.wait_ge(ev["fox_exp"], g + 1)
                    if g >= 2:
                        pe.wait_ge(ev["fox_pt"], g - 1)
                    for n in range(3):
                        ins = nc.tensor.transpose(PQ[:, 2 + b, n * P:(n + 1) * P], FP[:, b, n * P:(n + 1) * P], ID)
                    ins.then_inc(ev["fox_turned"], 1)
                    pe.wait_ge(ev["fox_pt"], g + 1)
                    if g >= 2:
                        pe.wait_ge(ev["fox_out"], g - 1)
                    mm(PP[:, b, 0, 0:P], FPT[:, b, 0:P], FV[:, 0, g * P:(g + 1) * P], start=True, stop=True)
                    mm(PP[:, b, 0, P:2 * P], FPT[:, b, P:2 * P], FV[:, 0, g * P:(g + 1) * P], start=True, stop=False)
                    mm(PP[:, b, 0, P:2 * P], FPT[:, b, 2 * P:384], FV[:, 1, g * P:(g + 1) * P], start=False,
                       stop=True).then_inc(ev["fox_pv"], 1)
            mlstm_pe(pe, mm)
            turn()
            product("wout", 0, 4, False)
            turn()
            product("wq", 0, 4, True)
            pe.wait_ge(ev["keys_in"], 16)
            pe.wait_ge(ev["act_free"], ACT0["peer"])
            pe.wait_ge(ev["dve_free"], DVE0["peer"])
            for n in range(8):
                t, g = n // 4, n % 4
                if t == 1:
                    pe.wait_ge(*nth("scores_out", n - 3))
                for m in range(4):
                    hq = 4 * g + m
                    ins = mm(PQ[:, g, m * P:(m + 1) * P], PQT[:, hq, t * P:(t + 1) * P], KEYS[:, hq % 2, :],
                             start=True, stop=True)
                ins.then_inc(ev["scores_mm"], 1)
            pe.wait_ge(*nth("scores_out", 8))
            pe.wait_ge(*nth("sel_ready", 4))
            pe.wait_ge(*nth("gate_ready", 1))
            for q in range(2):
                for t in range(NT):
                    nc.tensor.transpose(PQ[:, 0, q * T + t * P:q * T + (t + 1) * P], SEL[:, q, t, :], ID)
            for t in range(NT):
                ins = nc.tensor.transpose(PQ[:, 1, t * P:(t + 1) * P], GA[:, t, :], ID)
            ins.then_inc(ev["hk_turned"], 1)
            pe.wait_ge(*nth("hk_ready", 1))
            for _ in range(2):
                pe.nop().then_inc(ev["rows_used"], 1)
            with pe.Fori(0, T // 8, 1) as i:
                for b in range(2):
                    pe.wait_ge(ev["onehots"], 2 * i + b + 1)
                    pe.wait_ge(ev["bank_empty"], 2 * i + b + 1)
                    for t in range(4):
                        ins = mm(PQ[:, b, t * P:(t + 1) * P], A0[:, b, t, :], B0[:, b, t, :], start=True, stop=True)
                    ins.then_inc(ev["rows_used"], 1)
            two_pe(pe, mm, "peer", EB)
            stage2_pe(pe, mm, product, turn)
def rows_of(w):
    k, n = w.shape
    return w.reshape(k // BLK, 4, P, n // BLK, BLK).transpose(3, 0, 2, 1, 4).reshape(-1, P, 4 * BLK)


def second_of(w):
    k, n = w.shape
    return w.reshape(k // BLK, 4, P, n // BLK, BLK).transpose(0, 3, 2, 1, 4).reshape(-1, P, 4 * BLK)


def columns(vec):
    return np.asarray(vec).reshape(-1, P).T


def layout(i):
    f, mq = 1024, 512
    w = i["w_in"][0]
    cut = {}
    at = 0
    for name, n in (("fq", f), ("fk", f), ("fv", f), ("ff", 8), ("mq", mq), ("mk", mq), ("mv", f), ("mi", 4), ("mf", 4), ("mo", f)):
        cut[name] = w[:, at:at + n]
        at += n
    arrays = {
        "x": i["x"][0],
        "win": rows_of(np.concatenate([cut[n] for n in ("mq", "mk", "fq", "fk", "fv", "mv", "mo")], 1)),
        "w_gates": np.concatenate([cut[n] for n in ("ff", "mi", "mf")], 1).reshape(KT, P, 16).transpose(1, 0, 2).reshape(P, -1),
        "wout": rows_of(i["w_out"][0]),
        "wq": rows_of(i["peer_w_q"][0]),
        "keys": i["peer_keys"][0].transpose(2, 0, 1).reshape(P, -1),
        "pu": i["peer_u"][0].reshape(P, EB, 4, 4, 4, P).transpose(1, 3, 5, 4, 2, 0).reshape(-1, P, 2048),
        "pv": i["peer_v"][0].reshape(P, EB, 4, 4, BLK).transpose(1, 3, 0, 2, 4).reshape(-1, P, 2048),
        "cols1": np.concatenate([
            columns(i["norm1_w"][0]), columns(i["fox_out_norm_w"][0]), columns(i["mlstm_out_norm_w"][0]),
            columns(i["norm2_w"][0]), i["mlstm_conv_w"][0].reshape(4, 8, P).transpose(2, 1, 0).reshape(P, -1),
            columns(i["mlstm_conv_b"][0])], 1),
        "rows": np.concatenate([i["fox_f_bias"][0], i["mlstm_i_bias"][0], i["mlstm_f_bias"][0],
                                i["dn_a_log_2"][0], i["dn_dt_bias_2"][0]]),
    }
    w = i["w_in_2"][0]
    f = 1024
    dn, rw = w[:, 0:4 * f + 16], w[:, 4 * f + 16:]
    small = np.concatenate([dn[:, 4 * f:], rw[:, 3 * f:]], 1)
    mu = i["rw_mu_2"][0]
    arrays.update({
        "dn": rows_of(dn[:, 0:4 * f]),
        "small": small.reshape(4, 4, P, 272).transpose(0, 2, 1, 3).reshape(4, P, 4 * 272),
        "rw": rows_of(np.concatenate([rw[:, f * n + BLK * h:f * n + BLK * (h + 1)] for h in range(2) for n in range(3)], 1)),
        "w2": i["rw_w2_2"][0], "a2": i["rw_a2_2"][0], "g2": i["rw_g2_2"][0],
        "out2": rows_of(i["w_out_2"][0]),
        "mem": i["mem_2"][0],
        "xk": rows_of(i["xa_wk_2"][0]), "xv": rows_of(i["xa_wv_2"][0]), "xq": rows_of(i["xa_wq_2"][0]),
        "xo": second_of(i["xa_wo_2"][0]),
        "f1": rows_of(i["ffn_w1_2"][0]), "f2": second_of(i["ffn_w2_2"][0]),
        "fnw1": i["final_norm_w"], "fnw": i["final_norm_w_2"],
        "cols2": np.concatenate([
            columns(i["mix_norm_w_2"][0]), columns(i["xa_norm_w_2"][0]), columns(i["mem_norm_w_2"][0]),
            columns(i["ffn_norm_w_2"][0]), i["dn_conv_w_2"][0].reshape(4, 24, P).transpose(2, 1, 0).reshape(P, -1),
            columns(i["dn_norm_w_2"][0]), columns(mu), columns(i["rw_w0_2"][0]), columns(i["rw_a0_2"][0]),
            columns(i["rw_k_k_2"][0]), columns(i["rw_k_a_2"][0]), columns(i["rw_r_k_2"][0]),
            columns(i["rw_ln_w_2"][0]), columns(i["rw_ln_b_2"][0])], 1),
    })
    return {k: np.ascontiguousarray(v) for k, v in arrays.items()}


def kernel(**inputs):
    import concourse.bacc as bacc
    from concourse.bass_utils import run_bass_kernel_spmd

    arrays = layout({k: np.asarray(v) for k, v in inputs.items()})
    nc = bacc.Bacc("TRN2", target_bir_lowering=False, num_devices=1)
    handles = {k: nc.dram_tensor(k, v.shape, mybir.dt.from_np(v.dtype), kind="ExternalInput").ap()
               for k, v in arrays.items()}
    out = nc.dram_tensor("out", (T, D), F32, kind="ExternalOutput").ap()
    build(nc, handles, out)
    r = run_bass_kernel_spmd(nc, [arrays], core_ids=[0])
    return r.results[0]["out"].reshape(1, T, D)
```

```python
from contextlib import ExitStack

import numpy as np
import concourse.bass as bass
from concourse import mybir

F32 = mybir.dt.float32
F22 = mybir.dt.float32r
U32 = mybir.dt.uint32
I32 = mybir.dt.int32
ALU = mybir.AluOpType
ACT = mybir.ActivationFunctionType
AX = mybir.AxisListType

P = 128
T = 256
NT = T // P
D = 2048
KT = D // P
BLK = 512
EPS = 1e-6
NEG = -1e30
FH, MH, MV = 8, 4, 256
PH, NK, TOPK = 8, 128, 16
EB = NK // 4
FB = 4 * D // BLK
DH = 8
QK_SCALE = float(P) ** -0.5
RW_EPS = 64e-5
DECAY = float(np.exp(-0.5))

STREAM = [("win", 12), ("wout", 4), ("wq", 4), ("peer", 2 * EB), ("dn", 8), ("small", 1), ("rw", 6),
          ("out2", 4), ("xk", 1), ("xv", 1), ("xq", 1), ("xo", 1), ("ffn", 2 * FB)]
SLOT0, _n = {}, 0
for _name, _groups in STREAM:
    SLOT0[_name] = _n
    _n += 4 * _groups
UNITS = [("win", 12, 1, 1), ("wout", 4, 1, 0), ("wq", 4, 1, 1), ("peer", 4 * EB, 1, 0), ("dn", 8, 1, 1),
         ("small", 1, 1, 1), ("rw", 6, 1, 1), ("out2", 4, 1, 0), ("xk", 1, 1, 1), ("xv", 1, 1, 1),
         ("xq", 1, 1, 1), ("xo", 4, 1, 0), ("ffn", 4 * FB, 1, 0)]
UNIT0, DVE0, ACT0 = {}, {}, {}
_u, _d, _a = 0, 2, 2
for _name, _units, _dv, _ac in UNITS:
    UNIT0[_name], DVE0[_name], ACT0[_name] = _u, _d, _a
    _u, _d, _a = _u + _units, _d + _units * _dv, _a + _units * _ac

COLS1 = [("norm1", 16), ("mix", 16), ("norm2", 16), ("cw", 32), ("cb", 8)]
COLS2 = [("mix2", 16), ("xa", 16), ("mem", 16), ("ffn", 16), ("dcw", 96), ("dnw", 1), ("mur", 8), ("muk", 8),
         ("muv", 8), ("muw", 1), ("mug", 1), ("w0", 8), ("a0", 8), ("kk", 8), ("ka", 8), ("rk", 8),
         ("lnw", 8), ("lnb", 8)]


STEPS = {
    "scalar_steps": [("gate_ln", 1), ("qk_silu", 1), ("mo_gate", 1), ("m_exp", 1), ("smt_out", 2), ("cp_out", 4),
                     ("inter_out", 4), ("mix_sq", 1), ("mix_root", 1), ("scores_out", 8), ("gate_exp", 1),
                     ("dn_silu", 6), ("z_silu", 1), ("dn_sq", 1), ("l2_root", 1), ("g_act", 1), ("gc_exp", 1),
                     ("dec_out", 1), ("atn_out", 4), ("at_out", 4), ("v_tok", 4), ("qs_out", 8), ("od_sq", 1),
                     ("od_root", 1), ("xa_exp", 1), ("xa_pt", 4), ("xo_high", 1)],
    "tensor_steps": [("gate_mm", 1), ("cumsum_mm", 1), ("r_mm", 1), ("qk_mm", 2), ("k_turned", 1), ("sm_turned", 2),
                     ("cp_mm", 4), ("num0_mm", 4), ("inter_mm", 4), ("num1_mm", 4), ("scores_mm", 8), ("hk_turned", 1),
                     ("l2_mm", 3), ("gc_mm", 1), ("dec_mm", 4), ("kk_gram", 4), ("qk_gram", 4), ("qd_turned", 4),
                     ("a_turned", 4), ("v_turned", 4), ("kd_turned", 1), ("xa_mm", 1), ("xa_turned", 4), ("xa_o", 4)],
    "vector_steps": [("gate_abs", 1), ("log_f", 1), ("fox_diag", 1), ("conv_out", 1), ("mo_ready", 1), ("m_diag", 1),
                     ("r_read", 2), ("m_arg", 1), ("sm_ready", 2), ("ka_ready", 1), ("num0_out", 4), ("mix_ready", 2),
                     ("mix_sum", 1), ("gate_arg", 1), ("sel_ready", 4), ("gate_ready", 1), ("hk_ready", 1),
                     ("cin_pad", 1), ("dn_conv", 6), ("g_abs", 1), ("l2_inv", 1), ("dn_qk", 1), ("g_ready", 1), ("gc_out", 1),
                     ("dn_diag", 1), ("dec_arg", 1), ("a_ready", 1), ("qd_ready", 4), ("kd_ready", 1), ("xa_max", 1),
                     ("xa_p", 1)],
}
STEP = {}
for _sem, _list in STEPS.items():
    _n = 0
    for _name, _times in _list:
        STEP[_name] = (_sem, _n)
        _n += _times


def offsets(table):
    out, at = {}, 0
    for name, n in table:
        out[name] = at
        at += n
    return out, at


C1, NC1 = offsets(COLS1)
C2, NC2 = offsets(COLS2)


class Own:

    def __init__(self, eng, order):
        self.eng, self.order, self.n = eng, order, {}

    def tell(self, ins, sem):
        self.n[id(sem)] = self.n.get(id(sem), 0) + 1
        ins.then_inc(sem, 1)

    def done(self, ins, sem=None):
        sem = self.order if sem is None else sem
        self.tell(ins, sem)
        self.eng.wait_ge(sem, self.n[id(sem)])


def build(nc, a, out):
    ctx = ExitStack()
    with ctx:
        base = nc.sbuf_base + (-nc.sbuf_base) % 32
        ctx.enter_context(nc.sbuf_tensor("all", [P, 53184 + 8], F32))

        def sb(name, off, cols, dt=F32):
            return nc.alloc_sbuf_tensor_at(name, [P, cols], dt, offset=base + 4 * off)

        def half_words(name, off, cols, *dims):
            parts = []
            for k, part in enumerate(("high", "low")):
                parts.append(sb(f"{name}_{part}", off + k * cols, cols, F22))
            return parts

        X_ = sb("x_res", 0, NT * D)
        ring = [sb(f"ring{i}", 4096 + 2048 * i, 4 * BLK)[:, :].rearrange("p (k n) -> p k n", k=4) for i in range(4)]
        CT = sb("constants", 12288, 3912)
        AR0 = 16200
        AR = sb("arena", AR0, 36984)
        ID, ONES, IOTA, SM = CT[:, 0:128], CT[:, 128:256], CT[:, 256:384], CT[:, 384:704]
        XTH_, XTL_ = half_words("x_t", AR0, KT * T)
        WH = [sb(f"w_high{i}", AR0 + 8192 + 2048 * i, 2048, F22) for i in range(2)]
        WL = [sb(f"w_low{i}", AR0 + 12288 + 2048 * i, 2048, F22) for i in range(2)]
        WGH, WGL = half_words("w_gates", AR0 + 31008, 256)
        AH = [sb(f"act_high{i}", AR0 + 28672 + 2048 * i, 1024, F22) for i in range(2)]
        AL = [sb(f"act_low{i}", AR0 + 29696 + 2048 * i, 1024, F22) for i in range(2)]
        PP = ctx.enter_context(nc.psum_tensor("pairs", [P, 2, 2, BLK], F32))
        PQ = ctx.enter_context(nc.psum_tensor("quad", [P, 4, BLK], F32))
        g_dram = nc.dram_tensor("gates_spilled", [4, P, P * 64], F32, kind="Internal").ap()

        X = X_[:, :].rearrange("p (t d) -> p t d", t=NT)
        XTH, XTL = (x[:, :].rearrange("p (k t) -> p k t", k=KT) for x in (XTH_, XTL_))

        class Signals(dict):

            def __missing__(self, name):
                if name in STEP:
                    return self[STEP[name][0]]
                self[name] = ctx.enter_context(nc.semaphore(name))
                return self[name]

        ev = Signals()

        def nth(name, n):
            return ev[name], STEP[name][1] + n

        used = ev["weights_used"]
        slot_full = [ev[f"slot_full{i}"] for i in range(4)]

        def av(off, *dims):
            n = int(np.prod(dims))
            assert off + n <= 36984
            v = AR[:, off:off + n]
            if len(dims) == 2:
                v = v.rearrange("p (a b) -> p a b", a=dims[0])
            if len(dims) == 3:
                v = v.rearrange("p (a b c) -> p a b c", a=dims[0], b=dims[1])
            if len(dims) == 4:
                v = v.rearrange("p (a b c d) -> p a b c d", a=dims[0], b=dims[1], c=dims[2])
            return v

        def bc(ap, n):
            return ap.unsqueeze(len(ap.shape)).broadcast_to([*ap.shape, n])

        def rep(ap, n):
            return ap.unsqueeze(1).broadcast_to([ap.shape[0], n, *ap.shape[1:]])

        def cv(off, *dims):
            v = CT[:, off:off + int(np.prod(dims))]
            return v.rearrange("p (a b) -> p a b", a=dims[0]) if len(dims) == 2 else v

        MB = 704
        UI = cv(MB, 128)
        LS = cv(MB + 128, 128)
        TRI = cv(MB + 256, 256)
        COL1 = cv(MB + 512, NC1)
        COL2 = cv(MB + 512 + NC1, NC2)
        ROW = cv(MB + 512 + NC1 + NC2, 32)
        at = MB + 544 + NC1 + NC2
        BD = [cv(at + 128 * i, 128) for i in range(7)]
        LV = [cv(at + 896 + 128 * i, 128) for i in range(7)]
        LVA = cv(at + 896, 7, 128)
        M4 = cv(at + 1792, 4, 128)
        assert at + 2304 <= 3912
        EPSC, RWEPSC = SM[:, 0:1], SM[:, 1:2]
        COL16 = SM[:, 160:191]
        SS, RS, RSTD = SM[:, 2:4], SM[:, 4:6], SM[:, 6:8]

        def col1(name, i=0, n=1):
            return COL1[:, C1[name] + i:C1[name] + i + n]

        def col2(name, i=0, n=1):
            return COL2[:, C2[name] + i:C2[name] + i + n]

        SCR = av(8192, NT, D)
        XTS = av(28704, 2, BLK)
        SCN = av(16384, NT, D)
        FQ = av(16384, FH, T)
        FK = av(18432, FH, T)
        FV = av(20480, NT, FH * P)
        MQK = av(22528, 8, T + 3)
        MQC = av(24600, 8, T)
        MV1 = av(26648, NT, MH, MV + 1)
        MO = av(28704, NT, MH * MV)
        MIX = av(0, NT, D)
        WG = av(30752, KT, 16)
        GT = av(31520, NT, 16)
        LF = av(31552, NT, 16)
        CS = av(31584, 4, 16)
        TM = av(31648, 8, 16)
        RC = av(31776, NT, MH)
        KCOL = av(31784, MH)
        MT = av(31788, NT, MH)
        EXB = av(31796, NT, MH)
        EM = av(31804, NT, MH)
        INTER = av(31812, MH)
        RM = av(31816, NT, MH)
        MREC = av(31824, 2, MH)
        FCOL = av(31832, NT, FH)
        NFCOL = av(31848, NT, FH)
        FST = av(31864, 2, 4)
        HN = av(31872, 2, 24)
        DG = av(31928, FH, NT, P)
        FS = av(33976, 2, 384)
        FP = av(34744, 2, 384)
        FPT = av(35512, 2, 384)
        DGM = av(8192, NT, MH, P)
        DM = av(9216, NT, MH, P)
        SMM = av(10240, NT, MH, P)
        SMT = av(11264, NT, MH, P)
        KA = av(12288, MH, P)
        CP = av(12800, MH, MV + 1)
        NUM = av(16384, NT, MH, MV + 1)
        TMP = av(20480, MH, MV + 1)
        PQT = av(16384, 16, T)
        SC = av(20480, NT, 16, NK)
        SW = av(24576, NT, 16, NK)
        CD = av(28672, NT, PH, 256)
        KEYS = av(32768, 2, NK)
        S16 = av(33024, NT, 16, TOPK)
        I16 = av(33536, NT, 16, TOPK)
        SF = av(34048, NT, PH, TOPK)
        PF = av(34304, NT, PH, TOPK)
        PA = av(34560, NT, PH, TOPK)
        PB = av(34816, NT, PH, TOPK)
        SEL = av(35072, 2, NT, P)
        IF = av(35584, NT, 16, TOPK)
        GS = av(36096, 4, NT, PH)
        GA = av(36160, NT, P)
        OH = av(20480, P, TOPK)
        OH2 = av(22528, P, TOPK)
        IO32 = SM[:, 32:160].bitcast(I32)
        CW = av(24576, NT, PH, 256)
        GST = [av(8192, P, 64), av(16384, P, 64)]
        A0 = av(24576, 2, 4, P)
        B0 = av(25600, 2, 4, P)
        HKT = av(26624, 3 * T)
        HK = HKT.rearrange("p (w t) -> p w t", w=3)
        GBK = [av(32768 + 1024 * i, 4, 4, 64) for i in range(2)]
        HID = av(34816, 1024)

        CIN = av(16384, 8, T + 3)
        QKV = av(18456, 24, T)
        ZT = av(24600, NT, DH * P)
        YT = av(8192, KT, T)
        LW = av(32816, T + 1)
        LG = av(33073, T + 1)
        GB = av(33330, NT, 16)
        DST = av(33362, 12, NT, 8)
        VT = av(12288, NT, DH, P)
        KD = av(33554, DH, P)
        DEC = av(14336, NT, DH, P)
        AM = av(0, 16, P)
        AT_ = av(2048, 16, P)
        TI = av(4096, 16, P)
        TTI = av(6144, 16, P)
        DGD = TI
        SQD = av(0, 16, T)
        L2 = av(34578, T)
        ATN = av(16384, 16, P)
        VN = av(2048, DH, P)
        RH = av(14336, DH, P)
        SD = av(15360, DH, P)
        OD = av(0, NT, DH * P)
        OTM = av(4096, DH, P)
        AOFS = [av(14336, 4, 4, P), av(33554, 4, 4, P), av(33554, 4, 4, P)]
        M1B = av(35602, 2, 4, P)

        J, HH = 4, 8
        W2, A2, G2 = av(12288, 1024), av(13312, 1024), av(14336, 1024)
        GATE = av(15360, J, T)
        BON = av(16384, J, T)
        KRS = av(17408, 2, J, P)
        BKS = av(18432, 2, J, P)
        VTK = av(19456, NT, 512)
        BKT = av(20480, 2, J * P)
        RX = av(33554, 512)
        S1 = av(34066, J, P)
        E2 = av(33554, J, T)
        E1 = YT[:, 12:16, :]
        KRD = av(0, J, 2, T)
        BKD = av(2048, 2, J, T)
        KRO = av(4096, J, 2, NT, 64)
        BKO = av(5120, 2, J, NT, 64)
        RAWS = [av(26648 + 3084 * h, 3, J, T + 1) for h in range(2)]
        RKV = av(21504, 3, J, T)
        LDX = av(24576, J, T)
        AA = av(25600, J, T)
        CUM = av(34578, J, T)
        KKN = av(35602, J, T)
        GR = av(21504, 16, 4, P)
        RAM, RTI, RTT = av(0, 16, P), av(2048, 16, P), av(4096, 16, P)
        RY = av(34578, NT, 512)
        RY2 = av(35602, NT, 512)
        SAB = av(6144, 512)
        RST = av(6656, 4, 16)

        MEMX = av(16384, NT, D)
        XK = av(20480, 4, T)
        XV = av(21504, NT, 512)
        XQ = av(22528, 4, T)
        XP = av(23552, 4, NT, T)
        XPT = av(25600, 4, NT, T)
        FNW = av(32768, D)
        XST = av(35840, 3, 8)

        block = ctx.enter_context(nc.Block())

        def flat(ap):
            n = len(ap.shape)
            if n == 3:
                return ap.rearrange("p a b -> p (a b)")
            if n == 4:
                return ap.rearrange("p a b c -> p (a b c)")
            return ap

        def stage2_loads(sp, slots, two_layer):
            for name, groups in (("dn", 8), ("small", 1), ("rw", 6), ("out2", 4), ("xk", 1), ("xv", 1), ("xq", 1),
                                 ("xo", 1)):
                slots(name, SLOT0[name], groups, width=4 * 272 if name == "small" else 2048)
            two_layer("f1", "f2", SLOT0["ffn"], FB)
            for t in range(NT):
                sp.wait_ge(ev["final"], t + 1)
                sp.dma_start(out[t * P:(t + 1) * P, :], X[:, t, :]).then_inc(ev["stored"], 16)
            sp.wait_ge(ev["stored"], 16 * NT)

        @block.sync
        def _(sp):
            def slots(name, base, groups, rows=None, width=2048):
                w = a[name]
                def one(i, s, n):
                    if not isinstance(n, int) or n >= 4:
                        sp.wait_ge(ev["split_low"], n - 3)
                    src = w[bass.ds(4 * i + s, 1)].rearrange("a p b -> (a p) b")
                    sp.dma_start(flat(ring[s])[:, 0:width], src).then_inc(slot_full[s], 16)
                if base == 0:
                    for s in range(4):
                        one(0, s, s)
                    with sp.Fori(1, groups, 1) as i:
                        for s in range(4):
                            one(i, s, base + 4 * i + s)
                elif groups == 1:
                    for s in range(4):
                        one(0, s, base + s)
                else:
                    with sp.Fori(0, groups, 1) as i:
                        for s in range(4):
                            one(i, s, base + 4 * i + s)

            def two_layer(first, second, base, blocks):
                u, v = a[first], a[second]
                def four(w, i, n):
                    for s in range(4):
                        sp.wait_ge(ev["split_low"], n + s - 3)
                        src = w[bass.ds(4 * i + s, 1)].rearrange("a p b -> (a p) b")
                        sp.dma_start(flat(ring[s]), src).then_inc(slot_full[s], 16)
                def gates(b, i, par):
                    src = g_dram[:, :, bass.ds(256 * b, 256)].rearrange("q p n -> p q n")
                    sp.dma_start(GBK[par].rearrange("p q j t -> p q (j t)"), src).then_inc(ev[f"gates_in{par}"], 16)

                four(u, 0, base)
                four(u, 1, base + 4)
                if first == "pu":
                    rows = lambda q: GST[q % 2].rearrange("p j t -> p (j t)")
                    for q in range(3):
                        sp.wait_ge(ev["bank_empty"], 2 + 16 * (q + 1))
                        sp.dma_start(g_dram[q], rows(q)).then_inc(ev[f"gates_stored{q % 2}"], 16)
                    sp.wait_ge(ev["bank_empty"], 2 + 16 * 4)
                    sp.dma_start(g_dram[3, :, 0:512], rows(3)[:, 0:512]).then_inc(ev["gates_first"], 16)
                    sp.wait_ge(ev["gates_stored0"], 32)
                    sp.wait_ge(ev["gates_stored1"], 16)
                    sp.wait_ge(ev["gates_first"], 16)
                    gates(0, 0, 0)
                    gates(1, 0, 1)
                    sp.dma_start(g_dram[3, :, 512:64 * P], rows(3)[:, 512:64 * P]).then_inc(ev["gates_stored1"], 16)
                with sp.Fori(0, blocks // 2 - 1, 1) as i:
                    for par in range(2):
                        b = 2 * i + par
                        four(v, b, base + 8 + 16 * i + 8 * par)
                        four(u, b + 2, base + 12 + 16 * i + 8 * par)
                        if first == "pu":
                            sp.wait_ge(ev["gates_stored1"], 32)
                            sp.wait_ge(ev["peer_gated"], b + 1)
                            gates(b + 2, 0, par)
                four(v, blocks - 2, base + 8 * blocks - 8)
                four(v, blocks - 1, base + 8 * blocks - 4)

            for t in range(NT):
                sp.dma_start(X[:, t, :], a["x"][t * P:(t + 1) * P, :]).then_inc(ev["x_loaded"], 16)
            sp.dma_start(COL1, a["cols1"]).then_inc(ev["consts1"], 16)
            sp.dma_start(ROW, a["rows"].partition_broadcast(P)).then_inc(ev["consts1"], 16)
            sp.dma_start(flat(WG), a["w_gates"]).then_inc(ev["consts1"], 16)
            slots("win", SLOT0["win"], 12)
            slots("wout", SLOT0["wout"], 4)
            slots("wq", SLOT0["wq"], 4)
            sp.wait_ge(ev["tp_scaled"], 6)
            sp.dma_start(flat(KEYS), a["keys"]).then_inc(ev["keys_in"], 16)
            two_layer("pu", "pv", SLOT0["peer"], EB)
            stage2_loads(sp, slots, two_layer)

        def inverse_pool(pool, c, At):
            def between(q, level):
                nc.gpsimd.tensor_tensor(AOFS[c][:, q], At[:, 4 * q:4 * q + 4, :],
                                        level.broadcast_to([P, 4, P]), ALU.mult).then_inc(ev["inv_off"], 1)

            for l in range(1, 7):
                for q in range(4):
                    if l >= 2:
                        pool.wait_ge(ev["inv_m1"], 4 * l + (24 * c - 5 + q))
                    between(q, LVA[:, l:l + 1, :])

        def stage2_pool(pool, o):
            pool.wait_ge(ev["peer_ready"], EB)
            pool.dma_start(FNW, a["fnw1"].partition_broadcast(P)).then_inc(ev["fnw_in"], 16)
            pool.wait_ge(ev["norm_root"], 4)
            o.done(nc.gpsimd.memset(LW[:, 0:1], 0.0))
            o.done(nc.gpsimd.memset(LG[:, 0:1], 0.0), ev["pads"])
            pool.wait_ge(*nth("at_out", 4))
            inverse_pool(pool, 0, AT_)
            pool.wait_ge(ev["dn_done"], 1)
            o.done(nc.gpsimd.memset(W2[64:P, :], 0.0))
            o.done(nc.gpsimd.memset(A2[0:64, :], 0.0), ev["lora_zero"])
            pool.dma_start(W2[0:64, :], a["w2"]).then_inc(ev["lora_in"], 16)
            pool.dma_start(A2[64:P, :], a["a2"]).then_inc(ev["lora_in"], 16)
            pool.dma_start(G2, a["g2"]).then_inc(ev["lora_in"], 16)
            for hf in range(2):
                pool.wait_ge(ev["decayed"], hf + 1)
                pool.wait_ge(ev["gram_out"], 16 * hf + 16)
                inverse_pool(pool, 1 + hf, GR[:, :, 0, :])
            pool.wait_ge(ev["rw_done"], 2)
            for t in range(NT):
                pool.dma_start(MEMX[:, t, :], a["mem"][t * P:(t + 1) * P, :]).then_inc(ev["mem_in"], 16)
            pool.dma_start(FNW, a["fnw"].partition_broadcast(P)).then_inc(ev["fnw_in"], 16)

        @block.gpsimd
        def _(pool):
            o = Own(pool, ev["pool_order"])

            def select(out, in_, op, pattern, base, cm, fill=0.0):
                return nc.gpsimd.affine_select(out=out, in_=in_, compare_op=op, fill=fill, base=base,
                                               pattern=pattern, channel_multiplier=cm)

            def masks():
                o.tell(select(UI, ONES, ALU.is_ge, [[1, P]], 0, -1), ev["masks"])
                o.tell(select(LS, ONES, ALU.is_gt, [[-1, P]], 0, 1), ev["masks"])
                o.done(nc.gpsimd.memset(TRI, 0.0))
                o.done(select(TRI[:, P:2 * P], TRI[:, P:2 * P], ALU.is_ge, [[-1, P]], 0, 1, NEG), ev["masks"])
                for i in range(7):
                    b = 1 << i
                    v = BD[i].rearrange("p (n b) -> p n b", b=b)
                    one = ONES.rearrange("p (n b) -> p n b", b=b)
                    o.done(select(v, one, ALU.is_ge, [[-b, P // b], [0, b]], 0, 1))
                    o.done(select(v, v, ALU.is_ge, [[b, P // b], [0, b]], b - 1, -1), ev["masks"])
                for i in range(7):
                    o.done(nc.gpsimd.tensor_tensor(LV[i], BD[i + 1] if i < 6 else ONES, BD[i], ALU.subtract), ev["masks"])
                for i in range(2):
                    o.done(nc.gpsimd.tensor_tensor(M4[:, 2 * i + 1, :], UI, BD[6], ALU.mult))
                    o.done(nc.gpsimd.tensor_tensor(M4[:, 2 * i, :], M4[:, 2 * i + 1, :], ID, ALU.subtract), ev["masks"])

            pool.dma_start(COL2, a["cols2"]).then_inc(ev["consts2"], 16)
            o.done(nc.gpsimd.memset(ONES, 1.0))
            o.done(select(ID, ONES, ALU.is_equal, [[-1, P]], 0, 1))
            o.done(nc.gpsimd.iota(IO32, pattern=[[1, P]], base=0, channel_multiplier=0))
            o.done(nc.gpsimd.tensor_copy(IOTA, IO32))
            o.done(nc.gpsimd.memset(COL16, 0.0))
            o.done(nc.gpsimd.memset(COL16[:, 15:16], 1.0))
            o.done(nc.gpsimd.memset(MQK[:, :, 0:3], 0.0))
            o.done(nc.gpsimd.memset(MV1[:, :, :, MV:MV + 1], 1.0))
            masks()
            stage2_pool(pool, o)
        def gates_act(act, o):
            act.wait_ge(*nth("gate_abs", 1))
            o.done(nc.scalar.activation(TM[:, 0:2, :], TM[:, 0:2, :], ACT.Exp, scale=-1.0))
            o.tell(nc.scalar.activation(TM[:, 0:2, :], TM[:, 0:2, :], ACT.Ln, bias=1.0), ev["gate_ln"])

        def mlstm_act(act, o):
            act.wait_ge(*nth("m_arg", 1))
            nc.scalar.activation(flat(DM), flat(DM), ACT.Exp)
            nc.scalar.activation(INTER, INTER, ACT.Exp)
            nc.scalar.activation(KCOL, KCOL, ACT.Exp)
            o.tell(nc.scalar.activation(EM, MT, ACT.Exp, scale=-1.0), ev["m_exp"])
            for c in range(NT):
                act.wait_ge(*nth("sm_turned", c + 1))
                o.tell(nc.scalar.copy(flat(SMT[:, c]), PQ[:, c, :]), ev["smt_out"])
            for h in range(MH):
                act.wait_ge(*nth("cp_mm", h + 1))
                o.tell(nc.scalar.copy(CP[:, h, :], PQ[:, h, 0:MV + 1]), ev["cp_out"])
            act.wait_ge(*nth("m_exp", 1))
            for h in range(MH):
                act.wait_ge(*nth("inter_mm", h + 1))
                o.tell(nc.scalar.mul(TMP[:, h, :], PQ[:, h, 0:MV + 1], INTER[:, h:h + 1]), ev["inter_out"])

        def two_act(act, name, blocks, func, high):
            base = SLOT0[name]
            h = PQ[:, 0:2, :].rearrange("p a b -> p (a b)")
            gated = ev[name + "_gated"]

            def hidden(used_by):
                act.wait_ge(used, used_by)
                nc.scalar.activation(HID, h, func).then_inc(ev[name + "_acted"], 1)

            def hidden_high(b, par):
                act.wait_ge(gated, b + 1)
                nc.scalar.copy(AH[par][:, :], HID).then_inc(ev[name + "_high"], 1)

            def block(n, b, par):
                for s in range(4):
                    high(n + s, s)
                high(n + 4, 0)
                high(n + 5, 1)
                hidden(n + 4)
                high(n + 6, 2)
                hidden_high(b, par)
                high(n + 7, 3)

            if name == "peer":
                act.wait_ge(ev["rows_used"], T // 4 + 2)
                act.wait_ge(ev["gates_stored0"], 32)
            if name != "peer":
                high(base + 2, 2)
                high(base + 3, 3)
            hidden(base + 4)
            hidden_high(0, 0)
            with act.Fori(0, blocks // 2 - 1, 1) as i:
                for par in range(2):
                    block(16 * i + (base + 4 + 8 * par), 2 * i + (1 + par), 1 - par)
            block(base + 8 * blocks - 12, blocks - 1, 1)
            for s in range(4):
                high(base + 8 * blocks - 4 + s, s)

        def inverse_act(act, c):
            if c == 0:
                for _ in range(2):
                    act.nop().then_inc(ev["inv_m1_out"], 1)
            with act.Fori(1, 7, 1) as l:
                for q in range(4):
                    g = 4 * l + (24 * c - 4 + q)
                    act.wait_ge(ev["inv_m1"], g + 3)
                    act.wait_ge(ev["inv_t"], g + 1)
                    nc.scalar.copy(M1B[:, q % 2], PQ[:, q % 2, :].rearrange("p (m j) -> p m j", m=4)
                                   ).then_inc(ev["inv_m1_out"], 1)

        def stage2_act(act, o, half, freed, sums, high, highs, split_rows):
            highs("dn", 0, (0, 1))
            sums(2, X, (ev["dve_free"], DVE0["dn"]))
            sums(3, X, (ev["block1_out"], 2))
            split_rows()
            units = [("dn", j) for j in range(8)] + [("small", 0)] + [("rw", j) for j in range(6)]
            highs("dn", 0, (2, 3))
            for u, (name, j) in enumerate(units):
                after = units[u + 1] if u + 1 < len(units) else None
                w = 4 * 272 if after and after[0] == "small" else 2048
                if after:
                    highs(*after, (0, 1), w)
                if name == "small":
                    act.wait_ge(ev["pads"], 1)
                ps = half(name, j)
                if name == "rw":
                    dst = RAWS[j // 3][:, j % 3, 2:4, 1:1 + T]
                    freed(nc.scalar.copy(dst, ps.rearrange("p (n t) -> p n t", n=2)))
                elif name == "small":
                    nc.scalar.copy(LW[:, 1:1 + T], ps[:, 0:T])
                    freed(nc.scalar.copy(LG[:, 1:1 + T], ps[:, T:2 * T]))
                elif j < 6:
                    if j == 0:
                        act.wait_ge(*nth("cin_pad", 1))
                    if j >= 2:
                        act.wait_ge(*nth("dn_conv", j - 1))
                    c = 4 * (j % 2)
                    freed(nc.scalar.copy(CIN[:, c + 2:c + 4, 3:3 + T], ps.rearrange("p (n t) -> p n t", n=2)))
                else:
                    freed(nc.scalar.activation(ZT[:, 1, BLK * (j - 6):BLK * (j - 5)], ps, ACT.Silu))
                if after:
                    highs(*after, (2, 3), w)
                if name == "dn" and 1 <= j < 7:
                    act.wait_ge(*nth("dn_conv", j))
                    o.tell(nc.scalar.activation(flat(QKV[:, 4 * j - 4:4 * j, :]), flat(QKV[:, 4 * j - 4:4 * j, :]), ACT.Silu),
                           ev["dn_silu"])
            act.wait_ge(ev["dve_free"], DVE0["dn"] + 8)
            o.tell(nc.scalar.activation(ZT[:, 0, :], ZT[:, 0, :], ACT.Silu), ev["z_silu"])
            act.wait_ge(used, SLOT0["out2"])
            act.wait_ge(*nth("dn_silu", 6))
            o.tell(nc.scalar.activation(flat(SQD), flat(QKV[:, 0:16, :]), ACT.Square), ev["dn_sq"])
            act.wait_ge(*nth("dn_sq", 1))
            act.wait_ge(*nth("l2_mm", 1))
            o.tell(nc.scalar.activation(L2[0:16, :], PQ[0:16, 0, 0:T], ACT.Sqrt, bias=EPSC[0:16, :]), ev["l2_root"])
            act.wait_ge(*nth("g_abs", 1))
            o.done(nc.scalar.activation(DST[:, 1], DST[:, 1], ACT.Exp, scale=-1.0))
            nc.scalar.activation(DST[:, 1], DST[:, 1], ACT.Ln, bias=1.0)
            nc.scalar.activation(DST[:, 5, 0, :], ROW[:, 16:24], ACT.Exp)
            o.tell(nc.scalar.activation(DST[:, 4], GB[:, :, 8:16], ACT.Sigmoid), ev["g_act"])
            act.wait_ge(*nth("gc_out", 1))
            nc.scalar.activation(DST[:, 8], DST[:, 6], ACT.Exp)
            o.tell(nc.scalar.activation(DST[:, 9], DST[:, 9], ACT.Exp), ev["gc_exp"])
            act.wait_ge(*nth("dec_arg", 1))
            o.tell(nc.scalar.activation(flat(DEC), flat(DEC), ACT.Exp), ev["dec_out"])
            for n in range(4):
                act.wait_ge(*nth("qd_turned", n + 1))
                o.tell(nc.scalar.copy(flat(ATN)[:, BLK * n:BLK * (n + 1)], PP[:, n // 2, n % 2, :]), ev["atn_out"])
            for n in range(4):
                act.wait_ge(*nth("a_turned", n + 1))
                o.tell(nc.scalar.copy(flat(AT_)[:, BLK * n:BLK * (n + 1)], PQ[:, n, :]), ev["at_out"])
            for n in range(4):
                act.wait_ge(*nth("v_turned", n + 1))
                o.tell(nc.scalar.copy(VT[:, n // 2, 4 * (n % 2):4 * (n % 2) + 4, :],
                                      PP[:, n // 2, n % 2, :].rearrange("p (h d) -> p h d", h=4)), ev["v_tok"])
            inverse_act(act, 0)
            act.wait_ge(ev["qs_mm"], 1)
            for h in range(DH):
                o.tell(nc.scalar.mul(OTM[:, h, :], PP[:, 0, h // 4, (h % 4) * P:(h % 4 + 1) * P], DST[:, 8, 1, h:h + 1]),
                       ev["qs_out"])
            act.wait_ge(ev["od_ready"], 1)
            o.done(nc.scalar.activation(flat(VT), flat(OD), ACT.Square), ev["od_sq"])
            act.wait_ge(ev["od_sum"], 1)
            o.tell(nc.scalar.activation(DST[:, 1], DST[:, 0], ACT.Sqrt, scale=1.0 / P, bias=EPSC), ev["od_root"])
            for hf in range(2):
                rw_act(act, o, hf, half, freed)
            act.wait_ge(ev["rw_done"], 2)
            nc.scalar.copy(XTH_[:, :], flat(YT)).then_inc(ev["yt_high"], 1)
            act.wait_ge(ev["yt_low"], 1)
            for j in range(4):
                highs("out2", j, range(4))
            highs("xk", 0, (0, 1))
            act.wait_ge(used, SLOT0["xk"])
            sums(4, MEMX, (ev["mem_in"], 32), av(20480, NT, D))
            split_rows()
            highs("xk", 0, (2, 3))
            highs("xv", 0, (0, 1))
            freed(nc.scalar.copy(flat(XK[:, 2:4, :]), half("xk", 0)))
            highs("xv", 0, (2, 3))
            freed(nc.scalar.copy(XV[:, 1, :], half("xv", 0)))
            highs("xq", 0, (0, 1))
            act.wait_ge(used, SLOT0["xq"])
            sums(5, X, (ev["dve_free"], DVE0["xk"]))
            split_rows()
            highs("xq", 0, (2, 3))
            freed(nc.scalar.copy(flat(XQ[:, 2:4, :]), half("xq", 0)))
            act.wait_ge(*nth("xa_max", 1))
            for n in range(8):
                ins = nc.scalar.activation(XP[:, n // 2, n % 2, :], PQ[:, n // 2, (n % 2) * T:(n % 2 + 1) * T], ACT.Exp,
                                           scale=QK_SCALE, bias=XST[:, 0, n:n + 1], accum_out=XST[:, 1, n:n + 1])
            o.tell(ins, ev["xa_exp"])
            for n in range(4):
                act.wait_ge(*nth("xa_turned", n + 1))
                o.tell(nc.scalar.copy(flat(XPT[:, n]), PP[:, n // 2, n % 2, :]), ev["xa_pt"])
            for n in range(4):
                act.wait_ge(*nth("xa_o", n + 1))
                ins = nc.scalar.copy(HID[:, n * T:(n + 1) * T], PQ[:, n, 0:T])
            o.done(ins)
            o.tell(nc.scalar.copy(AH[0][:, :], HID), ev["xo_high"])
            highs("xo", 0, range(4))
            highs("ffn", 0, (0, 1))
            sums(6, X, (ev["dve_free"], DVE0["ffn"]))
            split_rows()
            two_act(act, "ffn", FB, ACT.Relu, high)
            sums(7, X, (ev["dve_free"], DVE0["ffn"] + 4 * FB))

        def rw_act(act, o, hf, half, freed):
            if hf == 0:
                act.wait_ge(ev["lw_shift"], 1)
                nc.scalar.activation(LW[0:64, 0:T], LW[0:64, 0:T], ACT.Tanh)
                o.tell(nc.scalar.activation(LG[:, 0:T], LG[:, 0:T], ACT.Sigmoid), ev["lw_act"])
            for n, (dst, bias) in enumerate(((LDX, "w0"), (AA, "a0"), (GATE, None))):
                act.wait_ge(ev["lora_mm"], 3 * hf + n + 1)
                for j in range(J):
                    b = 2 * (n % 2) + j // 2
                    src = PQ[:, b, (j % 2) * T:(j % 2 + 1) * T]
                    if bias:
                        ins = nc.scalar.activation(dst[:, j, :], src, ACT.Sigmoid, bias=col2(bias, J * hf + j))
                    else:
                        ins = nc.scalar.copy(dst[:, j, :], src)
                o.tell(ins, ev["lora_out"])
            act.wait_ge(ev["kk_mm"], hf + 1)
            o.tell(nc.scalar.activation(flat(E1), PQ[:, 2:4, :].rearrange("p a b -> p (a b)"), ACT.Sqrt), ev["kk_root"])
            for n in range(9):
                act.wait_ge(ev["decay_arg"], 9 * hf + n + 1)
                cols = slice(0, 1024) if n < 3 else slice(512 * ((n + 1) % 2), 512 * ((n + 1) % 2 + 1))
                o.tell(nc.scalar.activation(flat(E2)[:, cols], flat(E1)[:, cols], ACT.Exp, scale=-1.0 if n == 1 else 1.0),
                       ev["decay_exp"])
            for n in range(2):
                act.wait_ge(ev["rv_turned"], 2 * hf + n + 1)
                o.tell(nc.scalar.copy(VTK[:, n, :], PP[:, n, 0, :]), ev["rv_tok"])
            for n in range(2):
                act.wait_ge(ev["bk_turned"], 2 * hf + n + 1)
                o.tell(nc.scalar.copy(BKT[:, n, :], PP[:, n, 1, :]), ev["bk_tok"])
            for m in range(16):
                act.wait_ge(ev["gram_diag"], 16 * hf + m + 1)
                o.tell(nc.scalar.copy(GR[0:64, m, :, 64:P], PP[0:64, (m % 4) // 2, m % 2, 0:256].rearrange("p (a t) -> p a t", a=4)),
                       ev["gram_out"])
            inverse_act(act, 1 + hf)
            act.wait_ge(ev["gn_mean"], hf + 1)
            o.tell(nc.scalar.activation(flat(RY2), flat(RY), ACT.Square), ev["gn_sq"])
            act.wait_ge(ev["gn_sum"], hf + 1)
            o.tell(nc.scalar.activation(RST[:, 1, :], RST[:, 0, :], ACT.Sqrt, scale=1.0 / 64, bias=RWEPSC), ev["gn_root"])

        @block.scalar
        def _(act):
            o = Own(act, ev["act_order"])

            def half(name, j):
                act.wait_ge(used, SLOT0[name] + 4 * (j + 1))
                return PP[:, (UNIT0[name] + j) % 2, 1, :]

            def freed(ins):
                o.tell(ins, ev["act_free"])

            def high(n, s, w=2048):
                act.wait_ge(slot_full[s], 4 * n + (16 - 4 * s))
                if not isinstance(n, int) or n >= 2:
                    act.wait_ge(used, n - 1)
                nc.scalar.copy(WH[s % 2][:, 0:w], flat(ring[s])[:, 0:w]).then_inc(ev["split_high"], 1)

            def highs(name, j, slots, w=2048):
                for s in slots:
                    high(SLOT0[name] + 4 * j + s, s, w)

            def split_rows(banks=8):
                for _ in range(banks):
                    n = split_rows.n
                    t, g = (n % 8) // 4, n % 4
                    act.wait_ge(ev["rows_out"], n + 1)
                    nc.scalar.copy(XTH[:, 4 * g:4 * g + 4, t * P:(t + 1) * P],
                                   XTS[:, n % 2, :].rearrange("p (n t) -> p n t", n=4)).then_inc(ev["rows_high"], 1)
                    split_rows.n += 1
            split_rows.n = 0

            def sums(i, src, ready, squares=SCN):
                nc.scalar.activation(SM[:, 8:9], EPSC, ACT.Sqrt)
                act.wait_ge(*ready)
                for t in range(NT):
                    o.tell(nc.scalar.activation(squares[:, t, :], src[:, t, :], ACT.Square,
                                                accum_out=SS[:, t:t + 1]), o.order)
                act.wait_ge(o.order, o.n[id(o.order)])
                o.tell(nc.scalar.activation(RS, SS, ACT.Sqrt, scale=1.0 / D, bias=EPSC), ev["norm_root"])

            for _ in range(2):
                act.nop().then_inc(ev["act_free"], 1)
            act.wait_ge(ev["dve_init"], 2)
            sums(0, X, (ev["x_loaded"], 32))
            act.wait_ge(ev["consts1"], 48)
            nc.scalar.copy(WGH[:, :], flat(WG)).then_inc(ev["wg_high"], 1)
            split_rows()
            highs("win", 0, (0, 1))
            gates_act(act, o)
            highs("win", 0, (2, 3))
            for j in range(12):
                if j < 11:
                    highs("win", j + 1, (0, 1))
                ps = half("win", j)
                if j < 2:
                    freed(nc.scalar.copy(MQK[:, 4 * j + 2:4 * j + 4, 3:3 + T], ps.rearrange("p (n t) -> p n t", n=2)))
                elif j < 4:
                    freed(nc.scalar.mul(flat(FQ[:, 4 * (j - 2) + 2:4 * (j - 2) + 4, :]), ps, QK_SCALE))
                elif j < 6:
                    freed(nc.scalar.copy(flat(FK[:, 4 * (j - 4) + 2:4 * (j - 4) + 4, :]), ps))
                elif j < 8:
                    freed(nc.scalar.copy(FV[:, 1, BLK * (j - 6):BLK * (j - 5)], ps))
                elif j < 10:
                    freed(nc.scalar.copy(MV1[:, 1, 2 * (j - 8):2 * (j - 8) + 2, 0:MV], ps.rearrange("p (h v) -> p h v", h=2)))
                else:
                    freed(nc.scalar.copy(MO[:, 1, BLK * (j - 10):BLK * (j - 9)], ps))
                if j < 11:
                    highs("win", j + 1, (2, 3))
            act.wait_ge(*nth("conv_out", 1))
            o.done(nc.scalar.activation(flat(MQC), flat(MQC), ACT.Silu), ev["qk_silu"])
            act.wait_ge(*nth("mo_ready", 1))
            act.wait_ge(ev["act_free"], 2 + 12)
            o.done(nc.scalar.activation(flat(MO), flat(MO), ACT.Sigmoid), ev["mo_gate"])
            for h in range(FH):
                act.wait_ge(ev["fox_max"], h + 1)
                b = h % 2
                nc.scalar.activation(FP[:, b, 0:P], FS[:, b, 0:P], ACT.Exp, bias=FST[:, b, 0:1], accum_out=FST[:, b, 2:3])
                o.tell(nc.scalar.activation(FP[:, b, P:384], FS[:, b, P:384], ACT.Exp, bias=FST[:, b, 1:2],
                                            accum_out=FST[:, b, 3:4]), ev["fox_exp"])
                act.wait_ge(ev["fox_turned"], h + 1)
                if h >= 2:
                    act.wait_ge(ev["fox_pv"], h - 1)
                o.tell(nc.scalar.copy(FPT[:, b, :], PQ[:, 2 + b, 0:384]), ev["fox_pt"])
            mlstm_act(act, o)
            act.wait_ge(*nth("mix_ready", 2))
            o.done(nc.scalar.activation(flat(SCR), flat(MIX), ACT.Square), ev["mix_sq"])
            act.wait_ge(*nth("mix_sum", 1))
            nc.scalar.activation(HN[:, 1, 0:16], HN[:, 0, 0:16], ACT.Sqrt, scale=1.0 / P, bias=EPSC)
            o.tell(nc.scalar.activation(HN[:, 1, 16:24], HN[:, 0, 16:24], ACT.Sqrt, scale=1.0 / MV, bias=EPSC),
                   ev["mix_root"])
            split_rows()
            for j in range(4):
                highs("wout", j, range(4))
            highs("wq", 0, (0, 1))
            sums(1, X, (ev["dve_free"], DVE0["wq"]))
            split_rows()
            highs("wq", 0, (2, 3))
            for j in range(4):
                if j < 3:
                    highs("wq", j + 1, (0, 1))
                ps = half("wq", j)
                freed(nc.scalar.copy(flat(PQT[:, 4 * j + 2:4 * j + 4, :]), ps))
                if j < 3:
                    highs("wq", j + 1, (2, 3))
            for n in range(8):
                act.wait_ge(*nth("scores_mm", n + 1))
                o.tell(nc.scalar.copy(flat(SC)[:, BLK * n:BLK * (n + 1)], PQ[:, n % 4, :]), ev["scores_out"])
            highs("peer", 0, range(4))
            act.wait_ge(*nth("gate_arg", 1))
            o.tell(nc.scalar.activation(flat(SF), flat(SF), ACT.Exp), ev["gate_exp"])
            for _ in range(2):
                act.nop().then_inc(ev["bank_empty"], 1)
            for q in range(4):
                gview = GST[q % 2].rearrange("p j t -> p t j")
                if q >= 2:
                    act.wait_ge(ev[f"gates_stored{q % 2}"], 16)
                with act.Fori(0, 8, 1) as i:
                    for b in range(2):
                        act.wait_ge(ev["rows_used"], 2 * i + (16 * q + b + 3))
                        nc.scalar.copy(gview[:, bass.ds(8 * i + 4 * b, 4), :],
                                       PQ[:, 2 + b, :].rearrange("p (t j) -> p t j", t=4)).then_inc(ev["bank_empty"], 1)
            two_act(act, "peer", EB, ACT.Gelu, high)
            stage2_act(act, o, half, freed, sums, high, highs, split_rows)
        def mlstm_dve(dve, o, v):
            B = CS[:, 0:2, 12:16]
            o.done(v.tensor_tensor(RC, GT[:, :, 8:12], B, ALU.subtract))
            o.done(v.tensor_tensor(DGM.rearrange("p c h s -> p (c h) s"), rep(ID, 8),
                                   bc(RC.rearrange("p c h -> p (c h)"), P), ALU.mult), ev["m_diag"])
            dve.wait_ge(*nth("r_mm", 1))
            R = [PQ[:, c, :].rearrange("p (h s) -> p h s", h=MH) for c in range(NT)]
            o.done(v.tensor_reduce(MREC[:, 0, :], R[0], AX.X, ALU.max))
            for c in range(NT):
                o.tell(v.tensor_tensor(DM[:, c], R[c], rep(TRI[:, P:2 * P], MH), ALU.add), ev["r_read"])
            dve.wait_ge(*nth("r_read", 2))
            o.done(v.tensor_reduce(RM, DM, AX.X, ALU.max))
            BL = CS[:, 2, 12:16]
            W = TM[:, 0, :]
            o.done(v.tensor_tensor(W[:, 0:4], BL, MREC[:, 0, :], ALU.add))
            o.done(v.tensor_tensor(W[:, 0:4], BL, W[:, 0:4], ALU.max))
            o.done(v.tensor_tensor(RM, RM, B, ALU.add))
            o.done(v.tensor_tensor(MT[:, 0], B[:, 0], RM[:, 0], ALU.max))
            o.done(v.tensor_tensor(W[:, 4:8], B[:, 1], W[:, 0:4], ALU.add))
            o.done(v.tensor_tensor(MT[:, 1], W[:, 4:8], RM[:, 1], ALU.max))
            o.done(v.tensor_tensor(INTER, W[:, 4:8], MT[:, 1], ALU.subtract))
            o.done(v.tensor_tensor(EXB, B, MT, ALU.subtract))
            o.done(v.tensor_tensor(W[:, 8:12], BL, W[:, 0:4], ALU.subtract))
            o.done(v.tensor_tensor(KCOL, RC[:, 0], W[:, 8:12], ALU.add))
            o.done(v.tensor_tensor(DM, DM, bc(EXB, P), ALU.add), ev["m_arg"])
            dve.wait_ge(*nth("m_exp", 1))
            for c in range(NT):
                dve.wait_ge(*nth("qk_mm", c + 1))
                o.done(v.scalar_tensor_tensor(SMM[:, c], PP[:, c, 0, :].rearrange("p (h s) -> p h s", h=MH), QK_SCALE,
                                              DM[:, c], ALU.mult, ALU.mult), ev["sm_ready"])
            dve.wait_ge(*nth("k_turned", 1))
            o.done(v.tensor_scalar(KCOL, KCOL, QK_SCALE, None, ALU.mult))
            o.done(v.tensor_tensor(KA, PQ[:, 2, :].rearrange("p (h s) -> p h s", h=MH), bc(KCOL, P), ALU.mult),
                   ev["ka_ready"])
            for h in range(MH):
                dve.wait_ge(*nth("num0_mm", h + 1))
                ins = v.tensor_copy(NUM[:, 0, h, :], PP[:, h // 2, h % 2, 0:MV + 1])
                o.tell(ins, ev["num0_out"])
            for h in range(MH):
                dve.wait_ge(*nth("num1_mm", h + 1))
                dve.wait_ge(*nth("inter_out", h + 1))
                o.tell(v.tensor_tensor(NUM[:, 1, h, :], PP[:, h // 2, h % 2, 0:MV + 1], TMP[:, h, :], ALU.add), o.order)
            dve.wait_ge(*nth("num0_out", 4))
            dve.wait_ge(o.order, o.n[id(o.order)])
            DEN = NUM[:, :, :, MV:MV + 1].rearrange("p c h o -> p c (h o)")
            o.done(v.scalar_tensor_tensor(MREC, DEN, -1.0, DEN, ALU.mult, ALU.max))
            o.done(v.tensor_tensor(MREC, MREC, EM, ALU.max))
            o.done(v.reciprocal(MREC, MREC))
            dve.wait_ge(*nth("mo_gate", 1))
            for c in range(NT):
                for h in range(MH):
                    ins = v.scalar_tensor_tensor(MIX[:, c, 1024 + MV * h:1024 + MV * (h + 1)], NUM[:, c, h, 0:MV],
                                                 MREC[:, c, h:h + 1], MO[:, c, MV * h:MV * (h + 1)], ALU.mult, ALU.mult)
                o.tell(ins, ev["mix_ready"])

        def select_dve(dve, o, v, lows):
            dve.wait_ge(*nth("scores_out", 8))
            I16U, PFU = I16.bitcast(U32), PF.bitcast(U32)
            rows = [(SC[:, t, n, :], SW[:, t, n, :], S16[:, t, n, :], I16U[:, t, n, :]) for t in range(NT) for n in range(16)]
            top16(o, v, rows)
            lows("peer", 0, range(2))
            o.done(v.tensor_copy(flat(IF), flat(I16U)))
            s16 = S16.rearrange("p t (h q) k -> p t h q k", q=2)
            for t in range(NT):
                for h in range(PH):
                    ins = v.tensor_tensor(CD[:, t, h, :].rearrange("p (a b) -> p a b", a=TOPK), bc(s16[:, t, h, 0, :], TOPK),
                                          rep(s16[:, t, h, 1, :], TOPK), ALU.add)
            o.done(ins)
            rows = [(CD[:, t, h, :], CW[:, t, h, :], SF[:, t, h, :], PFU[:, t, h, :]) for t in range(NT) for h in range(PH)]
            top16(o, v, rows)
            o.done(v.tensor_copy(GS[:, 0], SF[:, :, :, 0]))
            o.done(v.tensor_tensor(SF.rearrange("p t h k -> p (t h) k"), SF.rearrange("p t h k -> p (t h) k"),
                                   bc(GS[:, 0].rearrange("p t h -> p (t h)"), TOPK), ALU.subtract), ev["gate_arg"])
            o.done(v.tensor_scalar(PA.bitcast(U32), PFU, 4, None, ALU.logical_shift_right))
            o.done(v.tensor_scalar(PB.bitcast(U32), PFU, 15, None, ALU.bitwise_and))
            o.done(v.tensor_copy(flat(PA), flat(PA.bitcast(U32))))
            o.done(v.tensor_copy(flat(PB), flat(PB.bitcast(U32))))
            i16 = IF.rearrange("p t (h q) k -> p t h q k", q=2)
            for t in range(NT):
                for q, place in ((0, PA), (1, PB)):
                    o.done(v.tensor_tensor(OH, bc(place[:, t].rearrange("p h k -> p (h k)"), TOPK), rep(IOTA[:, 0:TOPK], P),
                                           ALU.is_equal))
                    for h in range(PH):
                        ins = v.tensor_tensor(OH2[:, TOPK * h:TOPK * (h + 1), :], OH[:, TOPK * h:TOPK * (h + 1), :],
                                              rep(i16[:, t, h, q, :], TOPK), ALU.mult)
                    o.done(ins)
                    o.done(v.tensor_reduce(SEL[:, q, t, :], OH2, AX.X, ALU.add), ev["sel_ready"])
                if t == 0:
                    lows("peer", 0, (2, 3))
            dve.wait_ge(*nth("gate_exp", 1))
            o.done(v.tensor_reduce(GS[:, 1], SF, AX.X, ALU.add))
            o.done(v.reciprocal(GS[:, 2], GS[:, 1]))
            o.done(v.tensor_tensor(GA.rearrange("p t (h k) -> p (t h) k", k=TOPK), SF.rearrange("p t h k -> p (t h) k"),
                                   bc(GS[:, 2].rearrange("p t h -> p (t h)"), TOPK), ALU.mult), ev["gate_ready"])
            dve.wait_ge(*nth("hk_turned", 1))
            o.tell(v.tensor_copy(HKT[:, 0:512], PQ[:, 2, :]), o.order)
            dve.wait_ge(o.order, o.n[id(o.order)])
            o.done(v.tensor_copy(HKT[:, 512:768], PQ[:, 3, 0:256]), ev["hk_ready"])

        def top16(o, v, rows):
            def wave(make):
                for r in rows:
                    ins = make(*r)
                o.done(ins)
            wave(lambda s, w, top, idx: v.max(top[:, 0:8], s))
            wave(lambda s, w, top, idx: v.max_index(idx[:, 0:8], top[:, 0:8], s))
            wave(lambda s, w, top, idx: v.match_replace(w, top[:, 0:8], s, -3e38))
            wave(lambda s, w, top, idx: v.max(top[:, 8:16], w))
            wave(lambda s, w, top, idx: v.max_index(idx[:, 8:16], top[:, 8:16], w))

        def two_dve(dve, o, v, name, blocks, low):
            base = SLOT0[name]
            gated = ev[name + "_gated"]

            def gate(b, i, par):
                dve.wait_ge(ev[name + "_acted"], b + 1)
                if name == "peer":
                    dve.wait_ge(ev[f"gates_in{par}"], 16 * i + 16)
                    hid = HID.rearrange("p (j q t) -> p j q t", j=4, q=4)
                    g = GBK[par].rearrange("p q j t -> p j q t")
                    for j in range(4):
                        ins = v.tensor_tensor(hid[:, j], hid[:, j], g[:, j], ALU.mult)
                else:
                    ins = v.tensor_tensor(HID, HID, HID, ALU.mult)
                ins.then_inc(gated, 1)

            def hidden_low(b, par):
                dve.wait_ge(ev[name + "_high"], b + 1)
                v.tensor_tensor(AL[par][:, :], HID, AH[par][:, :].bitcast(F32), ALU.subtract).then_inc(ev[name + "_ready"], 1)

            def add(nb, done, before):
                dve.wait_ge(used, done)
                if nb == 0:
                    dve.wait_ge(ev["dve_free"], before)
                cols = slice(BLK * nb, BLK * (nb + 1))
                v.tensor_tensor(X[:, :, cols], X[:, :, cols], PP[:, (UNIT0[name] + nb) % 2],
                                ALU.add).then_inc(ev["dve_free"], 1)

            def block(n, b, i, par, before, first=False):
                if not first:
                    add(2, n - 1, None)
                low(n, 0)
                if not first:
                    add(3, n, None)
                low(n + 1, 1)
                low(n + 2, 2)
                low(n + 3, 3)
                low(n + 4, 0)
                low(n + 5, 1)
                gate(b, i, par)
                add(0, n + 5, before)
                low(n + 6, 2)
                hidden_low(b, par)
                add(1, n + 6, None)
                low(n + 7, 3)

            d0 = DVE0[name]
            if name != "peer":
                low(base + 2, 2)
                low(base + 3, 3)
            gate(0, 0, 0)
            hidden_low(0, 0)
            block(base + 4, 1, 0, 1, d0, first=True)
            with dve.Fori(0, blocks // 2 - 1, 1) as i:
                for par in range(2):
                    block(16 * i + (base + 12 + 8 * par), 2 * i + (2 + par), i + 1, par,
                          8 * i + (d0 + 4 + 4 * par))
            n = base + 8 * blocks - 4
            low(n, 0)
            add(2, n - 1, None)
            low(n + 1, 1)
            add(3, n, None)
            add(0, n + 1, d0 + 4 * (blocks - 1))
            low(n + 2, 2)
            add(1, n + 2, None)
            low(n + 3, 3)
            add(2, n + 3, None)
            add(3, n + 4, None)
            dve.wait_ge(ev["dve_free"], d0 + 4 * blocks)
            o.n[id(ev["dve_free"])] = d0 + 4 * blocks

        def inverse_dve(dve, o, v, c, A, At, Ti, Tt, ready):
            for q in range(4):
                ready(q)
                m = slice(4 * q, 4 * q + 4)
                v.tensor_tensor(Ti[:, m, :], A[:, m, :], rep(LV[0], 4), ALU.mult)
                o.done(v.tensor_tensor(Tt[:, m, :], At[:, m, :], rep(LV[0], 4), ALU.mult))
                v.tensor_tensor(Ti[:, m, :], rep(ID, 4), Ti[:, m, :], ALU.subtract)
                v.tensor_tensor(Tt[:, m, :], rep(ID, 4), Tt[:, m, :], ALU.subtract).then_inc(ev["inv_new"], 1)
            dve.wait_ge(ev["inv_new"], 28 * c + 4)
            with dve.Fori(1, 7, 1) as l:
                def update(q):
                    dve.wait_ge(ev["inv_t"], 4 * l + (24 * c - 4 + q) + 3)
                    m = slice(4 * q, 4 * q + 4)
                    v.tensor_tensor(Ti[:, m, :], Ti[:, m, :], PQ[:, 2 + q % 2, :].rearrange("p (m j) -> p m j", m=4),
                                    ALU.subtract)
                    v.tensor_tensor(Tt[:, m, :], Tt[:, m, :], PP[:, q % 2, 0, :].rearrange("p (m j) -> p m j", m=4),
                                    ALU.subtract).then_inc(ev["inv_new"], 1)
                for q in range(4):
                    update(q)
            dve.wait_ge(ev["inv_new"], 28 * (c + 1))

        def stage2_dve(dve, o, v, half, freed, turn_out, turn_out_y, scale_rows, add_pair, low, lows):
            lows("dn", 0, (0, 1))
            dve.wait_ge(ev["norm_root"], 3)
            o.done(v.reciprocal(RSTD, RS))
            dve.wait_ge(ev["fnw_in"], 16)
            for t in range(NT):
                o.tell(v.scalar_tensor_tensor(X[:, t, :], X[:, t, :], RSTD[:, t:t + 1], FNW, ALU.mult, ALU.mult),
                       ev["block1_out"])
            dve.wait_ge(ev["block1_out"], 2)
            scale_rows(3, X)
            dve.wait_ge(ev["consts2"], 16)
            turn_out(3, col2("mix2", 0, 16))
            o.done(v.memset(CIN[:, :, 0:3], 0.0), ev["cin_pad"])
            units = [("dn", j) for j in range(8)] + [("small", 0)] + [("rw", j) for j in range(6)]

            def conv(j, tap):
                c = 4 * (j % 2)
                if tap == 0:
                    dve.wait_ge(ev["dve_free"], DVE0["dn"] + j + 1)
                    dve.wait_ge(ev["act_free"], ACT0["dn"] + j + 1)
                for n in range(4):
                    w = col2("dcw", 4 * (4 * j + n) + tap)
                    if tap == 0:
                        ins = v.tensor_scalar(QKV[:, 4 * j + n, :], CIN[:, c + n, 0:T], w, None, ALU.mult)
                    else:
                        ins = v.scalar_tensor_tensor(QKV[:, 4 * j + n, :], CIN[:, c + n, tap:tap + T], w,
                                                     QKV[:, 4 * j + n, :], ALU.mult, ALU.add)
                o.done(ins, ev["dn_conv"] if tap == 3 else None)

            lows("dn", 0, (2, 3))
            for u, (name, j) in enumerate(units):
                convolves = name == "dn" and j < 6
                after = units[u + 1] if u + 1 < len(units) else None
                w = 4 * 272 if after and after[0] == "small" else 2048
                for s in range(2):
                    if after:
                        lows(*after, (s,), w)
                    if name == "dn" and 1 <= j < 7:
                        conv(j - 1, 2 + s)
                ps = half(name, j)
                if name == "rw":
                    dst = RAWS[j // 3][:, j % 3, 0:2, 1:1 + T]
                    freed(v.tensor_copy(dst, ps.rearrange("p (n t) -> p n t", n=2)))
                elif name == "small":
                    freed(v.tensor_copy(flat(GB), ps[:, 0:32]))
                elif convolves:
                    c = 4 * (j % 2)
                    freed(v.tensor_copy(CIN[:, c:c + 2, 3:3 + T], ps.rearrange("p (n t) -> p n t", n=2)))
                else:
                    freed(v.tensor_copy(ZT[:, 0, BLK * (j - 6):BLK * (j - 5)], ps))
                for s in range(2):
                    if after:
                        lows(*after, (2 + s,), w)
                    if convolves:
                        conv(j, s)
            dve.wait_ge(ev["dve_free"], DVE0["out2"])
            o.done(v.tensor_tensor(DST[:, 0], GB[:, :, 0:8], rep(ROW[:, 24:32], NT), ALU.add))
            o.done(v.scalar_tensor_tensor(DST[:, 1], DST[:, 0], -1.0, DST[:, 0], ALU.mult, ALU.max), ev["g_abs"])
            o.done(v.tensor_scalar(DST[:, 2], DST[:, 0], 0.0, None, ALU.max))
            dve.wait_ge(*nth("l2_root", 1))
            o.done(v.reciprocal(L2[0:16, :], L2[0:16, :]), ev["l2_inv"])
            for n, ps in enumerate((PQ, PP)):
                dve.wait_ge(*nth("l2_mm", 2 + n))
                ps = ps[:, :, :].rearrange("p a b -> p (a b)") if n == 0 else ps[:, :, :, :].rearrange("p a b c -> p (a b c)")
                x = flat(QKV[:, 8 * n:8 * n + 8, :])
                if n == 0:
                    v.scalar_tensor_tensor(x, x, QK_SCALE, ps, ALU.mult, ALU.mult)
                else:
                    o.done(v.tensor_tensor(x, x, ps, ALU.mult), ev["dn_qk"])
            dve.wait_ge(*nth("g_act", 1))
            o.done(v.tensor_tensor(DST[:, 2], DST[:, 2], DST[:, 1], ALU.add))
            o.done(v.scalar_tensor_tensor(DST[:, 3], DST[:, 2], -1.0, rep(DST[:, 5, 0, :], NT), ALU.mult, ALU.mult), ev["g_ready"])
            dve.wait_ge(*nth("gc_mm", 1))
            o.done(v.tensor_copy(DST[:, 6:8].rearrange("p a t h -> p (a t h)"), PQ[:, 0, 0:32]))
            o.done(v.tensor_tensor(DST[:, 9], DST[:, 7], DST[:, 6], ALU.subtract), ev["gc_out"])
            o.done(v.tensor_scalar(DST[:, 11], DST[:, 6], -1.0, None, ALU.mult))
            dve.wait_ge(ev["masks"], 19)
            o.done(v.tensor_tensor(DGD, rep(ID, 16), bc(DST[:, 11].rearrange("p t h -> p (t h)"), P), ALU.mult), ev["dn_diag"])
            for m in range(16):
                if m % 4 == 0:
                    dve.wait_ge(*nth("dec_mm", m // 4 + 1))
                t, h = m // 8, m % 8
                ins = v.scalar_tensor_tensor(DEC[:, t, h, :], PQ[:, m // 4, (m % 4) * P:(m % 4 + 1) * P],
                                             DST[:, 6, t, h:h + 1], TRI[:, P:2 * P], ALU.add, ALU.add)
            o.done(ins, ev["dec_arg"])
            dve.wait_ge(*nth("gc_exp", 1))
            o.done(v.tensor_scalar(DST[:, 10], DST[:, 8], -1.0, None, ALU.mult))
            dve.wait_ge(*nth("dec_out", 1))
            for m in range(16):
                if m % 4 == 0:
                    dve.wait_ge(*nth("kk_gram", m // 4 + 1))
                t, h = m // 8, m % 8
                ins = v.scalar_tensor_tensor(AM[:, m, :], PP[:, m // 8, (m // 4) % 2, (m % 4) * P:(m % 4 + 1) * P],
                                             DST[:, 4, t, h:h + 1], DEC[:, t, h, :], ALU.mult, ALU.mult)
            o.done(ins)
            o.done(v.tensor_tensor(AM, AM, rep(LS, 16), ALU.mult), ev["a_ready"])
            for n in range(4):
                dve.wait_ge(*nth("qk_gram", n + 1))
                o.tell(v.tensor_tensor(flat(TTI)[:, BLK * n:BLK * (n + 1)], PQ[:, n, :],
                                       DEC.rearrange("p t h s -> p (t h s)")[:, BLK * n:BLK * (n + 1)], ALU.mult), ev["qd_ready"])
            dve.wait_ge(*nth("kd_turned", 1))
            for n in range(2):
                ins = v.tensor_tensor(KD[:, 4 * n:4 * n + 4, :], PQ[:, n, :].rearrange("p (h d) -> p h d", h=4),
                                      bc(DST[:, 9, 0, 4 * n:4 * n + 4], P), ALU.mult)
            o.done(ins, ev["kd_ready"])
            dve.wait_ge(*nth("at_out", 4))
            dve.wait_ge(*nth("atn_out", 4))
            inverse_dve(dve, o, v, 0, AM, AT_, TI, TTI, lambda q: None)
            dve.wait_ge(*nth("v_tok", 4))
            o.done(v.tensor_tensor(RH, VT[:, 0], bc(DST[:, 4, 0, :], P), ALU.mult), ev["dn_rhs"])
            dve.wait_ge(ev["vn_mm"], 1)
            o.done(v.tensor_copy(flat(VN), PQ[:, 0:2, :].rearrange("p a b -> p (a b)")), ev["vn_out"])
            dve.wait_ge(ev["o_mm"], 1)
            o.tell(v.tensor_copy(OD[:, 0, :], PQ[:, 2:4, :].rearrange("p a b -> p (a b)")), ev["o_out"])
            dve.wait_ge(ev["s_mm"], 1)
            o.done(v.tensor_copy(flat(SD), PQ[:, 0:2, :].rearrange("p a b -> p (a b)")), ev["s_out"])
            dve.wait_ge(ev["ks_mm"], 1)
            for h in range(DH):
                ins = v.scalar_tensor_tensor(RH[:, h, :], PQ[:, 2 + h // 4, (h % 4) * P:(h % 4 + 1) * P], DST[:, 10, 1, h:h + 1],
                                             VT[:, 1, h, :], ALU.mult, ALU.add)
            o.done(ins)
            o.done(v.tensor_tensor(RH, RH, bc(DST[:, 4, 1, :], P), ALU.mult), ev["dn_rhs"])
            dve.wait_ge(ev["vn_mm"], 2)
            o.done(v.tensor_copy(flat(VN), PQ[:, 0:2, :].rearrange("p a b -> p (a b)")), ev["vn_out"])
            dve.wait_ge(ev["o_mm"], 2)
            dve.wait_ge(*nth("qs_out", 8))
            o.done(v.tensor_tensor(OD[:, 1, :], PQ[:, 2:4, :].rearrange("p a b -> p (a b)"), flat(OTM), ALU.add))
            dve.wait_ge(ev["o_out"], 1)
            o.tell(v.nop(), ev["od_ready"])
            dve.wait_ge(*nth("od_sq", 1))
            o.done(v.tensor_reduce(DST[:, 0], VT, AX.X, ALU.add), ev["od_sum"])
            dve.wait_ge(*nth("od_root", 1))
            o.done(v.reciprocal(DST[:, 0], DST[:, 1]))
            dve.wait_ge(*nth("z_silu", 1))
            for t in range(NT):
                odt = OD[:, t, :].rearrange("p (h d) -> p h d", h=DH)
                o.done(v.tensor_tensor(odt, odt, bc(DST[:, 0, t, :], P), ALU.mult))
                o.tell(v.tensor_tensor(OD[:, t, :], OD[:, t, :], ZT[:, t, :], ALU.mult), ev["tp_scaled"])
            turn_out_y(YT, col2("dnw"))
            o.tell(v.nop(), ev["dn_done"])
            for hf in range(2):
                rw_dve(dve, o, v, hf, half, freed)
            dve.wait_ge(ev["yt_high"], 1)
            o.done(v.tensor_tensor(XTL_[:, :], flat(YT), XTH_[:, :].bitcast(F32), ALU.subtract), ev["yt_low"])
            lows("out2", 0, range(4))
            for j in range(4):
                if j < 3:
                    lows("out2", j + 1, (0, 1))
                add_pair("out2", j)
                if j < 3:
                    lows("out2", j + 1, (2, 3))
            lows("xk", 0, (0, 1))
            scale_rows(4, MEMX, MEMX)
            turn_out(5, col2("mem", 0, 16))
            lows("xk", 0, (2, 3))
            lows("xv", 0, (0, 1))
            freed(v.tensor_copy(flat(XK[:, 0:2, :]), half("xk", 0)))
            lows("xv", 0, (2, 3))
            freed(v.tensor_copy(XV[:, 0, :], half("xv", 0)))
            dve.wait_ge(used, SLOT0["xq"])
            lows("xq", 0, (0, 1))
            scale_rows(5, X)
            turn_out(6, col2("xa", 0, 16))
            lows("xq", 0, (2, 3))
            freed(v.tensor_copy(flat(XQ[:, 0:2, :]), half("xq", 0)))
            dve.wait_ge(*nth("xa_mm", 1))
            o.done(v.tensor_reduce(XST[:, 0, :].rearrange("p (h t) -> p h t", t=NT), PQ[:, :, :].rearrange("p h (t m) -> p h t m", t=NT), AX.X, ALU.max))
            o.done(v.tensor_scalar(XST[:, 0, :], XST[:, 0, :], -QK_SCALE, None, ALU.mult), ev["xa_max"])
            dve.wait_ge(*nth("xa_exp", 1))
            o.done(v.reciprocal(XST[:, 2, :], XST[:, 1, :]))
            o.done(v.tensor_tensor(XP.rearrange("p h t m -> p (h t) m"), XP.rearrange("p h t m -> p (h t) m"), bc(XST[:, 2, :], T), ALU.mult), ev["xa_p"])
            dve.wait_ge(*nth("xo_high", 1))
            o.tell(v.tensor_tensor(AL[0][:, :], HID, AH[0][:, :].bitcast(F32), ALU.subtract), ev["xo_low"])
            lows("xo", 0, (0, 1))
            for nb in range(4):
                if nb >= 1 and nb < 3:
                    lows("xo", 0, (nb + 1,))
                dve.wait_ge(used, SLOT0["xo"] + nb + 1)
                cols = slice(BLK * nb, BLK * (nb + 1))
                freed(v.tensor_tensor(X[:, :, cols], X[:, :, cols], PP[:, (UNIT0["xo"] + nb) % 2], ALU.add))
            dve.wait_ge(ev["dve_free"], DVE0["ffn"])
            lows("ffn", 0, (0, 1))
            scale_rows(6, X)
            turn_out(7, col2("ffn", 0, 16))
            two_dve(dve, o, v, "ffn", FB, low)
            dve.wait_ge(ev["norm_root"], 8)
            o.done(v.reciprocal(RSTD, RS))
            dve.wait_ge(ev["fnw_in"], 32)
            for t in range(NT):
                o.tell(v.scalar_tensor_tensor(X[:, t, :], X[:, t, :], RSTD[:, t:t + 1], FNW, ALU.mult, ALU.mult), ev["final"])

        def rw_dve(dve, o, v, hf, half, freed):
            def mu(x, c, w):
                return v.scalar_tensor_tensor(x[0], x[1], c, x[2], ALU.mult, ALU.add)
            RAW = RAWS[hf]
            o.done(v.memset(RAW[:, :, :, 0:1], 0.0))
            dve.wait_ge(ev["act_free"], ACT0["out2"])
            for w in range(3):
                o.done(v.tensor_tensor(E1, RAW[:, w, :, 0:T], RAW[:, w, :, 1:1 + T], ALU.subtract))
                for j in range(J):
                    ins = v.scalar_tensor_tensor(RKV[:, w, j, :], E1[:, j, :], col2(("mur", "muk", "muv")[w], J * hf + j),
                                                 RAW[:, w, j, 1:1 + T], ALU.mult, ALU.add)
                o.done(ins)
            R, K, V = (RKV[:, w] for w in range(3))
            if hf == 0:
                for x, c in ((LW, "muw"), (LG, "mug")):
                    o.done(v.tensor_tensor(E1[:, 0, :], x[:, 0:T], x[:, 1:1 + T], ALU.subtract))
                    o.done(v.scalar_tensor_tensor(E1[:, 1, :], E1[:, 0, :], col2(c), x[:, 1:1 + T], ALU.mult, ALU.add))
                    o.done(v.tensor_copy(x[:, 0:T], E1[:, 1, :]))
                o.tell(v.nop(), ev["lw_shift"])
            dve.wait_ge(ev["lora_out"], 3 * hf + 2)
            o.done(v.tensor_scalar(flat(LDX), flat(LDX), -DECAY, None, ALU.mult))
            for j in range(J):
                for t in range(NT):
                    ins = v.tensor_tensor_scan(CUM[:, j, t * P:(t + 1) * P], ONES, LDX[:, j, t * P:(t + 1) * P], 0.0,
                                               ALU.mult, ALU.add)
            o.done(ins)
            o.done(v.tensor_tensor(LDX, CUM, LDX, ALU.subtract))
            for j in range(J):
                ins = v.tensor_scalar(KKN[:, j, :], K[:, j, :], col2("kk", J * hf + j), None, ALU.mult)
            o.done(ins)
            o.done(v.tensor_tensor(E1, KKN, KKN, ALU.mult), ev["kk_sq"])
            dve.wait_ge(ev["kk_root"], hf + 1)
            o.done(v.tensor_scalar(flat(E1), flat(E1), 1e-12, None, ALU.max))
            o.done(v.reciprocal(flat(E1), flat(E1)))
            o.done(v.tensor_tensor(KKN, KKN, E1, ALU.mult))
            for j in range(J):
                ins = v.tensor_scalar(E1[:, j, :], AA[:, j, :], 1.0, col2("ka", J * hf + j), ALU.subtract, ALU.mult)
            o.done(ins)
            o.done(v.scalar_tensor_tensor(flat(K), flat(E1), 1.0, flat(K), ALU.add, ALU.mult))
            o.done(v.tensor_tensor(AA, AA, KKN, ALU.mult))
            for j in range(J):
                ins = v.scalar_tensor_tensor(E1[:, j, :], R[:, j, :], col2("rk", J * hf + j), K[:, j, :], ALU.mult, ALU.mult)
            o.done(ins, ev["rk_ready"])
            dve.wait_ge(ev["bonus_mm"], hf + 1)
            o.done(v.tensor_tensor(flat(BON), PQ[:, 2:4, :].rearrange("p a b -> p (a b)"), flat(V), ALU.mult))
            blocks = lambda x: x.rearrange("p j (b s) -> p (j b) s", s=64)
            tiles = lambda x: x.rearrange("p j (t s) -> p (j t) s", s=P)
            mid = blocks(CUM)[:, :, 31:32].broadcast_to([P, 16, 64])
            edge = tiles(CUM)[:, :, 63:64].broadcast_to([P, 8, 64])
            end = CUM[:, :, P - 1:P].broadcast_to([P, J, P])
            e1b = flat(E1).rearrange("p (b s) -> p b s", s=64)
            lo, hi = (lambda x: tiles(x)[:, :, 0:64]), (lambda x: tiles(x)[:, :, 64:P])
            half_of = lambda x, n: flat(x)[:, 512 * (n % 2):512 * (n % 2 + 1)]
            h = lambda x, n: half_of(x, n).rearrange("p (b s) -> p b s", s=64)
            w = lambda x, n: half_of(x, n).rearrange("p (j s) -> p j s", s=P)
            osl = lambda x: x.rearrange("p j t s -> p (j t) s")
            t0, t1 = (lambda x: x[:, :, 0:P]), (lambda x: x[:, :, P:T])
            sub = lambda out, x, y: v.tensor_tensor(out, x, y, ALU.subtract)
            mul = lambda out, x, y: v.tensor_tensor(out, x, y, ALU.mult)
            tasks = [
                (lambda: sub(e1b, blocks(CUM), mid), [lambda: mul(KRD[:, :, 1, :], R, E2)]),
                (lambda: None, [lambda: mul(BKD[:, 0], AA, E2), lambda: mul(BKD[:, 1], K, E2)]),
                (lambda: sub(e1b, blocks(LDX), mid), [lambda: mul(KRD[:, :, 0, :], KKN, E2)]),
                (lambda: sub(h(E1, 0), hi(CUM), edge), [lambda j=j: mul(KRO[:, j, 1], h(E2, 0)[:, 2 * j:2 * j + 2, :], hi(R)[:, 2 * j:2 * j + 2, :]) for j in range(J)]),
                (lambda: sub(h(E1, 1), hi(LDX), edge), [lambda j=j: mul(KRO[:, j, 0], h(E2, 1)[:, 2 * j:2 * j + 2, :], hi(KKN)[:, 2 * j:2 * j + 2, :]) for j in range(J)]),
                (lambda: sub(h(E1, 0), edge, lo(CUM)), [lambda: mul(osl(BKO[:, 0]), lo(AA), h(E2, 0)), lambda: mul(osl(BKO[:, 1]), lo(K), h(E2, 0))]),
                (lambda: v.tensor_copy(w(E1, 1), t1(CUM)), [lambda: mul(KRS[:, 1], t1(R), w(E2, 1))]),
                (lambda: v.tensor_copy(w(E1, 0), t1(LDX)), [lambda: mul(KRS[:, 0], t1(KKN), w(E2, 0))]),
                (lambda: sub(w(E1, 1), end, t0(CUM)), [lambda: mul(BKS[:, 0], t0(AA), w(E2, 1)), lambda: mul(BKS[:, 1], t0(K), w(E2, 1))]),
            ]
            for n, (arg, uses) in enumerate(tasks):
                if n < 4:
                    o.done(arg() or v.nop(), ev["decay_arg"])
                if 3 <= n < 8:
                    o.tell(tasks[n + 1][0](), ev["decay_arg"])
                dve.wait_ge(ev["decay_exp"], 9 * hf + n + 1)
                for use in uses:
                    ins = use()
                o.done(ins)
            o.tell(v.nop(), ev["decayed"])
            dve.wait_ge(ev["rv_tok"], 2 * hf + 2)
            for m in range(16):
                dve.wait_ge(ev["gram_mm"], 16 * hf + m + 1)
                o.done(v.tensor_tensor(flat(GR[:, m]), PQ[:, m % 4, :], flat(M4), ALU.mult), ev["gram_diag"])
            def ram(n):
                dve.wait_ge(ev["ram_turned"], 4 * hf + n + 1)
                o.done(v.tensor_copy(flat(RAM)[:, BLK * n:BLK * (n + 1)], PQ[:, n, :]))

            dve.wait_ge(ev["gram_out"], 16 * hf + 16)
            inverse_dve(dve, o, v, 1 + hf, RAM, GR[:, :, 0, :], RTI, RTT, ram)
            n = 2 * hf
            for t in range(NT):
                dve.wait_ge(ev["rx_mm"], n + t + 1)
                o.done(v.tensor_scalar(RX, PQ[:, 0, :], -1.0, None, ALU.mult), ev["rx_out"])
                dve.wait_ge(ev["sa_mm"], n + t + 1)
                o.done(v.tensor_copy(SAB, PQ[:, 1, :]), ev["sa_out"])
                dve.wait_ge(ev["ry_mm"], n + t + 1)
                o.done(v.tensor_copy(RY[:, t, :], PQ[:, 2, :]), ev["ry_out"])
                if t == 0:
                    dve.wait_ge(ev["rs_mm"], hf + 1)
                    o.done(v.tensor_tensor(S1, PQ[:, 3, :].rearrange("p (j s) -> p j s", j=J), rep(BD[6], J), ALU.mult),
                           ev["rs_out"])
            y3 = flat(RY).rearrange("p (m d) -> p m d", d=64)
            y23 = flat(RY2).rearrange("p (m d) -> p m d", d=64)
            o.done(v.tensor_reduce(RST[:, 0, :], y3, AX.X, ALU.add))
            o.done(v.tensor_scalar(RST[:, 0, :], RST[:, 0, :], 1.0 / 64, None, ALU.mult))
            o.done(v.tensor_tensor(y3, y3, bc(RST[:, 0, :], 64), ALU.subtract), ev["gn_mean"])
            dve.wait_ge(ev["gn_sq"], hf + 1)
            o.done(v.tensor_reduce(RST[:, 0, :], y23, AX.X, ALU.add), ev["gn_sum"])
            dve.wait_ge(ev["gn_root"], hf + 1)
            o.done(v.reciprocal(RST[:, 2, :], RST[:, 1, :]))
            o.done(v.tensor_tensor(y3, y3, bc(RST[:, 2, :], 64), ALU.mult), ev["gn_out"])
            y0 = DH + J * hf
            for t in range(NT):
                dve.wait_ge(ev["ry_turned"], 2 * hf + t + 1)
                for j in range(J):
                    ins = v.tensor_scalar(YT[:, y0 + j, t * P:(t + 1) * P], PP[:, t, 0, j * P:(j + 1) * P],
                                          col2("lnw", J * hf + j), col2("lnb", J * hf + j), ALU.mult, ALU.add)
            o.done(ins)
            yt = flat(YT[:, y0:y0 + J, :])
            o.done(v.tensor_tensor(yt, yt, flat(BON), ALU.add))
            o.done(v.tensor_tensor(yt, yt, flat(GATE), ALU.mult), ev["rw_done"])

        @block.vector
        def _(dve):
            o = Own(dve, ev["dve_order"])
            v = nc.vector

            def half(name, j):
                dve.wait_ge(used, SLOT0[name] + 4 * (j + 1))
                return PP[:, (UNIT0[name] + j) % 2, 0, :]

            def freed(ins):
                o.tell(ins, ev["dve_free"])

            def low(n, s, w=2048):
                dve.wait_ge(ev["split_high"], n + 1)
                v.tensor_tensor(WL[s % 2][:, 0:w], flat(ring[s])[:, 0:w], WH[s % 2][:, 0:w].bitcast(F32),
                                ALU.subtract).then_inc(ev["split_low"], 1)

            def lows(name, j, slots, w=2048):
                for s in slots:
                    low(SLOT0[name] + 4 * j + s, s, w)

            def turn_out(i, weights):
                first = turn_out.rows
                for n in range(first, first + 9):
                    if n < first + 8:
                        t, g = (n % 8) // 4, n % 4
                        dve.wait_ge(ev["turned"], turn_out.n + 1)
                        turn_out.n += 1
                        ps = PQ[:, g, :].rearrange("p (n t) -> p n t", n=4)
                        o.tell(v.tensor_tensor(XTS[:, n % 2, :].rearrange("p (n t) -> p n t", n=4), ps,
                                               bc(weights[:, 4 * g:4 * g + 4], P), ALU.mult), ev["rows_out"])
                    if n > first:
                        m = n - 1
                        t, g = (m % 8) // 4, m % 4
                        dve.wait_ge(ev["rows_high"], m + 1)
                        tile = (slice(None), slice(4 * g, 4 * g + 4), slice(t * P, (t + 1) * P))
                        o.done(v.tensor_tensor(XTL[tile], XTS[:, m % 2, :].rearrange("p (n t) -> p n t", n=4),
                                               XTH[tile].bitcast(F32), ALU.subtract), ev["rows_low"])
                turn_out.rows += 8

            def turn_out_y(dst, weight):
                for t in range(NT):
                    for g in range(2):
                        dve.wait_ge(ev["turned"], turn_out.n + 1)
                        turn_out.n += 1
                        o.tell(v.tensor_tensor(dst[:, 4 * g:4 * g + 4, t * P:(t + 1) * P],
                                               PQ[:, g, :].rearrange("p (n t) -> p n t", n=4),
                                               bc(weight.broadcast_to([P, 4]), P), ALU.mult), ev["y_out"])
            turn_out.n = turn_out.rows = 0

            def scale_rows(i, src, dst=SCN):
                dve.wait_ge(ev["norm_root"], i + 1)
                o.done(v.reciprocal(RSTD, RS))
                for t in range(NT):
                    o.tell(v.tensor_scalar(dst[:, t, :], src[:, t, :], RSTD[:, t:t + 1], None, ALU.mult),
                           ev["tp_scaled"])

            def add_pair(name, j):
                dve.wait_ge(used, SLOT0[name] + 4 * (j + 1))
                cols = slice(BLK * j, BLK * (j + 1))
                freed(v.tensor_tensor(X[:, :, cols], X[:, :, cols], PP[:, (UNIT0[name] + j) % 2], ALU.add))

            for _ in range(2):
                dve.nop().then_inc(ev["dve_free"], 1)
                o.n[id(ev["dve_free"])] = o.n.get(id(ev["dve_free"]), 0) + 1
            v.memset(EPSC, EPS).then_inc(ev["dve_init"], 1)
            v.memset(RWEPSC, RW_EPS).then_inc(ev["dve_init"], 1)
            scale_rows(0, X)
            dve.wait_ge(ev["consts1"], 48)
            dve.wait_ge(ev["wg_high"], 1)
            v.tensor_tensor(WGL[:, :], flat(WG), WGH[:, :].bitcast(F32), ALU.subtract).then_inc(ev["wg_low"], 1)
            turn_out(0, col1("norm1", 0, 16))
            lows("win", 0, (0, 1))
            dve.wait_ge(*nth("gate_mm", 1))
            o.done(v.tensor_tensor(GT, PQ[:, 0, 0:32].rearrange("p (t g) -> p t g", t=2), rep(ROW[:, 0:16], NT), ALU.add))
            o.done(v.scalar_tensor_tensor(TM[:, 0:2, :], GT, -1.0, GT, ALU.mult, ALU.max), ev["gate_abs"])
            o.done(v.tensor_scalar(TM[:, 2:4, :], GT, 0.0, None, ALU.min))
            dve.wait_ge(*nth("gate_ln", 1))
            o.done(v.tensor_tensor(LF, TM[:, 2:4, :], TM[:, 0:2, :], ALU.subtract), ev["log_f"])
            lows("win", 0, (2, 3))
            for j in range(12):
                if j < 11:
                    lows("win", j + 1, (0, 1))
                ps = half("win", j)
                if j < 2:
                    freed(v.tensor_copy(MQK[:, 4 * j:4 * j + 2, 3:3 + T], ps.rearrange("p (n t) -> p n t", n=2)))
                elif j < 4:
                    freed(v.tensor_scalar(flat(FQ[:, 4 * (j - 2):4 * (j - 2) + 2, :]), ps, QK_SCALE, None, ALU.mult))
                elif j < 6:
                    freed(v.tensor_copy(flat(FK[:, 4 * (j - 4):4 * (j - 4) + 2, :]), ps))
                elif j < 8:
                    freed(v.tensor_copy(FV[:, 0, BLK * (j - 6):BLK * (j - 5)], ps))
                elif j < 10:
                    freed(v.tensor_copy(MV1[:, 0, 2 * (j - 8):2 * (j - 8) + 2, 0:MV], ps.rearrange("p (h v) -> p h v", h=2)))
                else:
                    ins = v.tensor_copy(MO[:, 0, BLK * (j - 10):BLK * (j - 9)], ps)
                    freed(ins)
                if j < 11:
                    lows("win", j + 1, (2, 3))
                if j == 1:
                    dve.wait_ge(*nth("cumsum_mm", 1))
                    o.done(v.tensor_copy(flat(CS), PQ[:, 1, 0:64]))
                    o.done(v.tensor_copy(FCOL[:, 0, :], CS[:, 0, 0:FH]))
                    o.done(v.tensor_tensor(FCOL[:, 1, :], CS[:, 1, 0:FH], CS[:, 2, 0:FH], ALU.add))
                    o.done(v.tensor_scalar(NFCOL, FCOL, -1.0, None, ALU.mult))
                    dve.wait_ge(ev["masks"], 3)
                    o.tell(v.tensor_tensor(DG, rep(ID, 16).rearrange("p (h t) s -> p h t s", t=2),
                                           bc(NFCOL.rearrange("p t h -> p h t"), P), ALU.mult), ev["fox_diag"])
                if j == 2:
                    dve.wait_ge(ev["act_free"], 4)
                    dve.wait_ge(ev["dve_free"], 4)
                    for n in range(8):
                        o.tell(v.tensor_scalar(MQC[:, n, :], MQK[:, n, 0:T], col1("cw", 4 * n), col1("cb", n),
                                               ALU.mult, ALU.add), o.order)
                    dve.wait_ge(o.order, o.n[id(o.order)])
                    for tap in range(1, 4):
                        for n in range(8):
                            ins = v.scalar_tensor_tensor(MQC[:, n, :], MQK[:, n, tap:tap + T], col1("cw", 4 * n + tap),
                                                         MQC[:, n, :], ALU.mult, ALU.add)
                            o.tell(ins, o.order)
                        dve.wait_ge(o.order, o.n[id(o.order)])
                    o.tell(v.nop(), ev["conv_out"])
            dve.wait_ge(ev["dve_free"], 2 + 12)
            o.tell(v.nop(), ev["mo_ready"])
            for h in range(FH + 1):
                if h < FH:
                    b = h % 2
                    dve.wait_ge(ev["fox_scores"], h + 1)
                    if h >= 2:
                        dve.wait_ge(ev["fox_exp"], h - 1)
                    o.tell(v.scalar_tensor_tensor(FS[:, b, 0:P], PQ[:, b, 0:P], FCOL[:, 0, h:h + 1], TRI[:, P:2 * P],
                                                  ALU.add, ALU.add), o.order)
                    o.done(v.scalar_tensor_tensor(FS[:, b, P:384], PQ[:, b, P:384], FCOL[:, 1, h:h + 1], TRI,
                                                  ALU.add, ALU.add))
                    v.tensor_reduce(FST[:, b, 0:1], FS[:, b, 0:P], AX.X, ALU.max, negate=True)
                    o.done(v.tensor_reduce(FST[:, b, 1:2], FS[:, b, P:384], AX.X, ALU.max, negate=True), ev["fox_max"])
                if h >= 1:
                    g, b = h - 1, (h - 1) % 2
                    dve.wait_ge(ev["fox_exp"], g + 1)
                    o.done(v.reciprocal(RM[:, 0, 2 * b:2 * b + 2], FST[:, b, 2:4]))
                    dve.wait_ge(ev["fox_pv"], g + 1)
                    for t in range(NT):
                        ins = v.tensor_scalar(MIX[:, t, g * P:(g + 1) * P], PP[:, b, 0, t * P:(t + 1) * P],
                                              RM[:, 0, 2 * b + t:2 * b + t + 1], None, ALU.mult)
                    o.done(ins, ev["fox_out"])
            mlstm_dve(dve, o, v)
            dve.wait_ge(*nth("mix_sq", 1))
            o.done(v.tensor_reduce(HN[:, 0, 0:16].rearrange("p (t h) -> p t h", t=NT),
                                   SCR[:, :, 0:1024].rearrange("p t (h d) -> p t h d", d=P), AX.X, ALU.add))
            o.done(v.tensor_reduce(HN[:, 0, 16:24].rearrange("p (t h) -> p t h", t=NT),
                                   SCR[:, :, 1024:2048].rearrange("p t (h d) -> p t h d", d=MV), AX.X, ALU.add),
                   ev["mix_sum"])
            dve.wait_ge(*nth("mix_root", 1))
            o.done(v.reciprocal(HN[:, 0, :], HN[:, 1, :]))
            for t in range(NT):
                v.tensor_tensor(SCR[:, t, 0:1024].rearrange("p (h d) -> p h d", d=P),
                                MIX[:, t, 0:1024].rearrange("p (h d) -> p h d", d=P),
                                bc(HN[:, 0, 8 * t:8 * t + 8], P), ALU.mult)
                o.tell(v.tensor_tensor(SCR[:, t, 1024:2048].rearrange("p (h d) -> p h d", d=MV),
                                       MIX[:, t, 1024:2048].rearrange("p (h d) -> p h d", d=MV),
                                       bc(HN[:, 0, 16 + 4 * t:20 + 4 * t], MV), ALU.mult), ev["tp_scaled"])
            turn_out(1, col1("mix", 0, 16))
            lows("wout", 0, range(4))
            for j in range(4):
                if j < 3:
                    lows("wout", j + 1, (0, 1))
                add_pair("wout", j)
                if j < 3:
                    lows("wout", j + 1, (2, 3))
            lows("wq", 0, (0, 1))
            scale_rows(1, X)
            turn_out(2, col1("norm2", 0, 16))
            lows("wq", 0, (2, 3))
            for j in range(4):
                if j < 3:
                    lows("wq", j + 1, (0, 1))
                ps = half("wq", j)
                freed(v.tensor_copy(flat(PQT[:, 4 * j:4 * j + 2, :]), ps))
                if j < 3:
                    lows("wq", j + 1, (2, 3))
            select_dve(dve, o, v, lows)
            with dve.Fori(0, T // 8, 1) as i:
                for b in range(2):
                    dve.wait_ge(ev["rows_used"], 2 * i + b + 1)
                    for t in range(4):
                        ins = v.tensor_scalar(A0[:, b, t, :], IOTA, HK[:, 0, bass.ds(8 * i + (4 * b + t), 1)],
                                              HK[:, 2, bass.ds(8 * i + (4 * b + t), 1)], ALU.is_equal, ALU.mult)
                    v.tensor_tensor(B0[:, b], rep(IOTA, 4), bc(HK[:, 1, bass.ds(8 * i + 4 * b, 4)], P),
                                    ALU.is_equal).then_inc(ev["onehots"], 1)
            two_dve(dve, o, v, "peer", EB, low)
            stage2_dve(dve, o, v, half, freed, turn_out, turn_out_y, scale_rows, add_pair, low, lows)
        def mlstm_pe(pe, mm):
            pe.wait_ge(*nth("m_diag", 1))
            pe.wait_ge(ev["fox_out"], FH)
            for c in range(NT):
                ins = mm(PQ[:, c, :], ONES, flat(DGM[:, c]), start=True, stop=True)
            ins.then_inc(ev["r_mm"], 1)
            pe.wait_ge(*nth("qk_silu", 1))
            for c in range(NT):
                for h in range(MH):
                    ins = mm(PP[:, c, 0, h * P:(h + 1) * P], MQC[:, h, c * P:(c + 1) * P],
                             MQC[:, MH + h, c * P:(c + 1) * P], start=True, stop=True)
                ins.then_inc(ev["qk_mm"], 1)
            for h in range(MH):
                ins = nc.tensor.transpose(PQ[:, 2, h * P:(h + 1) * P], MQC[:, MH + h, 0:P], ID)
            ins.then_inc(ev["k_turned"], 1)
            pe.wait_ge(*nth("r_read", 2))
            for c in range(NT):
                pe.wait_ge(*nth("sm_ready", c + 1))
                for h in range(MH):
                    ins = nc.tensor.transpose(PQ[:, c, h * P:(h + 1) * P], SMM[:, c, h, :], ID)
                ins.then_inc(ev["sm_turned"], 1)
            pe.wait_ge(*nth("ka_ready", 1))
            pe.wait_ge(*nth("smt_out", 2))
            for h in range(MH):
                mm(PQ[:, h, 0:MV + 1], KA[:, h, :], MV1[:, 0, h, :], start=True, stop=True).then_inc(ev["cp_mm"], 1)
            for h in range(MH):
                mm(PP[:, h // 2, h % 2, 0:MV + 1], SMT[:, 0, h, :], MV1[:, 0, h, :], start=True,
                   stop=True).then_inc(ev["num0_mm"], 1)
            for h in range(MH):
                pe.wait_ge(*nth("cp_out", h + 1))
                mm(PQ[:, h, 0:MV + 1], MQC[:, h, P:2 * P], CP[:, h, :], start=True, stop=True).then_inc(ev["inter_mm"], 1)
            for h in range(MH):
                pe.wait_ge(*nth("num0_out", h + 1))
                mm(PP[:, h // 2, h % 2, 0:MV + 1], SMT[:, 1, h, :], MV1[:, 1, h, :], start=True,
                   stop=True).then_inc(ev["num1_mm"], 1)
            pe.wait_ge(*nth("inter_out", MH))
            pe.wait_ge(*nth("mix_ready", 2))

        def passes(mm, out, stat, mov, start, stop):
            mm(out, stat[0], mov[0], start=start, stop=False, skip_group_check=True)
            mm(out, stat[0], mov[1], start=False, stop=False, skip_group_check=True)
            return mm(out, stat[1], mov[0], start=False, stop=stop, skip_group_check=True)

        def weights(s):
            return [w[s % 2][:, :].rearrange("p (k n) -> p k n", k=4) for w in (WH, WL)]

        def second(pe, mm, name, buf, n, d):
            for nb in range(4):
                pe.wait_ge(ev["dve_free"], d + nb)
                pe.wait_ge(ev["split_low"], n + (nb + 1))
                w = weights(nb)
                for t in range(NT):
                    for k in range(4):
                        c = slice(k * T + t * P, k * T + (t + 1) * P)
                        ins = passes(mm, PP[:, (UNIT0[name] + nb) % 2, t, :], [x[:, c] for x in buf],
                                     [x[:, k, :] for x in w], k == 0, k == 3)
                ins.then_inc(used, 1)

        def first_layer(pe, mm, pair, n):
            for s in range(4):
                pe.wait_ge(ev["split_low"], n + (s + 1))
                w = weights(s)
                for k in range(4):
                    kt = 4 * s + k
                    for m in range(4):
                        ins = passes(mm, pair[:, m // 2, (m % 2) * T:(m % 2 + 1) * T],
                                     [x[:, k, m * P:(m + 1) * P] for x in w], [XTH[:, kt, :], XTL[:, kt, :]],
                                     kt == 0 and m % 2 == 0, kt == KT - 1)
                ins.then_inc(used, 1)

        def two_pe(pe, mm, name, blocks):
            base, acted, ready = SLOT0[name], ev[name + "_acted"], ev[name + "_ready"]
            hid = PQ[:, 0:2, :]

            if name == "peer":
                pe.wait_ge(ev["bank_empty"], T // 4 + 2)
            pe.wait_ge(ev["act_free"], ACT0[name])
            pe.wait_ge(ev["dve_free"], DVE0[name])
            if name != "peer":
                first_layer(pe, mm, hid, base)
            with pe.Fori(0, blocks // 2 - 1, 1) as i:
                for par in range(2):
                    pe.wait_ge(acted, 2 * i + (par + 1))
                    first_layer(pe, mm, hid, 16 * i + (base + 4 + 8 * par))
                    pe.wait_ge(ready, 2 * i + (par + 1))
                    second(pe, mm, name, (AH[par], AL[par]), 16 * i + (base + 8 + 8 * par), 8 * i + (DVE0[name] - 1 + 4 * par))
            pe.wait_ge(acted, blocks - 1)
            first_layer(pe, mm, hid, base + 8 * blocks - 12)
            for b in (blocks - 2, blocks - 1):
                pe.wait_ge(ready, b + 1)
                n = base + 8 * blocks - (8 if b == blocks - 2 else 4)
                second(pe, mm, name, (AH[b % 2], AL[b % 2]), n, DVE0[name] - 1 + 4 * b)

        def inverse_pe(pe, mm, c, Ti, Tt):
            if c == 0:
                for _ in range(2):
                    pe.nop().then_inc(ev["inv_m1"], 1)
                    pe.nop().then_inc(ev["inv_t"], 1)
            with pe.Fori(1, 7, 1) as l:
                def first(q):
                    g = 4 * l + (24 * c - 4 + q)
                    pe.wait_ge(ev["inv_off"], g + 1)
                    pe.wait_ge(ev["inv_new"], 4 * l + (28 * c - 4 + q + 1))
                    pe.wait_ge(ev["inv_m1_out"], g + 1)
                    for m in range(4):
                        ins = mm(PQ[:, q % 2, m * P:(m + 1) * P], AOFS[c][:, q, m, :], Ti[:, 4 * q + m, :], start=True, stop=True)
                    ins.then_inc(ev["inv_m1"], 1)

                def then(q):
                    pe.wait_ge(ev["inv_m1_out"], 4 * l + (24 * c - 4 + q) + 3)
                    pe.wait_ge(ev["inv_new"], 4 * l + (28 * c - 4 + q + 3))
                    for m in range(4):
                        mm(PQ[:, 2 + q % 2, m * P:(m + 1) * P], Tt[:, 4 * q + m, :], M1B[:, q % 2, m, :], start=True, stop=True)
                    for m in range(4):
                        ins = mm(PP[:, q % 2, 0, m * P:(m + 1) * P], M1B[:, q % 2, m, :], Tt[:, 4 * q + m, :], start=True, stop=True)
                    ins.then_inc(ev["inv_t"], 1)
                first(0)
                first(1)
                then(0)
                first(2)
                then(1)
                first(3)
                then(2)
                then(3)

        def stage2_pe(pe, mm, product, turn):
            pe.wait_ge(ev["masks"], 19)
            turn()
            product("dn", 0, 6, True)
            product("dn", 6, 2, False)
            pair = PP[:, UNIT0["small"] % 2]
            pe.wait_ge(ev["dve_free"], DVE0["small"] - 1)
            pe.wait_ge(ev["act_free"], ACT0["small"] - 1)
            for s in range(4):
                w = [x[s % 2][:, 0:4 * 272].rearrange("p (k n) -> p k n", k=4) for x in (WH, WL)]
                pe.wait_ge(ev["split_low"], SLOT0["small"] + s + 1)
                for k in range(4):
                    kt = 4 * s + k
                    for t in range(NT):
                        tok = slice(t * P, (t + 1) * P)
                        passes(mm, pair[:, 0, 16 * t:16 * t + 16], [XTH[:, kt, tok], XTL[:, kt, tok]],
                               [x[:, k, 0:16] for x in w], kt == 0 and t == 0, kt == KT - 1)
                    for n in range(2):
                        ins = passes(mm, pair[:, 1, n * T:(n + 1) * T], [x[:, k, 16 + n * P:16 + (n + 1) * P] for x in w],
                                     [XTH[:, kt, :], XTL[:, kt, :]], kt == 0 and n == 0, kt == KT - 1)
                ins.then_inc(used, 1)
            product("rw", 0, 6, True)
            pe.wait_ge(*nth("dn_sq", 1))
            for n in range(16):
                ins = mm(PQ[0:16, 0, 0:T], COL16[:, 15 - n:31 - n], SQD[:, n, :], start=(n == 0), stop=(n == 15))
            ins.then_inc(ev["l2_mm"], 1)
            pe.wait_ge(*nth("l2_inv", 1))
            pe.wait_ge(ev["dve_free"], DVE0["out2"])
            pe.wait_ge(ev["act_free"], ACT0["out2"])
            for n in range(16):
                ps = PQ[:, n // 2, (n % 2) * T:(n % 2 + 1) * T] if n < 8 else PP[:, (n - 8) // 4, (n // 2) % 2, (n % 2) * T:(n % 2 + 1) * T]
                ins = mm(ps, ID[0:16, n:n + 1].broadcast_to([16, P]), L2[0:16, :], start=True, stop=True)
                if n % 8 == 7:
                    ins.then_inc(ev["l2_mm"], 1)
            pe.wait_ge(*nth("g_ready", 1))
            g16 = DST[:, 3].rearrange("p t h -> p (t h)")
            mm(PQ[:, 0, 0:16], UI, g16, start=True, stop=True)
            mm(PQ[:, 0, 16:32], ONES, g16, start=True, stop=True).then_inc(ev["gc_mm"], 1)
            pe.wait_ge(*nth("dn_diag", 1))
            for n in range(4):
                mm(PQ[:, n, :], ONES, flat(DGD)[:, BLK * n:BLK * (n + 1)], start=True, stop=True).then_inc(ev["dec_mm"], 1)
            pe.wait_ge(*nth("dn_qk", 1))
            pe.wait_ge(ev["dve_free"], DVE0["out2"])
            pe.wait_ge(ev["act_free"], ACT0["out2"])
            for dst, q0, e in ((None, 8, "kk_gram"), (PQ, 0, "qk_gram")):
                if dst is PQ:
                    pe.wait_ge(*nth("dec_arg", 1))
                for n in range(4):
                    for i in range(4):
                        m = 4 * n + i
                        t, h = m // 8, m % 8
                        ps = PP[:, n // 2, n % 2, i * P:(i + 1) * P] if dst is None else PQ[:, n, i * P:(i + 1) * P]
                        ins = mm(ps, QKV[:, q0 + h, t * P:(t + 1) * P], QKV[:, 8 + h, t * P:(t + 1) * P], start=True, stop=True)
                    ins.then_inc(ev[e], 1)
            pe.wait_ge(*nth("a_ready", 1))
            for n in range(4):
                pe.wait_ge(*nth("qd_ready", n + 1))
                for i in range(4):
                    ins = nc.tensor.transpose(PP[:, n // 2, n % 2, i * P:(i + 1) * P], TTI[:, 4 * n + i, :], ID)
                ins.then_inc(ev["qd_turned"], 1)
            for n in range(4):
                for i in range(4):
                    ins = nc.tensor.transpose(PQ[:, n, i * P:(i + 1) * P], AM[:, 4 * n + i, :], ID)
                ins.then_inc(ev["a_turned"], 1)
            pe.wait_ge(*nth("dn_silu", 6))
            for n in range(4):
                pe.wait_ge(*nth("atn_out", n + 1))
                for i in range(4):
                    m = 4 * n + i
                    t, h = m // 8, m % 8
                    ins = nc.tensor.transpose(PP[:, n // 2, n % 2, i * P:(i + 1) * P], QKV[:, 16 + h, t * P:(t + 1) * P], ID)
                ins.then_inc(ev["v_turned"], 1)
            pe.wait_ge(*nth("at_out", 4))
            for h in range(DH):
                ins = nc.tensor.transpose(PQ[:, h // 4, (h % 4) * P:(h % 4 + 1) * P], QKV[:, 8 + h, 0:P], ID)
            ins.then_inc(ev["kd_turned"], 1)
            pe.wait_ge(*nth("kd_ready", 1))
            pe.wait_ge(*nth("v_tok", 4))
            inverse_pe(pe, mm, 0, TI, TTI)
            at = lambda b, h: PQ[:, b + h // 4, (h % 4) * P:(h % 4 + 1) * P]
            pe.wait_ge(ev["inv_new"], 28)
            for t in range(NT):
                if t == 1:
                    pe.wait_ge(ev["s_out"], 1)
                    for h in range(DH):
                        ins = mm(at(2, h), QKV[:, 8 + h, P:T], SD[:, h, :], start=True, stop=True)
                    ins.then_inc(ev["ks_mm"], 1)
                    for h in range(DH):
                        ins = mm(PP[:, 0, h // 4, (h % 4) * P:(h % 4 + 1) * P], QKV[:, h, P:T], SD[:, h, :], start=True, stop=True)
                    ins.then_inc(ev["qs_mm"], 1)
                pe.wait_ge(ev["dn_rhs"], t + 1)
                for h in range(DH):
                    ins = mm(at(0, h), TTI[:, DH * t + h, :], RH[:, h, :], start=True, stop=True)
                ins.then_inc(ev["vn_mm"], 1)
                pe.wait_ge(ev["vn_out"], t + 1)
                for h in range(DH):
                    ins = mm(at(2, h), ATN[:, DH * t + h, :], VN[:, h, :], start=True, stop=True)
                ins.then_inc(ev["o_mm"], 1)
                if t == 0:
                    for h in range(DH):
                        ins = mm(at(0, h), KD[:, h, :], VN[:, h, :], start=True, stop=True)
                    ins.then_inc(ev["s_mm"], 1)
                    pe.wait_ge(ev["o_out"], 1)
            turn(8, OD)
            for hf in range(2):
                rw_pe(pe, mm, product, hf)
            pe.wait_ge(ev["yt_low"], 1)
            product("out2", 0, 4, False)
            turn(src=MEMX)
            product("xk", 0, 1, True)
            product("xv", 0, 1, False)
            turn()
            product("xq", 0, 1, True)
            pe.wait_ge(ev["dve_free"], DVE0["xo"])
            pe.wait_ge(ev["act_free"], ACT0["xo"])
            for n in range(8):
                h, t = n // 2, n % 2
                ins = mm(PQ[:, h, t * T:(t + 1) * T], XQ[:, h, t * P:(t + 1) * P], XK[:, h, :], start=True, stop=True)
            ins.then_inc(ev["xa_mm"], 1)
            pe.wait_ge(*nth("xa_p", 1))
            for h in range(4):
                for m in range(NT):
                    for t in range(NT):
                        ins = nc.tensor.transpose(PP[:, h // 2, h % 2, m * T + t * P:m * T + (t + 1) * P], XP[:, h, t, m * P:(m + 1) * P], ID)
                ins.then_inc(ev["xa_turned"], 1)
            for h in range(4):
                pe.wait_ge(*nth("xa_pt", h + 1))
                for m in range(NT):
                    ins = mm(PQ[:, h, 0:T], XV[:, m, h * P:(h + 1) * P], XPT[:, h, m, :], start=(m == 0), stop=(m == 1))
                ins.then_inc(ev["xa_o"], 1)
            pe.wait_ge(ev["xo_low"], 1)
            second(pe, mm, "xo", (AH[0], AL[0]), SLOT0["xo"], DVE0["xo"] - 1)
            turn()
            two_pe(pe, mm, "ffn", FB)

        def rw_pe(pe, mm, product, hf):
            if hf == 1:
                pe.wait_ge(ev["rw_done"], 1)
            if hf == 0:
                pe.wait_ge(ev["lw_act"], 1)
                pe.wait_ge(ev["lw_shift"], 1)
                pe.wait_ge(ev["lora_in"], 48)
                pe.wait_ge(ev["lora_zero"], 1)
            for n, (w, x) in enumerate(((W2, LW), (A2, LW), (G2, LG))):
                if n == 2:
                    pe.wait_ge(ev["lora_out"], 3 * hf + 1)
                for j in range(J):
                    c = J * hf + j
                    ins = mm(PQ[:, 2 * (n % 2) + j // 2, (j % 2) * T:(j % 2 + 1) * T], w[:, c * P:(c + 1) * P], x[:, 0:T],
                             start=True, stop=True)
                ins.then_inc(ev["lora_mm"], 1)
            for e, done in (("kk_sq", "kk_mm"), ("rk_ready", "bonus_mm")):
                pe.wait_ge(ev[e], hf + 1)
                for n in range(2):
                    ins = mm(PQ[:, 2 + n, :], BD[6], flat(E1)[:, BLK * n:BLK * (n + 1)], start=True, stop=True)
                ins.then_inc(ev[done], 1)
            for t in range(NT):
                for j in range(J):
                    ins = nc.tensor.transpose(PP[:, t, 0, j * P:(j + 1) * P], RKV[:, 2, j, t * P:(t + 1) * P], ID)
                ins.then_inc(ev["rv_turned"], 1)
            pe.wait_ge(ev["decayed"], hf + 1)
            for w in range(2):
                for j in range(J):
                    ins = nc.tensor.transpose(PP[:, w, 1, j * P:(j + 1) * P], BKS[:, w, j, :], ID)
                ins.then_inc(ev["bk_turned"], 1)
            pe.wait_ge(ev["rv_tok"], 2 * hf + 2)
            pe.wait_ge(ev["bk_tok"], 2 * hf + 2)
            pe.wait_ge(ev["lora_out"], 3 * hf + 3)
            for m in range(16):
                t, j, e = m // 8, (m % 8) // 2, m % 2
                rows = slice(64 * e, 64 * e + 64)
                if m >= 4:
                    pe.wait_ge(ev["gram_out"], 16 * hf + m - 3)
                for w in range(2):
                    mm(PQ[:, m % 4, w * T:(w + 1) * T], BKD[rows, w, j, t * P:(t + 1) * P],
                       KRD[rows, j, :, t * P:(t + 1) * P], start=True, stop=True)
                    ins = mm(PP[0:64, (m % 4) // 2, m % 2, w * P:(w + 1) * P], BKO[rows, w, j, t, :], KRO[rows, j, :, t, :],
                             start=True, stop=True)
                ins.then_inc(ev["gram_mm"], 1)
            pe.wait_ge(ev["gram_out"], 16 * hf + 16)
            for n in range(4):
                for i in range(4):
                    ins = nc.tensor.transpose(PQ[:, n, i * P:(i + 1) * P], GR[:, 4 * n + i, 0, :], ID)
                ins.then_inc(ev["ram_turned"], 1)
            inverse_pe(pe, mm, 1 + hf, RTI, RTT)
            pe.wait_ge(ev["inv_new"], 28 * (hf + 2))
            for t in range(NT):
                n = 2 * hf + t + 1
                if t == 1:
                    pe.wait_ge(ev["rs_out"], hf + 1)
                    for j in range(J):
                        mm(PQ[:, 0, j * P:(j + 1) * P], KRS[:, 0, j, :], S1[:, j, :], start=(j == 0), stop=False, skip_group_check=True)
                for h in range(HH):
                    c = slice(h * 64, h * 64 + 64)
                    ins = mm(PQ[:, 0, c], GR[:, HH * t + h, 2, :], VTK[:, t, c], start=(t == 0), stop=True, skip_group_check=True)
                ins.then_inc(ev["rx_mm"], 1)
                pe.wait_ge(ev["rx_out"], n)
                for h in range(HH):
                    c = slice(h * 64, h * 64 + 64)
                    ins = mm(PQ[:, 1, c], RTT[:, HH * t + h, :], RX[:, c], start=True, stop=True)
                ins.then_inc(ev["sa_mm"], 1)
                pe.wait_ge(ev["sa_out"], n)
                if t == 1:
                    for j in range(J):
                        mm(PQ[:, 2, j * P:(j + 1) * P], KRS[:, 1, j, :], S1[:, j, :], start=(j == 0), stop=False, skip_group_check=True)
                for h in range(HH):
                    c = slice(h * 64, h * 64 + 64)
                    mm(PQ[:, 2, c], GR[:, HH * t + h, 1, :], SAB[:, c], start=(t == 0), stop=False, skip_group_check=True)
                    ins = mm(PQ[:, 2, c], GR[:, HH * t + h, 3, :], VTK[:, t, c], start=False, stop=True, skip_group_check=True)
                ins.then_inc(ev["ry_mm"], 1)
                if t == 0:
                    for j in range(J):
                        c = slice(j * P, (j + 1) * P)
                        mm(PQ[:, 3, c], BKT[:, 0, c], SAB[:, c], start=True, stop=False)
                        ins = mm(PQ[:, 3, c], BKT[:, 1, c], VTK[:, 0, c], start=False, stop=True)
                    ins.then_inc(ev["rs_mm"], 1)
                    pe.wait_ge(ev["ry_out"], n)
            pe.wait_ge(ev["gn_out"], hf + 1)
            for t in range(NT):
                for j in range(J):
                    ins = nc.tensor.transpose(PP[:, t, 0, j * P:(j + 1) * P], RY[:, t, j * P:(j + 1) * P], ID)
                ins.then_inc(ev["ry_turned"], 1)
            pe.wait_ge(ev["rw_done"], hf + 1)

        @block.tensor
        def _(pe):
            o = Own(pe, ev["pe_order"])
            mm = nc.tensor.matmul

            def group(name, j, pair, feat):
                if feat:
                    first_layer(pe, mm, pair, 4 * j + SLOT0[name])
                    return
                for s in range(4):
                    pe.wait_ge(ev["split_low"], 4 * j + (SLOT0[name] + s + 1))
                    w = weights(s)
                    for k in range(4):
                        kt = 4 * s + k
                        for t in range(NT):
                            tok = slice(t * P, (t + 1) * P)
                            ins = passes(mm, pair[:, t, :], [XTH[:, kt, tok], XTL[:, kt, tok]],
                                         [x[:, k, :] for x in w], kt == 0, kt == KT - 1)
                    ins.then_inc(used, 1)

            def product(name, first, n, feat):
                d, ac = [(x[2], x[3]) for x in UNITS if x[0] == name][0]

                def one(j, par):
                    pe.wait_ge(ev["dve_free"], j * d + (DVE0[name] - d))
                    if ac:
                        pe.wait_ge(ev["act_free"], j * ac + (ACT0[name] - ac))
                    group(name, j, PP[:, (UNIT0[name] + par) % 2], feat)

                if first == 0:
                    pe.wait_ge(ev["dve_free"], DVE0[name])
                    pe.wait_ge(ev["act_free"], ACT0[name])
                if n % 2 or n == 2:
                    for j in range(first, first + n):
                        one(j, j)
                else:
                    with pe.Fori(0, n // 2, 1) as i:
                        for par in range(2):
                            one(2 * i + (first + par), first + par)

            def turn(tiles=16, src=SCN):
                e = ev["rows_out"] if tiles == 16 else ev["y_out"]
                out0 = turn.out if tiles == 16 else 0
                for t in range(NT):
                    pe.wait_ge(ev["tp_scaled"], turn.rows + 1)
                    turn.rows += 1
                    for g in range(tiles // 4):
                        if t == 1:
                            pe.wait_ge(e, out0 + g + 1)
                        for n in range(4):
                            kt = 4 * g + n
                            ins = nc.tensor.transpose(PQ[:, g, n * P:(n + 1) * P], src[:, t, kt * P:(kt + 1) * P], ID)
                        ins.then_inc(ev["turned"], 1)
                pe.wait_ge(e, out0 + tiles // 2)
                if tiles == 16:
                    turn.out += 8
                    pe.wait_ge(ev["rows_low"], turn.out)
            turn.out = 0
            turn.rows = 0

            pe.wait_ge(ev["masks"], 3)
            turn()
            pe.wait_ge(ev["wg_low"], 1)
            wg = [x[:, :].rearrange("p (k n) -> p k n", k=KT) for x in (WGH, WGL)]
            for t in range(NT):
                tok = slice(t * P, (t + 1) * P)
                for kt in range(KT):
                    ins = passes(mm, PQ[:, 0, 16 * t:16 * t + 16], [XTH[:, kt, tok], XTL[:, kt, tok]],
                                 [x[:, kt, :] for x in wg], kt == 0, kt == KT - 1)
            ins.then_inc(ev["gate_mm"], 1)
            product("win", 0, 2, True)
            pe.wait_ge(*nth("log_f", 1))
            for n, (w, t) in enumerate(((UI, 0), (UI, 1), (ONES, 0), (ONES, 1))):
                ins = mm(PQ[:, 1, 16 * n:16 * n + 16], w, LF[:, t, :], start=True, stop=True)
            ins.then_inc(ev["cumsum_mm"], 1)
            product("win", 2, 4, True)
            product("win", 6, 6, False)
            pe.wait_ge(*nth("fox_diag", 1))
            pe.wait_ge(ev["act_free"], 2 + 12)
            pe.wait_ge(ev["dve_free"], 2 + 12)
            for h in range(FH + 1):
                if h < FH:
                    b = h % 2
                    if h >= 2:
                        pe.wait_ge(ev["fox_max"], h - 1)
                    for t in range(NT):
                        dst = PQ[:, b, 0:P] if t == 0 else PQ[:, b, P:384]
                        mm(dst, FQ[:, h, t * P:(t + 1) * P], FK[:, h, 0:P * (t + 1)], start=True, stop=False)
                        ins = mm(dst, ONES, flat(DG[:, h, 0:t + 1, :]), start=False, stop=True)
                    ins.then_inc(ev["fox_scores"], 1)
                if h >= 1:
                    g, b = h - 1, (h - 1) % 2
                    pe.wait_ge(ev["fox_exp"], g + 1)
                    if g >= 2:
                        pe.wait_ge(ev["fox_pt"], g - 1)
                    for n in range(3):
                        ins = nc.tensor.transpose(PQ[:, 2 + b, n * P:(n + 1) * P], FP[:, b, n * P:(n + 1) * P], ID)
                    ins.then_inc(ev["fox_turned"], 1)
                    pe.wait_ge(ev["fox_pt"], g + 1)
                    if g >= 2:
                        pe.wait_ge(ev["fox_out"], g - 1)
                    mm(PP[:, b, 0, 0:P], FPT[:, b, 0:P], FV[:, 0, g * P:(g + 1) * P], start=True, stop=True)
                    mm(PP[:, b, 0, P:2 * P], FPT[:, b, P:2 * P], FV[:, 0, g * P:(g + 1) * P], start=True, stop=False)
                    mm(PP[:, b, 0, P:2 * P], FPT[:, b, 2 * P:384], FV[:, 1, g * P:(g + 1) * P], start=False,
                       stop=True).then_inc(ev["fox_pv"], 1)
            mlstm_pe(pe, mm)
            turn(src=SCR)
            product("wout", 0, 4, False)
            turn()
            product("wq", 0, 4, True)
            pe.wait_ge(ev["keys_in"], 16)
            pe.wait_ge(ev["act_free"], ACT0["peer"])
            pe.wait_ge(ev["dve_free"], DVE0["peer"])
            for n in range(8):
                t, g = n // 4, n % 4
                if t == 1:
                    pe.wait_ge(*nth("scores_out", n - 3))
                for m in range(4):
                    hq = 4 * g + m
                    ins = mm(PQ[:, g, m * P:(m + 1) * P], PQT[:, hq, t * P:(t + 1) * P], KEYS[:, hq % 2, :],
                             start=True, stop=True)
                ins.then_inc(ev["scores_mm"], 1)
            pe.wait_ge(*nth("scores_out", 8))
            first_layer(pe, mm, PQ[:, 0:2, :], SLOT0["peer"])
            pe.wait_ge(*nth("sel_ready", 4))
            pe.wait_ge(*nth("gate_ready", 1))
            for q in range(2):
                for t in range(NT):
                    nc.tensor.transpose(PQ[:, 2, q * T + t * P:q * T + (t + 1) * P], SEL[:, q, t, :], ID)
            for t in range(NT):
                ins = nc.tensor.transpose(PQ[:, 3, t * P:(t + 1) * P], GA[:, t, :], ID)
            ins.then_inc(ev["hk_turned"], 1)
            pe.wait_ge(*nth("hk_ready", 1))
            for _ in range(2):
                pe.nop().then_inc(ev["rows_used"], 1)
            with pe.Fori(0, T // 8, 1) as i:
                for b in range(2):
                    pe.wait_ge(ev["onehots"], 2 * i + b + 1)
                    pe.wait_ge(ev["bank_empty"], 2 * i + b + 1)
                    for t in range(4):
                        ins = mm(PQ[:, 2 + b, t * P:(t + 1) * P], A0[:, b, t, :], B0[:, b, t, :], start=True, stop=True)
                    ins.then_inc(ev["rows_used"], 1)
            two_pe(pe, mm, "peer", EB)
            stage2_pe(pe, mm, product, turn)


def rows_of(w):
    k, n = w.shape
    return w.reshape(k // BLK, 4, P, n // BLK, BLK).transpose(3, 0, 2, 1, 4).reshape(-1, P, 4 * BLK)


def second_of(w):
    k, n = w.shape
    return w.reshape(k // BLK, 4, P, n // BLK, BLK).transpose(0, 3, 2, 1, 4).reshape(-1, P, 4 * BLK)


def columns(vec):
    return np.asarray(vec).reshape(-1, P).T


def layout(i):
    f, mq = 1024, 512
    w = i["w_in"][0]
    cut = {}
    at = 0
    for name, n in (("fq", f), ("fk", f), ("fv", f), ("ff", 8), ("mq", mq), ("mk", mq), ("mv", f), ("mi", 4), ("mf", 4), ("mo", f)):
        cut[name] = w[:, at:at + n]
        at += n
    arrays = {
        "x": i["x"][0],
        "win": rows_of(np.concatenate([cut[n] for n in ("mq", "mk", "fq", "fk", "fv", "mv", "mo")], 1)),
        "w_gates": np.concatenate([cut[n] for n in ("ff", "mi", "mf")], 1).reshape(KT, P, 16).transpose(1, 0, 2).reshape(P, -1),
        "wout": rows_of(i["w_out"][0]),
        "wq": rows_of(i["peer_w_q"][0]),
        "keys": i["peer_keys"][0].transpose(2, 0, 1).reshape(P, -1),
        "pu": i["peer_u"][0].reshape(P, EB, 4, 4, 4, P).transpose(1, 3, 5, 4, 2, 0).reshape(-1, P, 2048),
        "pv": i["peer_v"][0].reshape(P, EB, 4, 4, BLK).transpose(1, 3, 0, 2, 4).reshape(-1, P, 2048),
        "cols1": np.concatenate([
            columns(i["norm1_w"][0]), columns(i["fox_out_norm_w"][0]), columns(i["mlstm_out_norm_w"][0]),
            columns(i["norm2_w"][0]), i["mlstm_conv_w"][0].reshape(4, 8, P).transpose(2, 1, 0).reshape(P, -1),
            columns(i["mlstm_conv_b"][0])], 1),
        "rows": np.concatenate([i["fox_f_bias"][0], i["mlstm_i_bias"][0], i["mlstm_f_bias"][0],
                                i["dn_a_log_2"][0], i["dn_dt_bias_2"][0]]),
    }
    w = i["w_in_2"][0]
    f = 1024
    dn, rw = w[:, 0:4 * f + 16], w[:, 4 * f + 16:]
    small = np.concatenate([dn[:, 4 * f:], rw[:, 3 * f:]], 1)
    mu = i["rw_mu_2"][0]
    arrays.update({
        "dn": rows_of(dn[:, 0:4 * f]),
        "small": small.reshape(4, 4, P, 272).transpose(0, 2, 1, 3).reshape(4, P, 4 * 272),
        "rw": rows_of(np.concatenate([rw[:, f * n + BLK * h:f * n + BLK * (h + 1)] for h in range(2) for n in range(3)], 1)),
        "w2": i["rw_w2_2"][0], "a2": i["rw_a2_2"][0], "g2": i["rw_g2_2"][0],
        "out2": rows_of(i["w_out_2"][0]),
        "mem": i["mem_2"][0],
        "xk": rows_of(i["xa_wk_2"][0]), "xv": rows_of(i["xa_wv_2"][0]), "xq": rows_of(i["xa_wq_2"][0]),
        "xo": second_of(i["xa_wo_2"][0]),
        "f1": rows_of(i["ffn_w1_2"][0]), "f2": second_of(i["ffn_w2_2"][0]),
        "fnw1": i["final_norm_w"], "fnw": i["final_norm_w_2"],
        "cols2": np.concatenate([
            columns(i["mix_norm_w_2"][0]), columns(i["xa_norm_w_2"][0]), columns(i["mem_norm_w_2"][0]),
            columns(i["ffn_norm_w_2"][0]), i["dn_conv_w_2"][0].reshape(4, 24, P).transpose(2, 1, 0).reshape(P, -1),
            columns(i["dn_norm_w_2"][0]), columns(mu), columns(i["rw_w0_2"][0]), columns(i["rw_a0_2"][0]),
            columns(i["rw_k_k_2"][0]), columns(i["rw_k_a_2"][0]), columns(i["rw_r_k_2"][0]),
            columns(i["rw_ln_w_2"][0]), columns(i["rw_ln_b_2"][0])], 1),
    })
    return {k: np.ascontiguousarray(v) for k, v in arrays.items()}


def kernel(**inputs):
    import concourse.bacc as bacc
    from concourse.bass_utils import run_bass_kernel_spmd

    arrays = layout({k: np.asarray(v) for k, v in inputs.items()})
    nc = bacc.Bacc("TRN2", target_bir_lowering=False, num_devices=1)
    handles = {k: nc.dram_tensor(k, v.shape, mybir.dt.from_np(v.dtype), kind="ExternalInput").ap()
               for k, v in arrays.items()}
    out = nc.dram_tensor("out", (T, D), F32, kind="ExternalOutput").ap()
    build(nc, handles, out)
    r = run_bass_kernel_spmd(nc, [arrays], core_ids=[0])
    return r.results[0]["out"].reshape(1, T, D)
```
